# Optimizing a Trainium2 kernel written in Bass

```python
import jax, jax.numpy as jnp
from jax import lax
import numpy as np

D_MODEL = 1024
BATCH = 1
SEQ = 1024
DEPTH = 1
DEC_BATCH = 8
DEC_SEQ = 8
PAST_LEN = 4096
PAGE_SIZE = 128

HEAD_DIM = 64
A_HEADS = 6
A_WIDTH = A_HEADS * HEAD_DIM
A_DECAY_LORA = 64
A_ICLR_LORA = 64
A_GATE_LORA = 128
A_GN_EPS = 64e-5
A_COLS = 3 * A_WIDTH + A_DECAY_LORA + A_ICLR_LORA + A_GATE_LORA
SB_HEADS = 4
SB_WIDTH = SB_HEADS * HEAD_DIM
SB_COLS = 3 * SB_WIDTH
SB_BIAS_INIT = -8.0
DIL_GROUPS = ((128, 1), (512, 4), (2048, 16))
DIL_HEADS_PER_GROUP = 2
DIL_HEADS = DIL_HEADS_PER_GROUP * len(DIL_GROUPS)
DIL_WIDTH = DIL_HEADS * HEAD_DIM
DIL_OUT_WIDTH = DIL_HEADS_PER_GROUP * HEAD_DIM
DIL_COLS = 3 * DIL_WIDTH
ALIBI_MAX_EXP = 8.0
N_BRANCHES = 3
GATE_COLS = N_BRANCHES * D_MODEL
IN_COLS = A_COLS + SB_COLS + DIL_COLS + GATE_COLS
D_FF = ((8 * D_MODEL // 3 + 127) // 128) * 128
CONV_WIDTH = 3
Q_BLOCK = 128
NORM_EPS = 1e-6

kernel_name = "hybrid_rwkv7_stickbreak_dilated_decoder_step"

def rmsnorm(x, g):
    xf = x.astype(jnp.float32)
    y = xf * lax.rsqrt(jnp.mean(xf * xf, axis=-1, keepdims=True) + NORM_EPS)
    return (y * g.astype(jnp.float32)).astype(x.dtype)

def alibi_slopes():
    return jnp.exp2(-ALIBI_MAX_EXP * jnp.arange(1, DIL_HEADS + 1, dtype=jnp.float32) / DIL_HEADS)

def over_query_blocks(fn, q, q_idx):
    B, T = q.shape[:2]
    if T <= Q_BLOCK:
        return fn(q, q_idx)
    nb = T // Q_BLOCK
    qb = jnp.moveaxis(q.reshape((B, nb, Q_BLOCK) + q.shape[2:]), 1, 0)
    ib = q_idx.reshape(nb, Q_BLOCK)
    out = lax.map(lambda a: fn(a[0], a[1]), (qb, ib))
    out = jnp.moveaxis(out, 0, 1)
    return out.reshape((B, T) + out.shape[3:])

def rwkv7_mix(pa, state0, w0, w2, a0, a2, g2, k_k, k_a, r_k, ln_w, ln_b):
    f32 = jnp.float32
    B, T, _ = pa.shape
    pa = pa.astype(f32)
    o0 = 3 * A_WIDTH
    r = pa[..., :A_WIDTH]
    k = pa[..., A_WIDTH:2 * A_WIDTH]
    v = pa[..., 2 * A_WIDTH:o0]
    lw = pa[..., o0:o0 + A_DECAY_LORA]
    la = pa[..., o0 + A_DECAY_LORA:o0 + A_DECAY_LORA + A_ICLR_LORA]
    lg = pa[..., o0 + A_DECAY_LORA + A_ICLR_LORA:]
    w_log = -jax.nn.softplus(-(w0.astype(f32) + jnp.tanh(lw) @ w2.astype(f32))) - 0.5
    decay = jnp.exp(-jnp.exp(w_log))
    a = jax.nn.sigmoid(a0.astype(f32) + la @ a2.astype(f32))
    g = jax.nn.sigmoid(lg) @ g2.astype(f32)
    heads = lambda t: t.reshape(B, T, A_HEADS, HEAD_DIM)
    kk = heads(k * k_k.astype(f32))
    kk = kk / jnp.maximum(jnp.sqrt(jnp.sum(kk * kk, axis=-1, keepdims=True)), 1e-12)
    k = heads(k * (1.0 + (a - 1.0) * k_a.astype(f32)))
    r, v, decay, a = heads(r), heads(v), heads(decay), heads(a)

    def step(S, inp):
        r_t, w_t, k_t, v_t, kk_t, a_t = inp
        sa = jnp.einsum('bhvk,bhk->bhv', S, -kk_t)
        S = (S * w_t[:, :, None, :] + sa[..., None] * (kk_t * a_t)[:, :, None, :]
             + v_t[..., None] * k_t[:, :, None, :])
        return S, jnp.einsum('bhvk,bhk->bhv', S, r_t)

    xs = tuple(jnp.moveaxis(t, 1, 0) for t in (r, decay, k, v, kk, a))
    S_T, out = lax.scan(step, state0.astype(f32), xs)
    out = jnp.moveaxis(out, 0, 1)
    mean = jnp.mean(out, axis=-1, keepdims=True)
    var = jnp.mean(jnp.square(out - mean), axis=-1, keepdims=True)
    o = ((out - mean) * lax.rsqrt(var + A_GN_EPS)).reshape(B, T, A_WIDTH)
    o = o * ln_w.astype(f32) + ln_b.astype(f32)
    bonus = jnp.sum(r * k * r_k.astype(f32), axis=-1, keepdims=True) * v
    o = (o + bonus.reshape(B, T, A_WIDTH)) * g
    return o, S_T.astype(state0.dtype)

def stick_breaking(q, k_all, v_all, q_idx, bias):
    f32 = jnp.float32
    z = jnp.einsum('bqhd,bkhd->bhqk', q.astype(f32), k_all.astype(f32)) * (HEAD_DIM ** -0.5)
    z = z + bias.astype(f32)[None, :, None, None]
    k_idx = jnp.arange(k_all.shape[1])
    before = k_idx[None, :] < q_idx[:, None]
    log_keep = jnp.where(before, jax.nn.log_sigmoid(-z), 0.0)
    log_between = lax.cumsum(log_keep, axis=3, reverse=True) - log_keep
    att = jnp.where(before, jnp.exp(jax.nn.log_sigmoid(z) + log_between), 0.0)
    return jnp.einsum('bhqk,bkhd->bqhd', att, v_all.astype(f32))

def dilated_group(q, k_all, v_all, q_idx, dil, n_keys, slopes):
    f32 = jnp.float32
    steps = jnp.arange(n_keys)
    idx = q_idx[:, None] - dil * steps[None, :]
    valid = idx >= 0
    idx = jnp.maximum(idx, 0)
    kg = jnp.take(k_all, idx, axis=1).astype(f32)
    vg = jnp.take(v_all, idx, axis=1).astype(f32)
    s = jnp.einsum('bqhd,bqmhd->bhqm', q.astype(f32), kg) * (HEAD_DIM ** -0.5)
    s = s - slopes[:, None, None] * (dil * steps).astype(f32)
    s = jnp.where(valid, s, -jnp.inf)
    lse = jax.nn.logsumexp(s, axis=-1)
    p = jnp.exp(s - lse[..., None])
    return jnp.einsum('bhqm,bqmhd->bqhd', p, vg), lse

def dilated_mixture(q, k, v, win_bufs):
    B, T = q.shape[:2]
    slopes = alibi_slopes()
    k_ext, v_ext, starts, new_bufs = [], [], [], []
    for g, (win, dil) in enumerate(DIL_GROUPS):
        hs = slice(g * DIL_HEADS_PER_GROUP, (g + 1) * DIL_HEADS_PER_GROUP)
        buf = win_bufs[g].astype(k.dtype)
        ext = jnp.concatenate([buf, jnp.stack([k[:, :, hs], v[:, :, hs]], axis=2)], axis=1)
        k_ext.append(ext[:, :, 0])
        v_ext.append(ext[:, :, 1])
        starts.append(buf.shape[1])
        new_bufs.append(ext[:, -min(win, ext.shape[1]):])

    def attend(q_blk, i_blk):
        outs, lses = [], []
        for g, (win, dil) in enumerate(DIL_GROUPS):
            hs = slice(g * DIL_HEADS_PER_GROUP, (g + 1) * DIL_HEADS_PER_GROUP)
            o, lse = dilated_group(q_blk[:, :, hs], k_ext[g], v_ext[g], starts[g] + i_blk,
                                   dil, win // dil + 1, slopes[hs])
            outs.append(o)
            lses.append(lse)
        wts = jax.nn.softmax(jnp.stack(lses), axis=0)
        wts = jnp.swapaxes(wts, 2, 3)[..., None]
        return jnp.sum(wts * jnp.stack(outs), axis=0)

    o = over_query_blocks(attend, q, jnp.arange(T))
    return o.reshape(B, T, DIL_OUT_WIDTH), new_bufs

def trunk_layer(x, prev_xn, wkv0, sb_k_past, sb_v_past, win_bufs, conv_buf,
                norm_mix, w_in, rwkv_mu, rwkv_w0, rwkv_w2, rwkv_a0, rwkv_a2, rwkv_g2,
                rwkv_k_k, rwkv_k_a, rwkv_r_k, rwkv_ln_w, rwkv_ln_b, sb_bias,
                w_branch_a, w_branch_b, w_branch_c, w_out,
                norm_ffn, w_up, conv_w, conv_b, w_down):
    dt = x.dtype
    B, T, _ = x.shape
    xn = rmsnorm(x, norm_mix)
    h = xn @ w_in
    pa = h[..., :A_COLS]
    pb = h[..., A_COLS:A_COLS + SB_COLS]
    pc = h[..., A_COLS + SB_COLS:A_COLS + SB_COLS + DIL_COLS]
    pg = h[..., A_COLS + SB_COLS + DIL_COLS:]
    prev_pa = prev_xn.astype(dt) @ w_in[:, :A_COLS]
    shifted = jnp.concatenate([prev_pa, pa[:, :-1]], axis=1)
    pa = pa + rwkv_mu * (shifted - pa)
    o_a, wkv = rwkv7_mix(pa, wkv0, rwkv_w0, rwkv_w2, rwkv_a0, rwkv_a2, rwkv_g2,
                         rwkv_k_k, rwkv_k_a, rwkv_r_k, rwkv_ln_w, rwkv_ln_b)
    q_b, k_b, v_b = [t.reshape(B, T, SB_HEADS, HEAD_DIM) for t in jnp.split(pb, 3, axis=-1)]
    k_all = jnp.concatenate([sb_k_past.astype(dt), k_b], axis=1)
    v_all = jnp.concatenate([sb_v_past.astype(dt), v_b], axis=1)
    n_past = sb_k_past.shape[1]
    o_b = over_query_blocks(lambda qq, ii: stick_breaking(qq, k_all, v_all, ii, sb_bias),
                            q_b, n_past + jnp.arange(T)).reshape(B, T, SB_WIDTH)
    q_c, k_c, v_c = [t.reshape(B, T, DIL_HEADS, HEAD_DIM) for t in jnp.split(pc, 3, axis=-1)]
    o_c, new_wins = dilated_mixture(q_c, k_c, v_c, win_bufs)
    gates = jax.nn.sigmoid(pg.astype(jnp.float32)).astype(dt).reshape(B, T, N_BRANCHES, D_MODEL)
    merged = (gates[:, :, 0] * (o_a.astype(dt) @ w_branch_a)
              + gates[:, :, 1] * (o_b.astype(dt) @ w_branch_b)
              + gates[:, :, 2] * (o_c.astype(dt) @ w_branch_c))
    x = x + merged @ w_out
    u = rmsnorm(x, norm_ffn) @ w_up
    ext = jnp.concatenate([conv_buf.astype(dt), u], axis=1)
    c = conv_b + sum(conv_w[i] * ext[:, i:i + T] for i in range(CONV_WIDTH))
    gate, val = jnp.split(c, 2, axis=-1)
    x = x + (jax.nn.silu(gate) * val) @ w_down
    new_state = (k_b, v_b, new_wins[0], new_wins[1], new_wins[2], wkv, xn[:, -1],
                 ext[:, -(CONV_WIDTH - 1):])
    return x, new_state

def setup_inputs(seed: int = 0) -> dict:
    key = jax.random.key(seed)
    keys = jax.random.split(key, 40)
    counter = [0]

    def nxt():
        counter[0] += 1
        return keys[counter[0] - 1]

    f32 = jnp.float32

    def nrm(shape, scale=1.0):
        return scale * jax.random.normal(nxt(), shape, f32)

    n_pages = PAST_LEN // PAGE_SIZE
    n_used = DEC_BATCH * n_pages
    n_pool = n_used + n_used // 4
    inp = {}
    inp['x_prompt'] = nrm((BATCH, SEQ, D_MODEL))
    inp['x_sample'] = nrm((DEC_BATCH, DEC_SEQ, D_MODEL))
    inp['cache_sb_k'] = nrm((DEPTH, n_pool, PAGE_SIZE, SB_HEADS, HEAD_DIM))
    inp['cache_sb_v'] = nrm((DEPTH, n_pool, PAGE_SIZE, SB_HEADS, HEAD_DIM))
    inp['page_table'] = jax.random.permutation(nxt(), n_pool)[:n_used].reshape(
        DEC_BATCH, n_pages).astype(jnp.int32)
    for g, (win, dil) in enumerate(DIL_GROUPS):
        inp['cache_win%d' % g] = nrm((DEPTH, DEC_BATCH, min(win, PAST_LEN), 2,
                                      DIL_HEADS_PER_GROUP, HEAD_DIM))
    inp['state_wkv'] = nrm((DEPTH, DEC_BATCH, A_HEADS, HEAD_DIM, HEAD_DIM), 0.5)
    inp['state_shift'] = nrm((DEPTH, DEC_BATCH, D_MODEL))
    inp['state_conv'] = nrm((DEPTH, DEC_BATCH, CONV_WIDTH - 1, 2 * D_FF))
    inp['norm_mix'] = 1.0 + nrm((DEPTH, D_MODEL), 0.02)
    inp['w_in'] = nrm((DEPTH, D_MODEL, IN_COLS), D_MODEL ** -0.5)
    inp['rwkv_mu'] = jax.random.uniform(nxt(), (DEPTH, A_COLS), f32)
    inp['rwkv_w0'] = nrm((DEPTH, A_WIDTH), 0.5)
    inp['rwkv_w2'] = nrm((DEPTH, A_DECAY_LORA, A_WIDTH), 0.5 * A_DECAY_LORA ** -0.5)
    inp['rwkv_a0'] = nrm((DEPTH, A_WIDTH), 0.5)
    inp['rwkv_a2'] = nrm((DEPTH, A_ICLR_LORA, A_WIDTH), 0.5 * A_ICLR_LORA ** -0.5)
    inp['rwkv_g2'] = nrm((DEPTH, A_GATE_LORA, A_WIDTH), A_GATE_LORA ** -0.5)
    inp['rwkv_k_k'] = 0.85 + nrm((DEPTH, A_WIDTH), 0.02)
    inp['rwkv_k_a'] = 1.0 + nrm((DEPTH, A_WIDTH), 0.02)
    inp['rwkv_r_k'] = nrm((DEPTH, A_HEADS, HEAD_DIM), 0.1)
    inp['rwkv_ln_w'] = 1.0 + nrm((DEPTH, A_WIDTH), 0.02)
    inp['rwkv_ln_b'] = nrm((DEPTH, A_WIDTH), 0.02)
    inp['sb_bias'] = SB_BIAS_INIT + nrm((DEPTH, SB_HEADS), 0.5)
    inp['w_branch_a'] = nrm((DEPTH, A_WIDTH, D_MODEL), A_WIDTH ** -0.5)
    inp['w_branch_b'] = nrm((DEPTH, SB_WIDTH, D_MODEL), SB_WIDTH ** -0.5)
    inp['w_branch_c'] = nrm((DEPTH, DIL_OUT_WIDTH, D_MODEL), DIL_OUT_WIDTH ** -0.5)
    inp['w_out'] = nrm((DEPTH, D_MODEL, D_MODEL), D_MODEL ** -0.5)
    inp['norm_ffn'] = 1.0 + nrm((DEPTH, D_MODEL), 0.02)
    inp['w_up'] = nrm((DEPTH, D_MODEL, 2 * D_FF), D_MODEL ** -0.5)
    inp['conv_w'] = nrm((DEPTH, CONV_WIDTH, 2 * D_FF), CONV_WIDTH ** -0.5)
    inp['conv_b'] = nrm((DEPTH, 2 * D_FF), 0.02)
    inp['w_down'] = nrm((DEPTH, D_FF, D_MODEL), D_FF ** -0.5)
    inp['norm_final'] = 1.0 + nrm((D_MODEL,), 0.02)
    return inp

def reference(x_prompt, x_sample, cache_sb_k, cache_sb_v, page_table,
              cache_win0, cache_win1, cache_win2, state_wkv, state_shift, state_conv,
              norm_mix, w_in, rwkv_mu, rwkv_w0, rwkv_w2, rwkv_a0, rwkv_a2, rwkv_g2,
              rwkv_k_k, rwkv_k_a, rwkv_r_k, rwkv_ln_w, rwkv_ln_b, sb_bias,
              w_branch_a, w_branch_b, w_branch_c, w_out,
              norm_ffn, w_up, conv_w, conv_b, w_down, norm_final):
    layer_weights = (norm_mix, w_in, rwkv_mu, rwkv_w0, rwkv_w2, rwkv_a0, rwkv_a2, rwkv_g2,
                     rwkv_k_k, rwkv_k_a, rwkv_r_k, rwkv_ln_w, rwkv_ln_b, sb_bias,
                     w_branch_a, w_branch_b, w_branch_c, w_out,
                     norm_ffn, w_up, conv_w, conv_b, w_down)
    dtp = x_prompt.dtype
    bp = x_prompt.shape[0]
    bs = x_sample.shape[0]
    xp, xs = x_prompt, x_sample
    n_state = 8
    new_p = [[] for _ in range(n_state)]
    new_s = [[] for _ in range(n_state)]
    for l in range(DEPTH):
        lw = [w[l] for w in layer_weights]
        empty_wins = [jnp.zeros((bp, 0, 2, DIL_HEADS_PER_GROUP, HEAD_DIM), dtp) for _ in DIL_GROUPS]
        xp, st = trunk_layer(
            xp, jnp.zeros((bp, 1, D_MODEL), dtp),
            jnp.zeros((bp, A_HEADS, HEAD_DIM, HEAD_DIM), dtp),
            jnp.zeros((bp, 0, SB_HEADS, HEAD_DIM), dtp), jnp.zeros((bp, 0, SB_HEADS, HEAD_DIM), dtp),
            empty_wins, jnp.zeros((bp, CONV_WIDTH - 1, 2 * D_FF), dtp), *lw)
        for lst, a in zip(new_p, st):
            lst.append(a)
        k_past = cache_sb_k[l][page_table].reshape(bs, -1, SB_HEADS, HEAD_DIM)
        v_past = cache_sb_v[l][page_table].reshape(bs, -1, SB_HEADS, HEAD_DIM)
        xs, st = trunk_layer(
            xs, state_shift[l][:, None, :], state_wkv[l], k_past, v_past,
            [cache_win0[l], cache_win1[l], cache_win2[l]], state_conv[l], *lw)
        for lst, a in zip(new_s, st):
            lst.append(a)
    sp = [jnp.stack(a) for a in new_p]
    ss = [jnp.stack(a) for a in new_s]
    y_prompt = rmsnorm(xp, norm_final)
    y_sample = rmsnorm(xs, norm_final)
    return (y_prompt, y_sample, sp[0], ss[0], sp[1], ss[1], sp[2], ss[2], sp[3], ss[3],
            sp[4], ss[4], sp[5], ss[5], sp[6], ss[6], sp[7], ss[7])


_drawn_inputs = setup_inputs


def setup_inputs(seed=0):
    import zlib

    import numpy as np

    out = dict(_drawn_inputs(seed))
    spreads = {}
    factors = {'cache_sb_k': 3.947,
     'cache_sb_v': 3.205,
     'rwkv_k_k': 8.0,
     'rwkv_k_a': 2.825,
     'rwkv_ln_w': 8.0,
     'rwkv_ln_b': 8.0,
     'sb_bias': 8.0,
     'w_branch_b': 3.204,
     'norm_ffn': 2.965,
     'conv_b': 4.023,
     'norm_final': 2.85}
    for name, (base, spread) in spreads.items():
        noise = np.random.default_rng([zlib.crc32(name.encode()), seed]).standard_normal(out[name].shape)
        drawn = base * np.exp(spread * noise) if base else spread * noise
        out[name] = __import__('jax').numpy.asarray(drawn.astype(out[name].dtype))
    for name, factor in factors.items():
        out[name] = (out[name] * factor).astype(out[name].dtype)
    return out
```

```python
from contextlib import ExitStack, contextmanager

import numpy as np

import concourse.bass as bass
from concourse import mybir

ALU = mybir.AluOpType
ACT = mybir.ActivationFunctionType
AX = mybir.AxisListType
F32, I32 = mybir.dt.float32, mybir.dt.int32

P = 128
D = 1024
KT = D // P
SEQ, NB, NQ = 1024, 8, 8
TS = NB * NQ
T = SEQ + TS
TP = T + NB
HD = 64
AH, AW = 6, 384
AT = 11
PAIRS = 3
SBH = 4
DILS = (1, 4, 16)
FF = 2816
FT = FF // P
UT = 2 * FT
EPS = 1e-6
GN_EPS = 64e-5
NPAGE = 32
PAST = 4096
CHUNK = P
NU = SEQ // CHUNK + 1
LEVELS = 7
CH = ((0, 384), (384, 352), (736, 352))
CHP = ((0, 384), (384, 352), (736, 360))
NEG = -1e30


PROWS, _at = {}, 0
for _n, _c in (("norm_mix", 8), ("rwkv_mu", 11), ("rwkv_w0", 3), ("rwkv_a0", 3), ("rwkv_k_k", 3),
               ("rwkv_k_a", 3), ("rwkv_r_k", 3), ("rwkv_ln_w", 3), ("rwkv_ln_b", 3), ("norm_ffn", 8),
               ("norm_final", 8), ("conv_b", 44)):
    PROWS[_n] = (_at, _c)
    _at += _c
NPROW = _at


def constants():
    r, c = np.arange(P)[:, None], np.arange(P)[None, :]
    same = lambda n: (r // n) == (c // n)
    f = np.zeros((P, 5, P), np.float32)
    f[:, 0] = r == c
    f[:, 1] = 1.0
    f[:, 2] = same(HD)
    f[:, 3] = r >= c
    f[:, 4] = r < c
    u = np.zeros((P, 2 * LEVELS + 6, P), np.int32)
    for l in range(1, LEVELS + 1):
        low = same(2 ** l) & (r % 2 ** l >= 2 ** (l - 1)) & (c % 2 ** l < 2 ** (l - 1))
        u[:, l - 1] = low
        u[:, LEVELS + l - 1] = low.T
    for n, s in enumerate((np.ones((P, P), bool), same(NQ))):
        u[:, 2 * LEVELS + 3 * n] = (c < r) & s
        u[:, 2 * LEVELS + 3 * n + 1] = (r < c) & s
        u[:, 2 * LEVELS + 3 * n + 2] = (r <= c) & s
    e = np.zeros((P, NB, TS), np.float32)
    e[:] = (np.arange(TS)[None, :] // NQ) == np.arange(NB)[:, None]
    h = np.zeros((TS, NB), np.float32)
    h[:] = (np.arange(TS)[:, None] // NQ) == np.arange(NB)[None, :]
    new = np.ones((P, NB, NQ), np.int32)
    k, b, q = np.arange(P)[:, None, None], np.arange(NB)[None, :, None], np.arange(NQ)[None, None, :]
    new[(k // NQ == b) & (k % NQ < q)] = 0
    slope = lambda h: 2.0 ** (-8.0 * (h + 1) / 6)
    bias = np.full((P, 3, 2, 256), NEG, np.float32)
    t, k = np.arange(P)[:, None], np.arange(256)[None, :]
    for gi, dil in enumerate(DILS):
        for half in range(2):
            d = t + P - k
            ok = (d >= 0) & (d <= P)
            if gi == 2:
                ok = (d >= 0) & (k >= P) & (d % 2 == 0)
                d = d // 2
            bias[:, gi, half] = np.where(ok, -slope(2 * gi + half) * dil * d, NEG)
    sbias = np.full((P, 3, 192), NEG, np.float32)
    row, i, n = np.arange(P)[:, None], np.arange(P)[None, :], np.arange(TS)[None, :]
    b, slot, q = row // 16, row // 8 % 2, row % 8
    for gi, dil in enumerate(DILS):
        sl = np.where(slot == 0, slope(2 * gi), slope(2 * gi + 1)) * dil
        d = P + q // dil - i
        sbias[:, gi, 0:P] = np.where(d <= P, -sl * d, NEG)
        d = q - n % 8
        sbias[:, gi, P:] = np.where((n // 8 == b) & (d >= 0) & (d % dil == 0), -sl * (d // dil), NEG)
    return {"c_bias": bias, "c_sbias": sbias, "c_later": (r >= c).astype(np.int32), "c_new": new, "c_f32": f, "c_mask": u, "c_col": e, "c_row": h}


class Tensors:
    pass


@contextmanager
def semaphores(g):
    made = []

    def sem(name):
        made.append(g.nc.alloc_semaphore(name))
        return made[-1]
    g.sem = sem
    yield
    g.nc.clear_and_free_semaphores(made)
    g.nc.all_engine_barrier()


def build(nc, a, outs, scratch):
    with ExitStack() as ctx:
        g = Tensors()
        g.nc, g.a, g.o, g.dr = nc, a, outs, scratch
        sb = lambda name, shape, dt=F32: ctx.enter_context(nc.sbuf_tensor(name, shape, dt))
        g.ps = ctx.enter_context(nc.psum_tensor("ps", [P, 8, 512], F32))
        g.cf = sb("cf", [P, 5, P])
        g.ident, g.ones, g.blk, g.tri = (g.cf[:, i, :] for i in range(4))
        g.par = sb("par", [P, NPROW])
        g.cw = sb("cw", [P, 3, UT])
        g.cst = sb("cst", [P, UT, 2 * NB])
        g.sbb = sb("sbb", [P, SBH])
        c0 = PROWS["conv_b"][0]
        g.cb = g.par[:, c0:c0 + UT]
        g.col = lambda name, i: g.par[:, PROWS[name][0] + i:PROWS[name][0] + i + 1]
        tensor = lambda name, shape: nc.sbuf_tensor(name, shape, F32)
        with tensor("oa", [P, PAIRS, T]) as g.oa, tensor("ob", [P, 2, T]) as g.ob, tensor("oc", [P, T]) as g.oc:
            with tensor("pa", [P, AT, T]) as g.pa:
                with semaphores(g), tensor("xn_a", [P, KT, TP]) as g.xn:
                    stage_load(g)
                    a_project(g)
                with semaphores(g):
                    stage_branch_a(g)
            with semaphores(g):
                stage_branch_b(g)
            with semaphores(g):
                stage_branch_c(g)
            with semaphores(g), tensor("merged", [P, KT, T]) as g.mg:
                stage_merge(g)
                with tensor("x1", [P, KT, T]) as x1:
                    copy_dram(g, "x1r", x1[:, :, :], scratch["xt"])
                    project_add(g, "wo", a["w_out"][0].rearrange("(k p) f -> p k f", p=P), KT, g.mg, x1)
                    copy_dram(g, "x1w", scratch["xt"], x1[:, :, :])
                    norm(g, "n2", x1, "norm_ffn", g.mg)
                with tensor("act", [P, FT, T]) as act:
                    stage_up(g, g.mg, act)
                    copy_dram(g, "x1b", g.mg[:, :, :], scratch["xt"])
                    project_add(g, "wd", a["w_down"][0].rearrange("(k p) f -> p k f", p=P), FT, act, g.mg)
                with tensor("y", [P, KT, T]) as y:
                    norm(g, "n3", g.mg, "norm_final", y)
                    store_rows(g, y)


def norm_program(g, pre, src, sq, inv, gain, dst, n_cols, chunks):
    nc = g.nc
    s_sq, s_sum, s_mean, s_root, s_inv, s_out = (g.sem(f"{pre}_{n}") for n in
                                                ("sq", "sum", "mean", "root", "inv", "out"))

    def act(eng):
        for k in range(KT):
            if k >= 2:
                eng.wait_ge(s_sum, k - 1)
            nc.scalar.activation(sq[:, k % 2, 0:n_cols], src[:, k, 0:n_cols], ACT.Square).then_inc(s_sq, 1)
        eng.wait_ge(s_mean, len(chunks))
        nc.scalar.activation(inv[:, 0:n_cols], inv[:, 0:n_cols], ACT.Sqrt).then_inc(s_root, 1)

    def pe(eng):
        for k in range(KT):
            eng.wait_ge(s_sq, k + 1)
            for b, (c0, n) in enumerate(chunks):
                mm = nc.tensor.matmul(g.ps[:, b, 0:n], g.ones, sq[:, k % 2, c0:c0 + n],
                                      start=(k == 0), stop=(k == KT - 1))
            mm.then_inc(s_sum, 1)

    def dve(eng):
        eng.wait_ge(s_sum, KT)
        for b, (c0, n) in enumerate(chunks):
            nc.vector.tensor_scalar(inv[:, c0:c0 + n], g.ps[:, b, 0:n], 1.0 / D, EPS, ALU.mult,
                                    ALU.add).then_inc(s_mean, 1)
        eng.wait_ge(s_root, 1)
        nc.vector.reciprocal(inv[:, 0:n_cols], inv[:, 0:n_cols]).then_inc(s_inv, 1)
        eng.wait_ge(s_inv, 1)
        for k in range(KT):
            nc.vector.scalar_tensor_tensor(out=dst[:, k, 0:n_cols], in0=src[:, k, 0:n_cols],
                                           scalar=g.col(gain, k), in1=inv[:, 0:n_cols],
                                           op0=ALU.mult, op1=ALU.mult).then_inc(s_out, 1)

    return act, pe, dve, s_out


def stage_load(g):
    nc, a = g.nc, g.a
    NT = SEQ // P
    with ExitStack() as ctx:
        sb = lambda name, shape, dt=F32: ctx.enter_context(nc.sbuf_tensor(name, shape, dt))
        prow = sb("prow", [NPROW, P])
        cwrow = sb("cwrow", [UT, 3, P])
        crow = sb("crow", [2 * NB, 2 * FF])
        shrow = sb("shrow", [NB, D])
        xrow = sb("xrow", [P, 3, D])
        xt = sb("xt", [P, KT, T])
        sq = sb("sq", [P, 2, T])
        inv = sb("inv", [P, T])
        last = sb("last", [NB + 1, D])
        s_par, s_ps = g.sem("s_par"), g.sem("s_ps")
        s_x = [g.sem(f"s_x{i}") for i in range(3)]
        s_xt, s_xc = g.sem("s_xt"), g.sem("s_xc")
        s_pt, s_pc = g.sem("s_pt"), g.sem("s_pc")
        s_lt, s_lc, s_st = g.sem("s_lt"), g.sem("s_lc"), g.sem("s_st")
        n_act, n_pe, n_dve, n_out = norm_program(g, "n1", xt, sq, inv, "norm_mix", g.xn, T, CH)
        loads = [0]

        with nc.Block() as block:
            @block.sync
            def _(eng):
                def par(dst, src):
                    eng.dma_start(dst, src).then_inc(s_par, 16)
                    loads[0] += 1
                par(g.cf[:, :, :], a["c_f32"])
                for n, (r0, rows) in PROWS.items():
                    src = a[n].rearrange("(r c) -> r c", c=P) if n == "norm_final" else \
                        a[n][0].rearrange("h c -> (h c)").rearrange("(r c) -> r c", c=P) if n == "rwkv_r_k" else \
                        a[n][0].rearrange("(r c) -> r c", c=P)
                    par(prow[r0:r0 + rows, :], src)
                for i in range(3):
                    par(cwrow[:, i, :], a["conv_w"][0, i].rearrange("(r c) -> r c", c=P))
                par(crow[:, :], a["state_conv"][0].rearrange("b r f -> (b r) f"))
                par(shrow[:, :], a["state_shift"][0])
                par(g.sbb[:, :], a["sb_bias"].broadcast_to([P, SBH]))
                for j in range(NT + 1):
                    if j >= 3:
                        eng.wait_ge(s_xt, 2 * (j - 2))
                    n = P if j < NT else TS
                    src = a["x_prompt"][0, j * P:(j + 1) * P, :] if j < NT else \
                        a["x_sample"].rearrange("b q d -> (b q) d")
                    eng.dma_start(xrow[0:n, j % 3, :], src).then_inc(s_x[j % 3], 16)
                eng.wait_ge(s_xc, 2 * (NT + 1))
                eng.dma_start(g.dr["xt"], xt[:, :, :]).then_inc(s_st, 16)
                eng.wait_ge(s_lc, 2)
                eng.dma_start(g.o["shift_prompt"][0], last[0:1, :]).then_inc(s_st, 16)
                eng.dma_start(g.o["shift_sample"][0], last[1:1 + NB, :]).then_inc(s_st, 16)
                eng.wait_ge(n_out, KT)
                eng.dma_start(g.dr["xn"], g.xn[:, :, 0:T]).then_inc(s_st, 16)
                eng.wait_ge(s_st, 64)

            @block.tensor
            def _(eng):
                eng.wait_ge(s_par, 16 * loads[0])
                nc.tensor.transpose(g.ps[:, 0, 0:NPROW], prow[:, :], g.ident[0:NPROW, 0:NPROW]).then_inc(s_pt, 1)
                for i in range(3):
                    mm = nc.tensor.transpose(g.ps[:, 1, i * UT:(i + 1) * UT], cwrow[:, i, :], g.ident[0:UT, 0:UT])
                mm.then_inc(s_pt, 1)
                for i in range(UT):
                    mm = nc.tensor.transpose(g.ps[:, 2 + i // 32, i % 32 * 16:i % 32 * 16 + 16],
                                             crow[:, i * P:(i + 1) * P], g.ident[0:16, 0:16])
                mm.then_inc(s_pt, 1)
                for i in range(KT):
                    mm = nc.tensor.transpose(g.ps[:, 4, i * NB:(i + 1) * NB], shrow[:, i * P:(i + 1) * P],
                                             g.ident[0:NB, 0:NB])
                mm.then_inc(s_pt, 1)
                eng.wait_ge(s_pc, 5)
                for j in range(NT + 1):
                    n = P if j < NT else TS
                    eng.wait_ge(s_x[j % 3], 16 * (j // 3 + 1))
                    for h in range(2):
                        u = 2 * j + h
                        if u >= 4:
                            eng.wait_ge(s_xc, u - 3)
                        for c in range(4):
                            k = 4 * h + c
                            mm = nc.tensor.transpose(g.ps[:, u % 4, c * P:c * P + n],
                                                     xrow[0:n, j % 3, k * P:(k + 1) * P], g.ident[0:n, 0:n])
                        mm.then_inc(s_xt, 1)
                eng.wait_ge(s_xc, 2 * (NT + 1))
                n_pe(eng)
                eng.wait_ge(n_out, KT)
                for h in range(2):
                    for c in range(4):
                        k = 4 * h + c
                        mm = nc.tensor.transpose(g.ps[0:NB + 1, 4 + h, c * P:(c + 1) * P],
                                                 g.xn[:, k, SEQ - 1:T:NQ], g.ident)
                    mm.then_inc(s_lt, 1)

            @block.scalar
            def _(eng):
                for u in range(0, 2 * NT + 2, 2):
                    n = P if u // 2 < NT else TS
                    eng.wait_ge(s_xt, u + 1)
                    if u:
                        eng.wait_ge(s_xc, u)
                    j = u // 2
                    nc.scalar.copy(xt[:, 0:4, j * P:j * P + n],
                                   g.ps[:, u % 4, :].rearrange("p (c n) -> p c n", n=P)[:, :, 0:n]).then_inc(s_xc, 1)
                eng.wait_ge(s_xc, 2 * (NT + 1))
                n_act(eng)

            @block.vector
            def _(eng):
                eng.wait_ge(s_pt, 4)
                nc.vector.tensor_copy(g.par[:, :], g.ps[:, 0, 0:NPROW]).then_inc(s_pc, 1)
                nc.vector.tensor_copy(g.cw[:, :, :].rearrange("p a b -> p (a b)"), g.ps[:, 1, 0:3 * UT]).then_inc(s_pc, 1)
                nc.vector.tensor_copy(g.cst[:, 0:32, :].rearrange("p a b -> p (a b)"), g.ps[:, 2, :]).then_inc(s_pc, 1)
                nc.vector.tensor_copy(g.cst[:, 32:UT, :].rearrange("p a b -> p (a b)"),
                                      g.ps[:, 3, 0:(UT - 32) * 16]).then_inc(s_pc, 1)
                nc.vector.tensor_copy(g.xn[:, :, T:TP], g.ps[:, 4, 0:KT * NB].rearrange("p (k b) -> p k b", b=NB)).then_inc(s_pc, 1)
                for u in range(1, 2 * NT + 2, 2):
                    n = P if u // 2 < NT else TS
                    eng.wait_ge(s_xt, u + 1)
                    eng.wait_ge(s_xc, u)
                    j = u // 2
                    nc.vector.tensor_copy(xt[:, 4:8, j * P:j * P + n],
                                          g.ps[:, u % 4, :].rearrange("p (c n) -> p c n", n=P)[:, :, 0:n]).then_inc(s_xc, 1)
                n_dve(eng)
                for h in range(2):
                    eng.wait_ge(s_lt, h + 1)
                    nc.vector.tensor_copy(last[:, h * 512:(h + 1) * 512], g.ps[0:NB + 1, 4 + h, :]).then_inc(s_lc, 1)


def in_pairs(eng, n, body):
    body(0, 0)
    body(1, 1)
    if n // 2 > 1:
        with eng.Fori(1, n // 2) as i:
            body(2 * i, 0)
            body(2 * i + 1, 1)
    if n % 2:
        body(n - 1, 0)


def first(t):
    return isinstance(t, int) and t < 2


def wait_apart(eng, sem, value, tick):
    eng.wait_ge(sem, value)
    eng.sem_inc(tick)


def stage_branch_a(g):
    nc = g.nc
    with ExitStack() as ctx:
        sb = lambda name, shape, dt=F32: ctx.enter_context(nc.sbuf_tensor(name, shape, dt))
        g.av = sb("av", [P, PAIRS, T])
        g.at = sb("at", [P, PAIRS, T])
        g.bn = sb("bn", [P, PAIRS, T])
        g.sc = sb("sc", [P, NU - 1, PAIRS])
        g.scs = sb("scs", [P, PAIRS, NB])
        a_prepare(g)
        a_delta_rule(g)
        a_finish(g)


def a_project(g):
    nc, a = g.nc, g.a
    w = a["w_in"][0].rearrange("(k p) f -> p k f", p=P)
    with ExitStack() as ctx:
        sb = lambda name, shape, dt=F32: ctx.enter_context(nc.sbuf_tensor(name, shape, dt))
        wt = sb("ap_w", [P, 2, KT, P])
        raw = sb("ap_raw", [P, 2, 1 + TP])
        dif = sb("ap_dif", [P, 2, T])
        s_w = [g.sem(f"ap_w{i}") for i in range(2)]
        s_mm, s_ev, s_z, s_d, s_mix = (g.sem(f"ap_{n}") for n in ("mm", "ev", "z", "d", "mix"))
        with nc.Block() as block:
            @block.sync
            def _(eng):
                def body(t, b):
                    if not first(t):
                        eng.wait_ge(s_mm, t - 1)
                    eng.dma_start(wt[:, b, :, :], w[:, :, bass.ds(t * P, P)]).then_inc(s_w[b], 16)
                in_pairs(eng, AT, body)

            @block.tensor
            def _(eng):
                def body(t, b):
                    eng.wait_ge(s_w[b], 16 * ((t - b) // 2 + 1) if isinstance(t, int) else 8 * (t - b) + 16)
                    if not first(t):
                        eng.wait_ge(s_ev, t - 1)
                    for c, (c0, n) in enumerate(CHP):
                        for k in range(KT):
                            mm = nc.tensor.matmul(g.ps[:, 3 * b + c, 0:n], wt[:, b, k, :], g.xn[:, k, c0:c0 + n],
                                                  start=(k == 0), stop=(k == KT - 1))
                    mm.then_inc(s_mm, 1)
                in_pairs(eng, AT, body)

            @block.scalar
            def _(eng):
                def body(t, b):
                    eng.wait_ge(s_mm, t + 1)
                    if not first(t):
                        eng.wait_ge(s_mix, t - 1)
                    nc.scalar.copy(raw[:, b, 1:1 + CHP[0][1]], g.ps[:, 3 * b, 0:CHP[0][1]])
                    nc.scalar.copy(raw[:, b, 1 + CHP[1][0]:1 + CHP[2][0]], g.ps[:, 3 * b + 1, 0:CHP[1][1]])
                    nc.scalar.copy(raw[:, b, 1 + CHP[2][0]:1 + TP], g.ps[:, 3 * b + 2, 0:CHP[2][1]]).then_inc(s_ev, 1)
                in_pairs(eng, AT, body)

            @block.vector
            def _(eng):
                nc.vector.memset(raw[:, :, 0:1], 0.0).then_inc(s_z, 1)
                eng.wait_ge(s_z, 1)

                def body(t, b):
                    eng.wait_ge(s_ev, t + 1)
                    if not first(t):
                        eng.wait_ge(s_mix, t - 1)
                    nc.vector.tensor_tensor(dif[:, b, :], raw[:, b, 0:T], raw[:, b, 1:1 + T], ALU.subtract).then_inc(s_d, 1)
                    eng.wait_ge(s_d, 2 * t + 1)
                    nc.vector.tensor_tensor(dif[:, b, SEQ:T:NQ], raw[:, b, 1 + T:1 + TP],
                                            raw[:, b, 1 + SEQ:1 + T:NQ], ALU.subtract).then_inc(s_d, 1)
                    eng.wait_ge(s_d, 2 * t + 2)
                    nc.vector.scalar_tensor_tensor(
                        out=g.pa[:, bass.ds(t, 1), :].rearrange("p a t -> p (a t)"), in0=dif[:, b, :],
                        scalar=g.par[:, bass.ds(PROWS["rwkv_mu"][0] + t, 1)], in1=raw[:, b, 1:1 + T],
                        op0=ALU.mult, op1=ALU.add).then_inc(s_mix, 1)
                in_pairs(eng, AT, body)


def a_prepare(g):
    nc, a, pa = g.nc, g.a, g.pa
    R, K, V, LWA, LG = 0, 3, 6, 9, 10
    with ExitStack() as ctx:
        sb = lambda name, shape, dt=F32: ctx.enter_context(nc.sbuf_tensor(name, shape, dt))
        wa2 = sb("wa2", [P, AW])
        keep = sb("keep", [P, T])
        ld = sb("ld", [P, PAIRS, T])
        cu = sb("cu", [P, PAIRS, T])
        kk = sb("kk", [P, PAIRS, T])
        tmp = sb("tmp", [P, 2, T])
        ex = sb("ex", [P, 3, T])
        mid = sb("mid", [P, NU - 1, PAIRS])
        end = sb("end", [P, NU - 1, PAIRS])
        ends = sb("ends", [P, PAIRS, NB])
        omk = sb("omk", [P, PAIRS])
        names = ("w", "th", "lo", "sg", "chain", "cu", "kk", "sq", "ss", "rk", "bs", "nm", "rt", "ex", "ux", "end", "kn")
        s = {n: g.sem(f"pp_{n}") for n in names}
        cols = lambda t: t.rearrange("p (c n) -> p c n", n=CHUNK)
        with nc.Block() as block:
            @block.sync
            def _(eng):
                eng.dma_start(wa2[0:HD, :], a["rwkv_w2"][0]).then_inc(s["w"], 16)
                eng.dma_start(wa2[HD:P, :], a["rwkv_a2"][0]).then_inc(s["w"], 16)

            @block.tensor
            def _(eng):
                eng.wait_ge(s["w"], 32)
                eng.wait_ge(s["th"], 1)
                for p in range(PAIRS):
                    if p:
                        eng.wait_ge(s["sg"], 2 * p)
                    for half in range(2):
                        rows = slice(HD * half, HD * half + HD)
                        for c, (c0, n) in enumerate(CH):
                            mm = nc.tensor.matmul(g.ps[:, 3 * half + c, 0:n], wa2[rows, p * P:(p + 1) * P],
                                                  pa[rows, LWA, c0:c0 + n], start=True, stop=True)
                        mm.then_inc(s["lo"], 1)
                eng.wait_ge(s["sg"], 2 * PAIRS)
                for p in range(PAIRS):
                    if p:
                        eng.wait_ge(s["nm"], 2 * p)
                    eng.wait_ge(s["sq"], p + 1)
                    for c, (c0, n) in enumerate(CH):
                        mm = nc.tensor.matmul(g.ps[:, c, 0:n], g.blk, ex[:, p, c0:c0 + n], start=True, stop=True)
                    mm.then_inc(s["ss"], 1)
                    eng.wait_ge(s["rk"], p + 1)
                    for c, (c0, n) in enumerate(CH):
                        mm = nc.tensor.matmul(g.ps[:, 3 + c, 0:n], g.blk, g.at[:, p, c0:c0 + n], start=True, stop=True)
                    mm.then_inc(s["bs"], 1)

            @block.scalar
            def _(eng):
                nc.scalar.activation(pa[0:HD, LWA, :], pa[0:HD, LWA, :], ACT.Tanh).then_inc(s["th"], 1)
                for p in range(PAIRS):
                    for half, (dst, par) in enumerate(((ld, "rwkv_w0"), (g.av, "rwkv_a0"))):
                        eng.wait_ge(s["lo"], 2 * p + half + 1)
                        for c, (c0, n) in enumerate(CH):
                            i = nc.scalar.activation(dst[:, p, c0:c0 + n], g.ps[:, 3 * half + c, 0:n], ACT.Sigmoid,
                                                     bias=g.col(par, p))
                        i.then_inc(s["sg"], 1)
                for p in range(PAIRS):
                    eng.wait_ge(s["kk"], p + 1)
                    nc.scalar.activation(ex[:, p, :], kk[:, p, :], ACT.Square).then_inc(s["sq"], 1)
                for p in range(PAIRS):
                    eng.wait_ge(s["nm"], 2 * p + 1)
                    nc.scalar.activation(ex[:, p, :], ex[:, p, :], ACT.Sqrt).then_inc(s["rt"], 1)
                eng.wait_ge(s["end"], 1)
                nc.scalar.activation(g.sc[:, :, :], end[:, :, :], ACT.Exp)
                nc.scalar.activation(g.scs[:, :, :], ends[:, :, :], ACT.Exp).then_inc(s["end"], 1)
                for p in range(PAIRS):
                    eng.wait_ge(s["kn"], PAIRS)
                    if p:
                        eng.wait_ge(s["ux"], p)
                    nc.scalar.activation(ex[:, 0, :], cu[:, p, :], ACT.Exp)
                    nc.scalar.activation(ex[:, 1, :], cu[:, p, :], ACT.Exp, scale=-1.0)
                    nc.scalar.activation(ex[:, 2, :], ld[:, p, :], ACT.Exp).then_inc(s["ex"], 1)

            @block.vector
            def _(eng):
                n_chain = [0]

                def link(ins):
                    n_chain[0] += 1
                    ins.then_inc(s["chain"], 1)
                    eng.wait_ge(s["chain"], n_chain[0])

                V_ = nc.vector
                link(V_.memset(keep[:, :], 1.0))
                link(V_.memset(keep[:, 0:SEQ:CHUNK], 0.0))
                link(V_.memset(keep[:, SEQ:T:NQ], 0.0))
                k0 = PROWS["rwkv_k_a"][0]
                link(V_.tensor_scalar(omk[:, :], g.par[:, k0:k0 + PAIRS], -1.0, 1.0, ALU.mult, ALU.add))
                for p in range(PAIRS):
                    V_.tensor_scalar(kk[:, p, :], pa[:, K + p, :], g.col("rwkv_k_k", p), None, ALU.mult).then_inc(s["kk"], 1)
                    eng.wait_ge(s["sg"], 2 * p + 1)
                    link(V_.tensor_scalar(ld[:, p, :], ld[:, p, :], -float(np.exp(-0.5)), None, ALU.mult))
                    link(V_.tensor_tensor_scan(cu[:, p, :], keep[:, :], ld[:, p, :], 0.0, ALU.mult, ALU.add))
                    V_.tensor_copy(mid[:, :, p], cu[:, p, CHUNK // 2 - 1:SEQ:CHUNK])
                    V_.tensor_copy(end[:, :, p], cu[:, p, CHUNK - 1:SEQ:CHUNK])
                    link(V_.tensor_copy(ends[:, p, :], cu[:, p, SEQ + NQ - 1:T:NQ]))
                    link(V_.tensor_tensor(cols(cu[:, p, 0:SEQ]), cols(cu[:, p, 0:SEQ]),
                                          mid[:, :, p:p + 1].broadcast_to([P, NU - 1, CHUNK]), ALU.subtract))
                    V_.tensor_tensor(ld[:, p, :], cu[:, p, :], ld[:, p, :], ALU.subtract).then_inc(s["cu"], 1)
                    eng.wait_ge(s["sg"], 2 * p + 2)
                    link(V_.tensor_scalar(tmp[:, 0, :], g.av[:, p, :], g.col("rwkv_k_a", p), omk[:, p:p + 1],
                                          ALU.mult, ALU.add))
                    link(V_.tensor_tensor(pa[:, K + p, :], pa[:, K + p, :], tmp[:, 0, :], ALU.mult))
                    V_.scalar_tensor_tensor(out=g.at[:, p, :], in0=pa[:, R + p, :], scalar=g.col("rwkv_r_k", p),
                                            in1=pa[:, K + p, :], op0=ALU.mult, op1=ALU.mult).then_inc(s["rk"], 1)
                link(V_.tensor_tensor(end[:, :, :], end[:, :, :], mid[:, :, :], ALU.subtract))
                V_.tensor_tensor(end[:, 0:NU - 2, :], end[:, 0:NU - 2, :], mid[:, 1:NU - 1, :], ALU.add).then_inc(s["end"], 1)
                for p in range(PAIRS):
                    eng.wait_ge(s["ss"], p + 1)
                    for c, (c0, n) in enumerate(CH):
                        i = V_.tensor_scalar(ex[:, p, c0:c0 + n], g.ps[:, c, 0:n], 1e-24, None, ALU.max)
                    i.then_inc(s["nm"], 1)
                    eng.wait_ge(s["bs"], p + 1)
                    for c, (c0, n) in enumerate(CH):
                        i = V_.tensor_tensor(g.bn[:, p, c0:c0 + n], g.ps[:, 3 + c, 0:n], pa[:, V + p, c0:c0 + n], ALU.mult)
                    i.then_inc(s["nm"], 1)
                for p in range(PAIRS):
                    eng.wait_ge(s["rt"], p + 1)
                    link(V_.reciprocal(tmp[:, 1, :], ex[:, p, :]))
                    V_.tensor_tensor(kk[:, p, :], kk[:, p, :], tmp[:, 1, :], ALU.mult).then_inc(s["kn"], 1)
                    eng.wait_ge(s["kn"], p + 1)
                for p in range(PAIRS):
                    eng.wait_ge(s["ex"], p + 1)
                    V_.tensor_tensor(pa[:, R + p, :], pa[:, R + p, :], ex[:, 0, :], ALU.mult)
                    V_.tensor_tensor(pa[:, K + p, :], pa[:, K + p, :], ex[:, 1, :], ALU.mult)
                    link(V_.tensor_tensor(g.av[:, p, :], g.av[:, p, :], ex[:, 1, :], ALU.mult))
                    V_.tensor_tensor(g.av[:, p, :], g.av[:, p, :], kk[:, p, :], ALU.mult)
                    V_.scalar_tensor_tensor(out=g.at[:, p, :], in0=kk[:, p, :], scalar=-1.0, in1=ex[:, 2, :],
                                            op0=ALU.mult, op1=ALU.mult).then_inc(s["ux"], 1)


def a_delta_rule(g):
    with ExitStack() as ctx:
        d = DeltaParts(g, ctx, "dp", 2, P)
        delta_prompt(g, ctx, d)
    with ExitStack() as ctx:
        d = DeltaParts(g, ctx, "ds", 1, TS)
        delta_sample(g, ctx, d)


R0, K0, V0 = 0, 3, 6
NM = 2 * LEVELS


class DeltaParts:

    def __init__(self, g, ctx, pre, nb, n):
        nc = g.nc
        sb = lambda name, shape, dt=F32: ctx.enter_context(nc.sbuf_tensor(f"{pre}_{name}", shape, dt))
        self.g, self.n = g, n
        self.msk = sb("msk", [n, NM + 6, n], I32)
        stg = sb("stg", [P, nb, 5, PAIRS, n])
        tok = sb("tok", [P, nb, 3, PAIRS, P])
        mats = [sb(x, [P, nb, 2, PAIRS, n]) for x in ("lm", "ak", "rb", "rk", "tm", "wm", "zm")]
        ym, um = sb("ym", [P, 2, PAIRS, HD]), sb("um", [P, 2, PAIRS, HD])
        names = ("c", "stg", "stv", "tp", "tk", "pr", "cp", "z", "ze", "pl", "lv", "y", "ye", "u", "ue",
                 "o", "oe", "se", "wi", "zi", "ft", "fe", "out", "x", "sx", "pe", "dve", "pool")
        self.s = {x: g.sem(f"{pre}_{x}") for x in names}
        self.all = (self.s, stg, tok, *mats, ym, um)

    def mask(self, i):
        return self.msk[0:self.n, i:i + 1, 0:self.n].broadcast_to([self.n, PAIRS, self.n])

    def banks(self, q, e):
        return self.g.ps[0:self.n, 2 * q + e, 0:PAIRS * P].rearrange("r (p n) -> r p n", n=P)[:, :, 0:self.n]

    def pe_products(self, eng, b, tp0, cp0):
        nc, g, n = self.g.nc, self.g, self.n
        s, stg = self.s, self.all[1]
        R, A, K, B, V = (stg[:, b, i] for i in range(5))
        eng.wait_ge(s["stg"], tp0 + 1)
        eng.wait_ge(s["stv"], tp0 + 1)
        for q, src in enumerate((K, B, V)):
            for p in range(PAIRS):
                mm = nc.tensor.transpose(g.ps[0:n, q, p * P:(p + 1) * P], src[:, p, :], g.ident)
        mm.then_inc(s["tp"], 1)
        for i, (q, lhs, rhs) in enumerate(((2, A, B), (3, B, A), (0, K, A), (1, B, R), (2, K, R))):
            if i == 2:
                eng.wait_ge(s["tk"], tp0 + 1)
            if i == 4:
                eng.wait_ge(s["cp"], cp0 + 1)
            for e, p, rows in HEADS:
                mm = nc.tensor.matmul(g.ps[0:n, 2 * q + e, p * P:p * P + n], lhs[rows, p, :], rhs[rows, p, :],
                                      start=True, stop=True)
            mm.then_inc(s["pr"], 1)

    def dve_products(self, eng, b, kind, cp0):
        s, _, _, lm, ak, rb, rk, tm, wm, _, _, _ = self.all
        mk = lambda i: self.mask(NM + 3 * kind + i)
        for i, (q, jobs) in enumerate(((2, ((lm, mk(0)), (tm, self.mask(0)))), (3, ((wm, self.mask(LEVELS)),)),
                                       (0, ((ak, mk(1)),)), (1, ((rb, mk(2)),)), (2, ((rk, mk(2)),)))):
            eng.wait_ge(s["zi"], 4)
            wait_apart(eng, s["pr"], cp0 + i + 1, s["dve"])
            for dst, m in jobs:
                for e in range(2):
                    ins = self.g.nc.vector.copy_predicated(dst[0:self.n, b, e], m, self.banks(q, e))
            ins.then_inc(s["cp"], 1)

    def pe_level(self, b, what, q):
        _, _, _, lm, _, _, _, tm, wm, zm, _, _ = self.all
        lhs, rhs = {"z": (lm, wm), "w": (tm, zm), "t": (zm, tm)}[what]
        for e, p, _ in HEADS:
            mm = self.g.nc.tensor.matmul(self.g.ps[0:self.n, 2 * q + e, p * P:p * P + self.n], lhs[0:self.n, b, e, p, :],
                                         rhs[0:self.n, b, e, p, :], start=True, stop=True)
        return mm

    def dve_level(self, b, dst, m, q):
        for e in range(2):
            ins = self.g.nc.vector.copy_predicated(dst[0:self.n, b, e], self.mask(m), self.banks(q, e))
        ins.then_inc(self.s["lv"], 1)


HEADS = [(e, p, slice(HD * e, HD * e + HD)) for e in range(2) for p in range(PAIRS)]


def delta_prompt(g, ctx, d):
    nc, a, pa, V_ = g.nc, g.a, g.pa, g.nc.vector
    sb = lambda name, shape, dt=F32: ctx.enter_context(nc.sbuf_tensor(name, shape, dt))
    st = sb("st", [P, PAIRS, HD])
    so = sb("so", [HD, PAIRS, P])
    s, stg, tok, lm, ak, rb, rk, tm, wm, zm, ym, um = d.all
    G = lambda q: slice(2 * q, 2 * q + 2)
    LV = 4 * (LEVELS - 1) - 2
    with nc.Block() as block:
        @block.sync
        def _(eng):
            eng.dma_start(d.msk[:, :, :], a["c_mask"][0:d.n, :, 0:d.n]).then_inc(s["c"], 16)
            eng.wait_ge(s["fe"], 1)
            eng.dma_start(g.o["wkv_prompt"][0, 0].rearrange("h v k -> v h k"),
                          so[:, :, :].rearrange("v p (e k) -> v (p e) k", e=2)).then_inc(s["out"], 16)
            eng.wait_ge(s["out"], 16)

        @block.gpsimd
        def _(eng):
            for i, t in enumerate((lm, ak, rb, rk)):
                eng.memset(t[:, :, :, :, :], 0.0).then_inc(s["zi"], 1)
            ident = g.ident.rearrange("p (a n) -> p a n", a=1).broadcast_to([P, 2 * PAIRS, P])

            def body(i, peeled):
                for b in range(2):
                    if not peeled:
                        eng.wait_ge(s["ue"], 2 * i + b - 1)
                        wait_apart(eng, s["o"], 2 * i + b - 1, s["pool"])
                    for q, t in enumerate((tm, wm)):
                        eng.tensor_copy(t[:, b].rearrange("p e a n -> p (e a) n"), ident).then_inc(s["wi"], 1)
                    c0 = (2 * i + b) * P
                    for q, t in enumerate((pa[:, R0:R0 + 3], g.at, pa[:, K0:K0 + 3], g.av)):
                        ins = eng.tensor_copy(stg[:, b, q], t[:, :, bass.ds(c0, P)])
                    ins.then_inc(s["stg"], 1)
            body(0, True)
            with eng.Fori(1, 4) as i:
                body(i, False)

        @block.tensor
        def _(eng):
            def sequential(b, u):
                tk, tb, tv = (tok[:, b, i] for i in range(3))
                eng.wait_ge(s["se"], u + 1)
                for e, p, rows in HEADS:
                    out = g.ps[:, e, p * HD:(p + 1) * HD]
                    nc.tensor.matmul(out, stg[rows, b, 1, p, :], st[rows, p, :], start=True, stop=False)
                    mm = nc.tensor.matmul(out, ak[:, b, e, p, :], tv[:, p, HD * e:HD * e + HD], start=False, stop=True)
                mm.then_inc(s["y"], 1)
                eng.wait_ge(s["ye"], u + 1)
                for e, p, rows in HEADS:
                    mm = nc.tensor.matmul(g.ps[:, 2 + e, p * HD:(p + 1) * HD], wm[:, b, e, p, :], ym[:, e, p, :],
                                          start=True, stop=True)
                mm.then_inc(s["u"], 1)
                wait_apart(eng, s["ue"], u + 1, s["pe"])
                for e, p, rows in HEADS:
                    out = g.ps[rows, 6 + e, p * HD:(p + 1) * HD]
                    hc = slice(HD * e, HD * e + HD)
                    nc.tensor.matmul(out, g.ident[rows, rows], st[rows, p, :], start=True, stop=False)
                    nc.tensor.matmul(out, tk[:, p, hc], tv[:, p, hc], start=False, stop=False)
                    mm = nc.tensor.matmul(out, tb[:, p, hc], um[:, e, p, :], start=False, stop=True)
                if not isinstance(u, int) or u:
                    wait_apart(eng, s["oe"], 2 * u, s["pe"])
                for e, p, rows in HEADS:
                    out = g.ps[rows, 4 + e, p * P:(p + 1) * P]
                    hc = slice(HD * e, HD * e + HD)
                    nc.tensor.matmul(out, st[rows, p, :], stg[rows, b, 0, p, :], start=True, stop=False)
                    nc.tensor.matmul(out, tv[:, p, hc], rk[:, b, e, p, :], start=False, stop=False)
                    mm = nc.tensor.matmul(out, um[:, e, p, :], rb[:, b, e, p, :], start=False, stop=True)
                mm.then_inc(s["o"], 1)

            def duo(i, peeled):
                for b in range(2):
                    u = 2 * i + b
                    if b == 0 and not peeled:
                        eng.wait_ge(s["oe"], 2 * u)
                        eng.wait_ge(s["se"], u + 1)
                    if not peeled or b:
                        eng.wait_ge(s["cp"], 5 * u)
                    d.pe_products(eng, b, u, 5 * u)
                for l in range(2, LEVELS + 1):
                    for b in range(2):
                        if l == 2:
                            if b == 0:
                                eng.wait_ge(s["cp"], 10 * i + 10)
                        elif l > 2:
                            eng.wait_ge(s["lv"], LV * i + 4 * (l - 2) - 2 + 2 * b)
                        d.pe_level(b, "z", b).then_inc(s["z"], 1)
                    for b in range(2):
                        eng.wait_ge(s["ze"], 12 * i + 2 * (l - 2) + b + 1)
                        for j, what in enumerate("wt" if l < LEVELS else "w"):
                            base = 4 * (l - 2) + 2 * b + j if l < LEVELS else 4 * (l - 2) + b
                            if b:
                                eng.wait_ge(s["lv"], LV * i + (base - 1 if l < LEVELS else base))
                            d.pe_level(b, what, 2 + j).then_inc(s["pl"], 1)
                eng.wait_ge(s["lv"], LV * i + LV)
                for b in range(2):
                    sequential(b, 2 * i + b)

            eng.wait_ge(s["wi"], 4)
            duo(0, True)
            with eng.Fori(1, 4) as i:
                duo(i, False)
            eng.wait_ge(s["se"], NU)
            for p in range(PAIRS):
                mm = nc.tensor.transpose(g.ps[0:HD, 6, p * P:(p + 1) * P], st[:, p, :], g.ident)
            mm.then_inc(s["ft"], 1)

        @block.scalar
        def _(eng):
            def sequential(b, u):
                eng.wait_ge(s["y"], u + 1)
                nc.scalar.copy(ym[:, :, :, :].rearrange("t e p v -> t e (p v)"),
                               g.ps[:, 0:2, 0:PAIRS * HD]).then_inc(s["ye"], 1)
                eng.wait_ge(s["o"], u + 1)
                for e in range(2):
                    rows = slice(HD * e, HD * e + HD)
                    nc.scalar.copy(g.oa[rows, :, bass.ds(u * P, P)],
                                   g.ps[rows, 4 + e, 0:PAIRS * P].rearrange("r (p t) -> r p t", t=P)).then_inc(s["oe"], 1)

            def duo(i):
                for b in range(2):
                    u = 2 * i + b
                    eng.wait_ge(s["tp"], u + 1)
                    nc.scalar.copy(tok[:, b].rearrange("t q p n -> t q (p n)"), g.ps[:, 0:3, 0:PAIRS * P]).then_inc(s["tk"], 1)
                for l in range(2, LEVELS + 1):
                    for b in range(2):
                        eng.wait_ge(s["z"], 12 * i + 2 * (l - 2) + b + 1)
                        nc.scalar.copy(zm[:, b].rearrange("t e p n -> t e (p n)"),
                                       g.ps[:, G(b), 0:PAIRS * P]).then_inc(s["ze"], 1)
                for b in range(2):
                    sequential(b, 2 * i + b)
            def stage_v(i, peeled):
                for b in range(2):
                    if not peeled:
                        eng.wait_ge(s["tp"], 2 * i + b - 1)
                    nc.scalar.copy(stg[:, b, 4], pa[:, V0:V0 + 3, bass.ds((2 * i + b) * P, P)]).then_inc(s["stv"], 1)
            stage_v(0, True)
            duo(0)
            with eng.Fori(1, 4) as i:
                stage_v(i, False)
                duo(i)

        @block.vector
        def _(eng):
            eng.wait_ge(s["c"], 16)
            eng.wait_ge(s["zi"], 4)
            V_.memset(st[:, :, :], 0.0).then_inc(s["se"], 1)

            def sequential(b, u):
                eng.wait_ge(s["u"], u + 1)
                V_.tensor_copy(um[:, :, :, :].rearrange("t e p v -> t e (p v)"),
                               g.ps[:, 2:4, 0:PAIRS * HD]).then_inc(s["ue"], 1)
                eng.wait_ge(s["o"], u + 1)
                for e in range(2):
                    rows = slice(HD * e, HD * e + HD)
                    ins = V_.tensor_tensor(st[rows, :, :],
                                           g.ps[rows, 6 + e, 0:PAIRS * HD].rearrange("r (p v) -> r p v", v=HD),
                                           g.sc[rows, bass.ds(u, 1), :].rearrange("r a p -> r (a p)").rearrange(
                                               "r (p a) -> r p a", a=1).broadcast_to([HD, PAIRS, HD]), ALU.mult)
                ins.then_inc(s["se"], 1)

            def duo(i, peeled):
                for b in range(2):
                    u = 2 * i + b
                    eng.wait_ge(s["wi"], 2 * u + 2)
                    d.dve_products(eng, b, 0, 5 * u)
                for l in range(2, LEVELS + 1):
                    for b in range(2):
                        base = 11 * i + 2 * (l - 2)
                        for j in range(2 if l < LEVELS else 1):
                            n_pl = LV * i + 4 * (l - 2) + (2 * b + j if l < LEVELS else b)
                            wait_apart(eng, s["pl"], n_pl + 1, s["dve"])
                            d.dve_level(b, (wm, tm)[j], (LEVELS + l - 1, l - 1)[j], 2 + j)
                for b in range(2):
                    sequential(b, 2 * i + b)
            duo(0, True)
            with eng.Fori(1, 4) as i:
                duo(i, False)
            eng.wait_ge(s["ft"], 1)
            V_.tensor_copy(so[:, :, :].rearrange("v p k -> v (p k)"), g.ps[0:HD, 6, 0:PAIRS * P]).then_inc(s["fe"], 1)


def delta_sample(g, ctx, d):
    nc, a, pa, V_ = g.nc, g.a, g.pa, g.nc.vector
    sb = lambda name, shape, dt=F32: ctx.enter_context(nc.sbuf_tensor(name, shape, dt))
    sr = sb("sr", [HD, NB, AH, HD])
    s0 = sb("s0", [P, PAIRS, NB, HD])
    sn = sb("sn", [HD, NB, AH, HD])
    am = sb("am", [P, PAIRS, NB, TS])
    ux = sb("ux", [P, 2, PAIRS, NB, HD])
    vx = sb("vx", [P, 2, PAIRS, NB, HD])
    colm = sb("colm", [P, NB, TS])
    rowm = sb("rowm", [TS, NB])
    s, stg, tok, lm, ak, rb, rk, tm, wm, zm, ym, um = d.all
    tk, tb, tv = (tok[:, 0, i] for i in range(3))
    NL = 3
    with nc.Block() as block:
        @block.sync
        def _(eng):
            eng.dma_start(d.msk[:, :, :], a["c_mask"][0:d.n, :, 0:d.n]).then_inc(s["c"], 16)
            eng.dma_start(colm[:, :, :], a["c_col"]).then_inc(s["c"], 16)
            eng.dma_start(rowm[:, :], a["c_row"]).then_inc(s["c"], 16)
            for b in range(NB):
                eng.dma_start(sr[:, b], a["state_wkv"][0, b].rearrange("h v k -> v h k")).then_inc(s["sx"], 16)
            for b in range(NB):
                eng.wait_ge(s["fe"], 2 * PAIRS)
                eng.dma_start(g.o["wkv_sample"][0, b].rearrange("h v k -> v h k"), sn[:, b]).then_inc(s["out"], 16)
            eng.wait_ge(s["out"], 16 * NB)

        @block.gpsimd
        def _(eng):
            for t in (tok, lm, ak, rb, rk, ux, vx):
                eng.memset(t[:, :, :, :, :], 0.0).then_inc(s["zi"], 1)
            eng.memset(um[:, :, :, :], 0.0).then_inc(s["zi"], 1)
            ident = g.ident[0:TS, 0:TS].rearrange("p (a n) -> p a n", a=1).broadcast_to([TS, 2 * PAIRS, TS])
            for t in (tm, wm):
                eng.tensor_copy(t[0:TS, 0].rearrange("p e a n -> p (e a) n"), ident).then_inc(s["wi"], 1)
            for q, t in enumerate((pa[:, R0:R0 + 3], g.at, pa[:, K0:K0 + 3], g.av)):
                ins = eng.tensor_copy(stg[:, 0, q], t[:, :, SEQ:T])
            ins.then_inc(s["stg"], 1)

        @block.tensor
        def _(eng):
            d.pe_products(eng, 0, 0, 0)
            for l in range(2, NL + 1):
                eng.wait_ge(s["cp"], 5)
                eng.wait_ge(s["lv"], 2 * (l - 2))
                d.pe_level(0, "z", 0).then_inc(s["z"], 1)
                eng.wait_ge(s["ze"], l - 1)
                d.pe_level(0, "w", 2).then_inc(s["pl"], 1)
                d.pe_level(0, "t", 3).then_inc(s["pl"], 1)
            eng.wait_ge(s["lv"], 2 * (NL - 1))
            eng.wait_ge(s["sx"], 16 * NB)
            for p in range(PAIRS):
                for b in range(NB):
                    mm = nc.tensor.transpose(g.ps[:, 2 + p, b * HD:(b + 1) * HD],
                                             sr[:, b, 2 * p:2 * p + 2, :].rearrange("v h k -> v (h k)"),
                                             g.ident[0:HD, 0:HD])
            mm.then_inc(s["x"], 1)
            eng.wait_ge(s["se"], 1)
            for e, p, rows in HEADS:
                out = g.ps[0:TS, e, p * HD:(p + 1) * HD]
                for b in range(NB):
                    nc.tensor.matmul(out, am[rows, p, b, :], s0[rows, p, b, :], start=(b == 0), stop=False)
                mm = nc.tensor.matmul(out, ak[:, 0, e, p, :], tv[:, p, HD * e:HD * e + HD], start=False, stop=True)
            mm.then_inc(s["y"], 1)
            eng.wait_ge(s["ye"], 1)
            for e, p, rows in HEADS:
                mm = nc.tensor.matmul(g.ps[0:TS, 2 + e, p * HD:(p + 1) * HD], wm[0:TS, 0, e, p, :], ym[0:TS, e, p, :],
                                      start=True, stop=True)
            mm.then_inc(s["u"], 1)
            eng.wait_ge(s["ue"], 1)
            for e, p, rows in HEADS:
                hc = slice(HD * e, HD * e + HD)
                for b in range(NB):
                    nc.tensor.matmul(g.ps[rows, e, p * TS + NQ * b:p * TS + NQ * b + NQ], s0[rows, p, b, :],
                                     stg[rows, 0, 0, p, NQ * b:NQ * b + NQ], start=(b == 0), stop=False,
                                     skip_group_check=True)
                out = g.ps[rows, e, p * TS:(p + 1) * TS]
                nc.tensor.matmul(out, tv[:, p, hc], rk[:, 0, e, p, :], start=False, stop=False, skip_group_check=True)
                mm = nc.tensor.matmul(out, um[:, e, p, :], rb[:, 0, e, p, :], start=False, stop=True,
                                      skip_group_check=True)
            mm.then_inc(s["o"], 1)
            eng.wait_ge(s["ue"], 2)
            for e, p, rows in HEADS:
                out = g.ps[rows, 2 + 2 * p + e, :]
                hc = slice(HD * e, HD * e + HD)
                nc.tensor.matmul(out, g.ident[rows, rows], s0[rows, p].rearrange("k b v -> k (b v)"), start=True, stop=False)
                nc.tensor.matmul(out, tk[:, p, hc], vx[:, e, p].rearrange("t b v -> t (b v)"), start=False, stop=False)
                mm = nc.tensor.matmul(out, tb[:, p, hc], ux[:, e, p].rearrange("t b v -> t (b v)"), start=False, stop=True)
            mm.then_inc(s["o"], 1)
            eng.wait_ge(s["oe"], 2)
            eng.wait_ge(s["se"], 2)
            for i in range(2 * PAIRS):
                p, half = i // 2, i % 2
                for j in range(4):
                    mm = nc.tensor.transpose(g.ps[0:HD, i, j * P:(j + 1) * P], s0[:, p, 4 * half + j, :], g.ident)
                mm.then_inc(s["ft"], 1)

        @block.scalar
        def _(eng):
            nc.scalar.copy(stg[:, 0, 4], pa[:, V0:V0 + 3, SEQ:T]).then_inc(s["stv"], 1)
            eng.wait_ge(s["tp"], 1)
            eng.wait_ge(s["zi"], 8)
            nc.scalar.copy(tok[0:TS, 0].rearrange("t q p n -> t q (p n)"), g.ps[0:TS, 0:3, 0:PAIRS * P]).then_inc(s["tk"], 1)
            for l in range(2, NL + 1):
                eng.wait_ge(s["z"], l - 1)
                for e in range(2):
                    ins = nc.scalar.copy(zm[0:TS, 0, e], d.banks(0, e))
                ins.then_inc(s["ze"], 1)
            eng.wait_ge(s["y"], 1)
            nc.scalar.copy(ym[0:TS, :, :, :].rearrange("t e p v -> t e (p v)"), g.ps[0:TS, 0:2, 0:PAIRS * HD]).then_inc(s["ye"], 1)
            eng.wait_ge(s["o"], 1)
            for e in range(2):
                rows = slice(HD * e, HD * e + HD)
                nc.scalar.copy(g.oa[rows, :, SEQ:T], g.ps[rows, e, 0:PAIRS * TS].rearrange("r (p t) -> r p t", t=TS)).then_inc(s["oe"], 1)
            eng.wait_ge(s["oe"], 2)

        @block.vector
        def _(eng):
            eng.wait_ge(s["c"], 48)
            eng.wait_ge(s["zi"], 8)
            eng.wait_ge(s["wi"], 2)
            d.dve_products(eng, 0, 1, 0)
            for l in range(2, NL + 1):
                for j in range(2):
                    eng.wait_ge(s["pl"], 2 * (l - 2) + j + 1)
                    d.dve_level(0, (wm, tm)[j], (LEVELS + l - 1, l - 1)[j], 2 + j)
            eng.wait_ge(s["stg"], 1)
            for p in range(PAIRS):
                V_.tensor_tensor(am[:, p], stg[:, 0, 1, p:p + 1, :].broadcast_to([P, NB, TS]), colm[:, :, :], ALU.mult)
            eng.wait_ge(s["x"], 1)
            V_.tensor_copy(s0[:, :, :, :].rearrange("k p b v -> k p (b v)"), g.ps[:, 2:5, :]).then_inc(s["se"], 1)
            eng.wait_ge(s["u"], 1)
            V_.tensor_copy(um[0:TS, :, :, :].rearrange("t e p v -> t e (p v)"), g.ps[0:TS, 2:4, 0:PAIRS * HD]).then_inc(s["ue"], 1)
            eng.wait_ge(s["ue"], 1)
            eng.wait_ge(s["tk"], 1)
            rm = rowm[:, :].rearrange("t (b a) -> t b a", a=1).broadcast_to([TS, NB, HD])
            for e, p, rows in HEADS:
                V_.tensor_tensor(ux[0:TS, e, p], um[0:TS, e, p:p + 1, :].broadcast_to([TS, NB, HD]), rm, ALU.mult)
                ins = V_.tensor_tensor(vx[0:TS, e, p], tv[0:TS, p:p + 1, HD * e:HD * e + HD].broadcast_to([TS, NB, HD]), rm, ALU.mult)
            ins.then_inc(s["ue"], 1)
            eng.wait_ge(s["o"], 2)
            for e, p, rows in HEADS:
                ins = V_.tensor_tensor(s0[rows, p], g.ps[rows, 2 + 2 * p + e, :].rearrange("k (b v) -> k b v", v=HD),
                                       g.scs[rows, p, :].rearrange("k (b a) -> k b a", a=1).broadcast_to([HD, NB, HD]), ALU.mult)
            ins.then_inc(s["se"], 1)
            for i in range(2 * PAIRS):
                p, half = i // 2, i % 2
                eng.wait_ge(s["ft"], i + 1)
                V_.tensor_copy(sn[:, 4 * half:4 * half + 4, 2 * p:2 * p + 2, :].rearrange("v b h k -> v b (h k)"),
                               g.ps[0:HD, i, :].rearrange("v (b x) -> v b x", x=P)).then_inc(s["fe"], 1)


def a_finish(g):
    nc, a, oa, V_ = g.nc, g.a, g.oa, g.nc.vector
    with ExitStack() as ctx:
        sb = lambda name, shape, dt=F32: ctx.enter_context(nc.sbuf_tensor(name, shape, dt))
        g2 = sb("g2", [P, AW])
        om = sb("om", [P, PAIRS, T])
        sq = sb("af_sq", [P, PAIRS, T])
        iv = sb("af_iv", [P, PAIRS, T])
        geps = sb("geps", [P, 1])
        names = ("w", "lg", "mean", "om", "sq", "var", "ms", "rt", "chain", "g", "done")
        s = {n: g.sem(f"af_{n}") for n in names}
        with nc.Block() as block:
            @block.sync
            def _(eng):
                eng.dma_start(g2[:, :], a["rwkv_g2"][0]).then_inc(s["w"], 16)

            @block.tensor
            def _(eng):
                def put(lhs, rhs, b0, inc):
                    for c, (c0, n) in enumerate(CH):
                        mm = nc.tensor.matmul(g.ps[:, b0 + c, 0:n], lhs, rhs[:, c0:c0 + n], start=True, stop=True)
                    mm.then_inc(s[inc], 1)
                for p in range(PAIRS):
                    if p > 0:
                        eng.wait_ge(s["om"], p)
                    put(g.blk, oa[:, p, :], 0, "mean")
                    if p > 0:
                        eng.wait_ge(s["ms"], p)
                    eng.wait_ge(s["sq"], p + 1)
                    put(g.blk, sq[:, p, :], 3, "var")
                eng.wait_ge(s["w"], 16)
                eng.wait_ge(s["lg"], 1)
                for p in range(PAIRS):
                    eng.wait_ge(s["om"], PAIRS)
                    eng.wait_ge(s["ms"], PAIRS)
                    if p == 2:
                        eng.wait_ge(s["done"], 1)
                    put(g2[:, p * P:(p + 1) * P], g.pa[:, 10, :], 3 * (p % 2), "g")

            @block.scalar
            def _(eng):
                nc.scalar.activation(g.pa[:, 10, :], g.pa[:, 10, :], ACT.Sigmoid).then_inc(s["lg"], 1)
                for p in range(PAIRS):
                    eng.wait_ge(s["om"], p + 1)
                    nc.scalar.activation(sq[:, p, :], om[:, p, :], ACT.Square).then_inc(s["sq"], 1)
                for p in range(PAIRS):
                    eng.wait_ge(s["ms"], p + 1)
                    nc.scalar.activation(iv[:, p, :], iv[:, p, :], ACT.Sqrt).then_inc(s["rt"], 1)

            @block.vector
            def _(eng):
                n_chain = [0]

                def link(ins):
                    n_chain[0] += 1
                    ins.then_inc(s["chain"], 1)
                    eng.wait_ge(s["chain"], n_chain[0])
                for p in range(PAIRS):
                    eng.wait_ge(s["mean"], p + 1)
                    for c, (c0, n) in enumerate(CH):
                        ins = V_.scalar_tensor_tensor(out=om[:, p, c0:c0 + n], in0=g.ps[:, c, 0:n], scalar=-1.0 / HD,
                                                      in1=oa[:, p, c0:c0 + n], op0=ALU.mult, op1=ALU.add)
                    ins.then_inc(s["om"], 1)
                    eng.wait_ge(s["var"], p + 1)
                    for c, (c0, n) in enumerate(CH):
                        ins = V_.tensor_scalar(iv[:, p, c0:c0 + n], g.ps[:, 3 + c, 0:n], 1.0 / HD, GN_EPS, ALU.mult, ALU.add)
                    ins.then_inc(s["ms"], 1)
                for p in range(PAIRS):
                    eng.wait_ge(s["rt"], p + 1)
                    link(V_.reciprocal(sq[:, p, :], iv[:, p, :]))
                    link(V_.tensor_tensor(om[:, p, :], om[:, p, :], sq[:, p, :], ALU.mult))
                    link(V_.scalar_tensor_tensor(out=om[:, p, :], in0=om[:, p, :], scalar=g.col("rwkv_ln_w", p),
                                                 in1=g.bn[:, p, :], op0=ALU.mult, op1=ALU.add))
                    eng.wait_ge(s["g"], p + 1)
                    for c, (c0, n) in enumerate(CH):
                        ins = V_.scalar_tensor_tensor(out=oa[:, p, c0:c0 + n], in0=om[:, p, c0:c0 + n],
                                                      scalar=g.col("rwkv_ln_b", p), in1=g.ps[:, 3 * (p % 2) + c, 0:n],
                                                      op0=ALU.add, op1=ALU.mult)
                    ins.then_inc(s["done"], 1)


def project(g, pre, w, n_tiles, src, dst):
    nc = g.nc
    with ExitStack() as ctx:
        wt = ctx.enter_context(nc.sbuf_tensor(f"{pre}_w", [P, 2, KT, P], F32))
        s_w = [g.sem(f"{pre}_w{i}") for i in range(2)]
        s_mm, s_a, s_v = (g.sem(f"{pre}_{n}") for n in ("mm", "a", "v"))
        with nc.Block() as block:
            @block.sync
            def _(eng):
                def body(t, b):
                    if not first(t):
                        eng.wait_ge(s_mm, t - 1)
                    eng.dma_start(wt[:, b, :, :], w[:, :, bass.ds(t * P, P)]).then_inc(s_w[b], 16)
                in_pairs(eng, n_tiles, body)

            @block.tensor
            def _(eng):
                def body(t, b):
                    eng.wait_ge(s_w[b], 16 * ((t - b) // 2 + 1) if isinstance(t, int) else 8 * (t - b) + 16)
                    if not first(t):
                        eng.wait_ge(s_a, t - 1)
                        eng.wait_ge(s_v, t - 1)
                    for c, (c0, n) in enumerate(CH):
                        for k in range(KT):
                            mm = nc.tensor.matmul(g.ps[:, 3 * b + c, 0:n], wt[:, b, k, :], src[:, k, c0:c0 + n],
                                                  start=(k == 0), stop=(k == KT - 1))
                    mm.then_inc(s_mm, 1)
                in_pairs(eng, n_tiles, body)

            def out(t, c0, n):
                return dst[:, bass.ds(t, 1), c0:c0 + n].rearrange("p a t -> p (a t)")

            @block.scalar
            def _(eng):
                def body(t, b):
                    eng.wait_ge(s_mm, t + 1)
                    nc.scalar.copy(out(t, *CH[0]), g.ps[:, 3 * b, 0:CH[0][1]]).then_inc(s_a, 1)
                in_pairs(eng, n_tiles, body)

            @block.vector
            def _(eng):
                def body(t, b):
                    eng.wait_ge(s_mm, t + 1)
                    n = CH[1][1]
                    nc.vector.tensor_copy(out(t, CH[1][0], 2 * n).rearrange("p (c t) -> p c t", t=n),
                                          g.ps[:, 3 * b + 1:3 * b + 3, 0:n]).then_inc(s_v, 1)
                in_pairs(eng, n_tiles, body)


def reload_xn(g, ctx, pre):
    nc = g.nc
    g.xn = ctx.enter_context(nc.sbuf_tensor(f"{pre}_xn", [P, KT, T], F32))
    s_x = g.sem(f"{pre}_x")
    with nc.Block() as block:
        @block.sync
        def _(eng):
            eng.dma_start(g.xn[:, :, :], g.dr["xn"]).then_inc(s_x, 16)
            eng.wait_ge(s_x, 16)


A_COLS, SB_COLS, DIL_COLS = 1408, 768, 1152


def stage_branch_b(g):
    nc, a = g.nc, g.a
    w_in = a["w_in"][0].rearrange("(k p) f -> p k f", p=P)
    with ExitStack() as ctx:
        g.qb = ctx.enter_context(nc.sbuf_tensor("qb", [P, 6, T], F32))
        with ExitStack() as xctx:
            reload_xn(g, xctx, "bx")
            project(g, "bp", w_in[:, :, A_COLS:A_COLS + SB_COLS], 6, g.xn, g.qb)
        g.kvt = ctx.enter_context(nc.sbuf_tensor("kvt", [P, SEQ // P + 1, 512], F32))
        b_prompt(g)
        b_sample(g)


def b_prompt(g):
    nc, a, V_ = g.nc, g.a, g.nc.vector
    NT = SEQ // P
    with ExitStack() as ctx:
        sb = lambda name, shape, dt=F32: ctx.enter_context(nc.sbuf_tensor(name, shape, dt))
        x = sb("bq_x", [P, 3, 512])
        l, sp, at = (sb(f"bq_{n}", [P, 2, 512]) for n in ("l", "sp", "at"))
        later = sb("bq_later", [P, P], I32)
        zero = sb("bq_zero", [P, P])
        names = ("c", "kt", "ka", "kv", "st", "z", "x", "l", "sp", "tri", "arg", "at", "am", "pv", "ob", "ch", "raw")
        s = {n: g.sem(f"bq_{n}") for n in names}
        units = [(p, j, b, e) for p in range(2) for j in range(2) for b in range(4 * j + 3, -1, -1) for e in range(2)]
        NUN = len(units)
        top = lambda j, b: b == 4 * j + 3
        skip = lambda j, b: max(0, b * P - 512 * j)
        diag = lambda j, b: b >= 4 * j
        masked = lambda i: sum(diag(j, b) for _, j, b, _ in units[:i + 1])
        group = lambda i: units[i][0] * 2 + units[i][1]

        with nc.Block() as block:
            @block.sync
            def _(eng):
                eng.dma_start(later[:, :], a["c_later"]).then_inc(s["c"], 16)
                eng.wait_ge(s["ka"], NT // 2 + 1)
                eng.wait_ge(s["kv"], NT // 2)
                for n, c in (("k", 0), ("v", 256)):
                    eng.dma_start(g.o[f"sb_{n}_prompt"][0, 0].rearrange("(j p) h d -> p j (h d)", p=P),
                                  g.kvt[:, 0:NT, c:c + 256]).then_inc(s["st"], 16)
                    eng.dma_start(g.o[f"sb_{n}_sample"][0].rearrange("b q h d -> (b q) (h d)"),
                                  g.kvt[0:TS, NT, c:c + 256]).then_inc(s["st"], 16)
                eng.wait_ge(s["st"], 64)

            @block.tensor
            def _(eng):
                for j in range(NT + 1):
                    n = P if j < NT else TS
                    if j >= 2:
                        eng.wait_ge(s["ka"] if j % 2 == 0 else s["kv"], j // 2)
                    for q in range(4):
                        mm = nc.tensor.transpose(g.ps[0:n, 6 + j % 2, q * P:(q + 1) * P],
                                                 g.qb[:, 2 + q, j * P:j * P + n], g.ident)
                    mm.then_inc(s["kt"], 1)
                eng.wait_ge(s["ka"], NT // 2 + 1)
                eng.wait_ge(s["kv"], NT // 2)

                def part(i):
                    p, j, b, e = units[i]
                    c0 = skip(j, b)
                    return p, j, b, e, c0, slice(HD * e, HD * e + HD)
                for i in range(NUN + 3):
                    if i < NUN:
                        p, j, b, e, c0, rows = part(i)
                        if i >= 2:
                            eng.wait_ge(s["x"], i - 1)
                        nc.tensor.matmul(g.ps[:, i % 2, c0:512], g.qb[rows, 2 + p, b * P:(b + 1) * P],
                                         g.qb[rows, p, 512 * j + c0:512 * (j + 1)], start=True, stop=True).then_inc(s["z"], 1)
                    if 2 <= i < NUN + 2:
                        p, j, b, e, c0, rows = part(i - 2)
                        eng.wait_ge(s["arg"], i - 1)
                        nc.tensor.matmul(g.ps[:, 2 + e, c0:512], g.cf[:, 4, :], sp[:, (i - 2) % 2, c0:512],
                                         start=False, stop=True, skip_group_check=True).then_inc(s["ch"], 1)
                    if 1 <= i < NUN + 1:
                        p, j, b, e, c0, rows = part(i - 1)
                        eng.wait_ge(s["sp"], i)
                        nc.tensor.matmul(g.ps[:, 2 + e, c0:512], g.tri, sp[:, (i - 1) % 2, c0:512],
                                         start=top(j, b), stop=True, skip_group_check=True).then_inc(s["tri"], 1)
                    if i >= 3:
                        p, j, b, e, c0, rows = part(i - 3)
                        eng.wait_ge(s["at"], i - 2)
                        eng.wait_ge(s["am"], masked(i - 3))
                        if top(j, b) and group(i - 3):
                            eng.wait_ge(s["ob"], 2 * (group(i - 3) - 1) + e + 1)
                        nc.tensor.matmul(g.ps[rows, 4 + e, c0:512], g.kvt[:, b, 256 + P * p + HD * e:256 + P * p + HD * e + HD],
                                         at[:, (i - 3) % 2, c0:512], start=top(j, b), stop=(b == 0),
                                         skip_group_check=True).then_inc(s["pv"], 1)

            @block.scalar
            def _(eng):
                nc.scalar.preload_act_table_set("natural_log_exp_and_others")
                for j in range(0, NT + 1, 2):
                    n = P if j < NT else TS
                    eng.wait_ge(s["kt"], j + 1)
                    nc.scalar.copy(g.kvt[0:n, j, :], g.ps[0:n, 6, :]).then_inc(s["ka"], 1)
                nl = 0
                for i in range(NUN + 2):
                    if i < NUN:
                        p, j, b, e = units[i]
                        c0, k = skip(j, b), i % 2
                        eng.wait_ge(s["x"], i + 1)
                        if i >= 2:
                            eng.wait_ge(s["sp"], i - 1)
                        for func, kw in ((ACT.Abs, {}), (ACT.Exp, {"scale": -1.0}), (ACT.Ln, {"bias": 1.0})):
                            src = x[:, i % 3, c0:512] if func == ACT.Abs else l[:, k, c0:512]
                            nl += 1
                            nc.scalar.activation(l[:, k, c0:512], src, func, **kw).then_inc(s["l"], 1)
                            eng.wait_ge(s["l"], nl)
                    if i >= 2:
                        p, j, b, e = units[i - 2]
                        c0, k = skip(j, b), i % 2
                        eng.wait_ge(s["arg"], i - 1)
                        if i >= 4:
                            eng.wait_ge(s["pv"], i - 3)
                        nc.scalar.activation(at[:, k, c0:512], at[:, k, c0:512], ACT.Exp).then_inc(s["at"], 1)

            @block.vector
            def _(eng):
                V_.memset(zero[:, :], 0.0).then_inc(s["c"], 1)
                for j in range(1, NT + 1, 2):
                    eng.wait_ge(s["kt"], j + 1)
                    V_.tensor_copy(g.kvt[:, j, :], g.ps[:, 7, :]).then_inc(s["kv"], 1)
                eng.wait_ge(s["c"], 17)
                for i in range(NUN + 3):
                    if i < NUN:
                        p, j, b, e = units[i]
                        c0 = skip(j, b)
                        eng.wait_ge(s["z"], i + 1)
                        if i >= 3:
                            eng.wait_ge(s["arg"], i - 2)
                        V_.tensor_scalar(x[:, i % 3, c0:512], g.ps[:, i % 2, c0:512], HD ** -0.5,
                                         g.sbb[:, 2 * p + e:2 * p + e + 1], ALU.mult, ALU.add).then_inc(s["x"], 1)
                    if 1 <= i < NUN + 1:
                        p, j, b, e = units[i - 1]
                        c0, k = skip(j, b), (i - 1) % 2
                        eng.wait_ge(s["l"], 3 * i)
                        eng.wait_ge(s["x"], i)
                        if i >= 3:
                            eng.wait_ge(s["ch"], i - 2)
                        ins = V_.scalar_tensor_tensor(out=sp[:, k, c0:512], in0=x[:, (i - 1) % 3, c0:512], scalar=0.0,
                                                      in1=l[:, k, c0:512], op0=ALU.max, op1=ALU.add)
                        if diag(j, b):
                            ins.then_inc(s["raw"], 1)
                            eng.wait_ge(s["raw"], masked(i - 1))
                            ins = V_.copy_predicated(sp[:, k, c0:c0 + P], later[:, :], zero[:, :])
                        ins.then_inc(s["sp"], 1)
                    if 2 <= i < NUN + 2:
                        p, j, b, e = units[i - 2]
                        c0, k = skip(j, b), (i - 2) % 2
                        eng.wait_ge(s["tri"], i - 1)
                        if i >= 4:
                            eng.wait_ge(s["pv"], i - 3)
                        V_.tensor_tensor(at[:, k, c0:512], x[:, (i - 2) % 3, c0:512], g.ps[:, 2 + e, c0:512],
                                         ALU.subtract).then_inc(s["arg"], 1)
                    if i >= 3:
                        p, j, b, e = units[i - 3]
                        c0, k = skip(j, b), (i - 3) % 2
                        eng.wait_ge(s["at"], i - 2)
                        if diag(j, b):
                            V_.copy_predicated(at[:, k, c0:c0 + P], later[:, :], zero[:, :]).then_inc(s["am"], 1)
                        if b == 0:
                            eng.wait_ge(s["pv"], i - 2)
                            rows = slice(HD * e, HD * e + HD)
                            V_.tensor_copy(g.ob[rows, p, 512 * j:512 * (j + 1)], g.ps[rows, 4 + e, :]).then_inc(s["ob"], 1)


def b_sample(g):
    nc, a, V_ = g.nc, g.a, g.nc.vector
    NS, HQ = NPAGE + 1, SBH * NQ
    PB = 11
    GP = 8
    with ExitStack() as ctx:
        sb = lambda name, shape, dt=F32: ctx.enter_context(nc.sbuf_tensor(name, shape, dt))
        kp, vp = sb("kp", [P, NPAGE, 256]), sb("vp", [P, NPAGE, 256])
        kT = sb("kT", [P, 2, NS, P])
        pt = sb("pt", [1, NB * NPAGE], I32)
        qs = sb("qs", [P, 2, 2, NQ])
        bias = sb("bs_bias", [P, NS, SBH, NQ])
        x, l, sp, at = (sb(f"bs_{n}", [P, NS * HQ]) for n in ("x", "l", "sp", "at"))
        tot, run, keep = (sb(f"bs_{n}", [P, HQ, NS]) for n in ("tot", "run", "keep"))
        hide_all = sb("bs_hide_all", [P, NB, NQ], I32)
        hide = sb("bs_hide", [P, SBH, NQ], I32)
        zero = sb("bs_zero", [P, HQ])
        s_k = [g.sem(f"bs_k{i}") for i in range(NPAGE // GP)]
        s_v = [g.sem(f"bs_v{i}") for i in range(NPAGE // GP)]
        names = ("c", "pt", "init", "init2", "tp", "ta", "tv", "q", "z", "x", "l", "sp0", "sp", "sum", "t1", "t2",
                 "t3", "arg", "at", "am", "pv", "ob", "dve", "pool", "qz", "sp_")
        s = {n: g.sem(f"bs_{n}") for n in names}
        banks = lambda b0: g.ps[:, b0:b0 + 3, 0:PB * HQ]
        flat = lambda t: t[:, :].rearrange("p (a n) -> p a n", a=3)
        by_slot = lambda t: t[:, :].rearrange("p (k h) -> p k h", h=HQ)
        O0 = 400

        def batches(eng, body):
            body(0, True)
            with eng.Fori(1, NB) as b:
                body(b, False)

        with nc.Block() as block:
            @block.sync
            def _(eng):
                eng.dma_start(hide_all[:, :, :], a["c_new"]).then_inc(s["c"], 16)
                eng.dma_start(pt[:, :], a["page_table"].rearrange("b n -> (b n)").rearrange("(a n) -> a n", a=1)).then_inc(s["pt"], 16)
                eng.wait_ge(s["pt"], 16)

                def body(b, peeled):
                    if not peeled:
                        wait_apart(eng, s["tp"], 16 * b, s["sp_"])
                    for dst, cache, sem, free in ((kp, "cache_sb_k", s_k, None), (vp, "cache_sb_v", s_v, "pv")):
                        if free and not peeled:
                            wait_apart(eng, s[free], b, s["sp_"])
                        for k in range(NPAGE):
                            page = eng.value_load(pt[0:1, bass.ds(b * NPAGE + (NPAGE - 1 - k), 1)], min_val=0,
                                                  max_val=a[cache].shape[1] - 1)
                            eng.dma_start(dst[:, k, :], a[cache][0, bass.ds(page, 1)].rearrange(
                                "a t h d -> (a t) (h d)")).then_inc(sem[k // GP], 16)
                batches(eng, body)

            @block.gpsimd
            def _(eng):
                eng.memset(kT[:, :, 0, TS:P], 0.0).then_inc(s["init"], 1)
                eng.memset(qs[:, :, :, :], 0.0).then_inc(s["init"], 1)
                eng.memset(tot[:, :, 0:1], 0.0).then_inc(s["init"], 1)
                eng.memset(keep[:, :, :], 1.0).then_inc(s["init"], 1)
                eng.memset(zero[:, :], 0.0).then_inc(s["init"], 1)
                eng.wait_ge(s["init"], 5)
                eng.memset(keep[:, :, 0:1], 0.0).then_inc(s["init"], 1)
                for p in range(2):
                    eng.tensor_copy(kT[:, p, 0, 0:TS], g.qb[:, 2 + p, SEQ:T]).then_inc(s["init"], 1)
                eng.wait_ge(s["c"], 16)

                def body(b, peeled):
                    if not peeled:
                        wait_apart(eng, s["am"], b, s["pool"])
                    eng.tensor_copy(hide[:, :, :], hide_all[:, bass.ds(b, 1), :].broadcast_to([P, SBH, NQ])).then_inc(s["q"], 1)
                batches(eng, body)

            @block.tensor
            def _(eng):
                eng.wait_ge(s["init"], 8)

                def body(b, peeled):
                    for f in range(NPAGE // 2):
                        if f % (GP // 2) == 0:
                            eng.wait_ge(s_k[f // (GP // 2)], 16 * GP * b + 16 * GP)
                        if f >= 2 or not peeled:
                            eng.wait_ge(s["ta" if f % 2 == 0 else "tv"], 8 * b + f // 2)
                        for p in range(2):
                            for k in range(2):
                                mm = nc.tensor.transpose(g.ps[:, 6 + f % 2, (2 * p + k) * P:(2 * p + k + 1) * P],
                                                         kp[:, 2 * f + k, p * P:(p + 1) * P], g.ident)
                        mm.then_inc(s["tp"], 1)
                    eng.wait_ge(s["ta"], 8 * b + 8)
                    eng.wait_ge(s["tv"], 8 * b + 8)
                    eng.wait_ge(s["qz"], 2 * b + 2)
                    if not peeled:
                        eng.wait_ge(s["t1"], b)
                    for k in range(NS):
                        for p in range(2):
                            c = k % PB * HQ + p * 16
                            mm = nc.tensor.matmul(g.ps[:, k // PB, c:c + 16], kT[:, p, k, :],
                                                  qs[:, p].rearrange("r e q -> r (e q)"), start=True, stop=True)
                    mm.then_inc(s["z"], 1)
                    eng.wait_ge(s["sp"], b + 1)
                    eng.wait_ge(s["x"], b + 1)
                    if not peeled:
                        eng.wait_ge(s["ob"], 4 * b)
                    for c in range(3):
                        nc.tensor.matmul(g.ps[:, c, 0:PB * HQ], g.ones, flat(sp)[:, c, :], start=True, stop=True)
                        mm = nc.tensor.matmul(g.ps[:, 3 + c, 0:PB * HQ], g.cf[:, 4, :], flat(sp)[:, c, :], start=True, stop=True)
                    mm.then_inc(s["sum"], 1)
                    eng.wait_ge(s["am"], b + 1)
                    for v in range(NPAGE // GP):
                        eng.wait_ge(s_v[v], 16 * GP * b + 16 * GP)
                    for p in range(2):
                        out = g.ps[:, 5, O0 + 16 * p:O0 + 16 * p + 16]
                        for k in range(NS):
                            rows = slice(0, P) if k else slice(0, TS)
                            lhs = vp[:, k - 1, p * P:(p + 1) * P] if k else g.kvt[0:TS, SEQ // P, 256 + p * P:256 + (p + 1) * P]
                            mm = nc.tensor.matmul(out, lhs, by_slot(at)[rows, k, 16 * p:16 * p + 16],
                                                  start=(k == 0), stop=(k == NS - 1))
                    mm.then_inc(s["pv"], 1)
                batches(eng, body)

            @block.scalar
            def _(eng):
                nc.scalar.preload_act_table_set("natural_log_exp_and_others")
                eng.wait_ge(s["init"], 8)

                def body(b, peeled):
                    if not peeled:
                        eng.wait_ge(s["z"], b)
                    for e in range(2):
                        rows = slice(HD * e, HD * e + HD)
                        nc.scalar.copy(qs[rows, :, e, :], g.qb[rows, 0:2, bass.ds(SEQ + b * NQ, NQ)]).then_inc(s["qz"], 1)
                    for f in range(0, NPAGE // 2, 2):
                        eng.wait_ge(s["tp"], 16 * b + f + 1)
                        nc.scalar.copy(kT[:, :, 1 + 2 * f:3 + 2 * f, :].rearrange("r p k n -> r p (k n)"),
                                       g.ps[:, 6, :].rearrange("r (p n) -> r p n", p=2)).then_inc(s["ta"], 1)
                    eng.wait_ge(s["x"], b + 1)
                    for i, (func, kw) in enumerate(((ACT.Abs, {}), (ACT.Exp, {"scale": -1.0}), (ACT.Ln, {"bias": 1.0}))):
                        nc.scalar.activation(l[:, :], (x if i == 0 else l)[:, :], func, **kw).then_inc(s["l"], 1)
                        eng.wait_ge(s["l"], 3 * b + i + 1)
                    eng.wait_ge(s["arg"], b + 1)
                    nc.scalar.activation(at[:, :], at[:, :], ACT.Exp).then_inc(s["at"], 1)
                batches(eng, body)

            @block.vector
            def _(eng):
                V_.tensor_copy(bias[:, 0], g.sbb[:, :].rearrange("p (h a) -> p h a", a=1).broadcast_to([P, SBH, NQ])).then_inc(s["init2"], 1)
                eng.wait_ge(s["init2"], 1)
                V_.tensor_copy(bias[:, 1:NS].rearrange("p k h q -> p k (h q)"),
                               bias[:, 0:1].rearrange("p k h q -> p k (h q)").broadcast_to([P, NS - 1, HQ])).then_inc(s["init2"], 1)
                eng.wait_ge(s["init2"], 2)
                eng.wait_ge(s["init"], 8)

                def body(b, peeled):
                    for f in range(1, NPAGE // 2, 2):
                        eng.wait_ge(s["tp"], 16 * b + f + 1)
                        V_.tensor_copy(kT[:, :, 1 + 2 * f:3 + 2 * f, :].rearrange("r p k n -> r p (k n)"),
                                       g.ps[:, 7, :].rearrange("r (p n) -> r p n", p=2)).then_inc(s["tv"], 1)
                    eng.wait_ge(s["z"], b + 1)
                    if not peeled:
                        eng.wait_ge(s["arg"], b)
                    V_.scalar_tensor_tensor(out=flat(x), in0=banks(0), scalar=HD ** -0.5,
                                            in1=bias[:, :, :, :].rearrange("p k h q -> p (k h q)").rearrange("p (a n) -> p a n", a=3),
                                            op0=ALU.mult, op1=ALU.add).then_inc(s["x"], 1)
                    eng.wait_ge(s["l"], 3 * b + 3)
                    V_.scalar_tensor_tensor(out=sp[:, :], in0=x[:, :], scalar=0.0, in1=l[:, :], op0=ALU.max,
                                            op1=ALU.add).then_inc(s["sp0"], 1)
                    eng.wait_ge(s["q"], b + 1)
                    wait_apart(eng, s["sp0"], b + 1, s["dve"])
                    hidden = hide[:, :, :].rearrange("p h q -> p (h q)")
                    V_.copy_predicated(by_slot(sp)[:, 0], hidden, zero[:, :]).then_inc(s["sp"], 1)
                    eng.wait_ge(s["sum"], b + 1)
                    if not peeled:
                        eng.wait_ge(s["t2"], b)
                    for c in range(3):
                        n = PB if c < 2 else PB - 1
                        ins = V_.tensor_copy(tot[:, :, 1 + PB * c:1 + PB * c + n],
                                             g.ps[:, c, 0:n * HQ].rearrange("p (k h) -> p h k", h=HQ))
                    ins.then_inc(s["t1"], 1)
                    eng.wait_ge(s["t1"], b + 1)
                    if not peeled:
                        eng.wait_ge(s["t3"], b)
                    V_.tensor_tensor_scan(run[:, :, :].rearrange("p h k -> p (h k)"), keep[:, :, :].rearrange("p h k -> p (h k)"),
                                          tot[:, :, :].rearrange("p h k -> p (h k)"), 0.0, ALU.mult, ALU.add).then_inc(s["t2"], 1)
                    eng.wait_ge(s["t2"], b + 1)
                    V_.tensor_tensor(by_slot(x), by_slot(x), run[:, :, :].rearrange("p h k -> p k h"), ALU.subtract).then_inc(s["t3"], 1)
                    eng.wait_ge(s["t3"], b + 1)
                    if not peeled:
                        eng.wait_ge(s["pv"], b)
                    V_.tensor_tensor(flat(at), flat(x), banks(3), ALU.add).then_inc(s["arg"], 1)
                    wait_apart(eng, s["at"], b + 1, s["dve"])
                    V_.copy_predicated(by_slot(at)[:, 0], hidden, zero[:, :]).then_inc(s["am"], 1)
                    eng.wait_ge(s["pv"], b + 1)
                    for p in range(2):
                        for e in range(2):
                            rows = slice(HD * e, HD * e + HD)
                            V_.tensor_copy(g.ob[rows, p, bass.ds(SEQ + b * NQ, NQ)],
                                           g.ps[rows, 5, O0 + 16 * p + NQ * e:O0 + 16 * p + NQ * e + NQ]).then_inc(s["ob"], 1)
                batches(eng, body)


def stage_branch_c(g):
    nc, a = g.nc, g.a
    w_in = a["w_in"][0].rearrange("(k p) f -> p k f", p=P)
    c0 = A_COLS + SB_COLS
    with ExitStack() as ctx:
        g.qc = ctx.enter_context(nc.sbuf_tensor("qc", [P, 9, T], F32))
        g.new = ctx.enter_context(nc.sbuf_tensor("new", [TS, 2, 3, P], F32))
        with ExitStack() as xctx:
            reload_xn(g, xctx, "cx")
            project(g, "cp", w_in[:, :, c0:c0 + DIL_COLS], 9, g.xn, g.qc)
        c_prompt(g)
        c_sample(g)


def c_tile(t, gi, m):
    if gi == 0:
        return t[:, m * P:(m + 1) * P]
    if gi == 1:
        return t[:, 512 * (m % 2) + m // 2:512 * (m % 2 + 1):4]
    return t[:, m:SEQ:8]


def c_prompt(g):
    nc, a, V_, qc = g.nc, g.a, g.nc.vector, g.qc
    with ExitStack() as ctx:
        sb = lambda name, shape, dt=F32: ctx.enter_context(nc.sbuf_tensor(name, shape, dt))
        vt = sb("cq_vt", [P, 3, 8, P])
        kt = sb("cq_kt", [P, 13, P])
        bias = sb("cq_bias", [P, 3, 2, 256])
        sc = sb("cq_sc", [P, 2, 2, 256])
        pT = sb("cq_pT", [P, 2, 512])
        dg = sb("cq_dg", [P, 2, 2, P])
        mx, nm = sb("cq_mx", [P, 2, 2]), sb("cq_nm", [P, 2, 2])
        res = sb("cq_res", [P, 3, 3, SEQ])
        kts = [(0, 7)] + [(1, m) for m in (1, 3, 5, 7)] + [(2, m) for m in range(8)]
        tr = [(6, gi, m, vt[:, gi, m, :]) for gi in range(3) for m in range(8)] + \
             [(3, gi, m, kt[:, i, :]) for i, (gi, m) in enumerate(kts)]
        names = ("c", "tr", "te", "nt", "ne", "s", "sc", "mx", "nm", "dg", "ex", "t", "pt", "o", "oe", "st", "mxb", "ch", "e2")
        s = {n: g.sem(f"cq_{n}") for n in names}
        units = [(gi, m) for gi in range(3) for m in range(8)]
        alone = lambda gi, m: gi == 2 or (gi == 0 and m == 0) or (gi == 1 and m % 2 == 0)
        NUN = len(units)
        NTR = (len(tr) + 3) // 4
        with nc.Block() as block:
            @block.sync
            def _(eng):
                eng.dma_start(bias[:, :, :, :], a["c_bias"]).then_inc(s["c"], 16)
                n = [0]

                def store(dst, src):
                    eng.dma_start(dst, src).then_inc(s["st"], 16)
                    n[0] += 1
                eng.wait_ge(s["te"], NTR)
                eng.wait_ge(s["ne"], 2)
                for kv in range(2):
                    src = lambda i, gi, m: (vt[:, gi, m, :] if kv else kt[:, i, :])
                    for i, (gi, m) in enumerate(kts):
                        w = g.o[f"win{gi}_prompt"][0, 0, :, kv].rearrange("t h d -> t (h d)")
                        if gi == 0:
                            store(w, src(i, gi, m))
                        elif gi == 1:
                            store(w.rearrange("(i s) n -> s i n", s=4)[m // 2], src(i, gi, m))
                        else:
                            store(w.rearrange("(i s) n -> s i n", s=8)[m], src(i, gi, m))
                    for gi in range(3):
                        W = 128 * DILS[gi]
                        for b in range(NB):
                            store(g.o[f"win{gi}_sample"][0, b, W - NQ:W, kv].rearrange("t h d -> t (h d)"),
                                  g.new[NQ * b:NQ * b + NQ, kv, gi, :])
                eng.wait_ge(s["st"], 16 * n[0])

            @block.tensor
            def _(eng):
                for kv in range(2):
                    for gi in range(3):
                        mm = nc.tensor.transpose(g.ps[0:TS, 6 + kv, gi * P:(gi + 1) * P],
                                                 qc[:, 3 + 3 * kv + gi, SEQ:T], g.ident)
                    mm.then_inc(s["nt"], 1)
                for f in range(NTR):
                    if f >= 2:
                        eng.wait_ge(s["te"], f - 1)
                    for q, (base, gi, m, _) in enumerate(tr[4 * f:4 * f + 4]):
                        mm = nc.tensor.transpose(g.ps[:, 4 + f % 2, q * P:(q + 1) * P], c_tile(qc[:, base + gi, :], gi, m), g.ident)
                    mm.then_inc(s["tr"], 1)
                eng.wait_ge(s["te"], NTR)
                eng.wait_ge(s["ne"], 2)
                for i in range(NUN + 2):
                    if i < NUN:
                        gi, m = units[i]
                        if i >= 2:
                            eng.wait_ge(s["sc"], i - 1)
                        for e in range(2):
                            rows = slice(HD * e, HD * e + HD)
                            for blk in ((1,) if alone(gi, m) else (0, 1)):
                                mm = nc.tensor.matmul(g.ps[:, 2 * (i % 2) + e, blk * P:(blk + 1) * P],
                                                      c_tile(qc[rows, gi, :], gi, m), c_tile(qc[rows, 3 + gi, :], gi, m + blk - 1),
                                                      start=True, stop=True)
                        mm.then_inc(s["s"], 1)
                    if 1 <= i < NUN + 1:
                        gi, m = units[i - 1]
                        eng.wait_ge(s["ex"], 2 * i)
                        if i >= 3:
                            eng.wait_ge(s["pt"], i - 2)
                        for e in range(2):
                            for blk in ((1,) if alone(gi, m) else (0, 1)):
                                mm = nc.tensor.transpose(g.ps[:, 4 + (i - 1) % 2, (2 * e + blk) * P:(2 * e + blk + 1) * P],
                                                         sc[:, (i - 1) % 2, e, blk * P:(blk + 1) * P], g.ident)
                        mm.then_inc(s["t"], 1)
                    if i >= 2:
                        gi, m = units[i - 2]
                        k = i % 2
                        eng.wait_ge(s["pt"], i - 1)
                        eng.wait_ge(s["dg"], 2 * (i - 1))
                        if i >= 4:
                            eng.wait_ge(s["oe"], 3 * (i - 3))
                        for e in range(2):
                            rows = slice(HD * e, HD * e + HD)
                            bl = (1,) if alone(gi, m) else (0, 1)
                            for what in range(2):
                                for blk in bl:
                                    lhs = g.ones[:, 0:HD] if what else vt[:, gi, m + blk - 1, HD * e:HD * e + HD]
                                    nc.tensor.matmul(g.ps[rows, 6 + k, what * P:(what + 1) * P], lhs,
                                                     pT[:, k, (2 * e + blk) * P:(2 * e + blk + 1) * P],
                                                     start=(blk == bl[0]), stop=(blk == 1))
                            mm = nc.tensor.matmul(g.ps[rows, 6 + k, 2 * P:3 * P], g.ones[:, 0:HD], dg[:, k, e, :],
                                                  start=True, stop=True)
                        mm.then_inc(s["o"], 1)

            @block.scalar
            def _(eng):
                for i in range(NUN + 2):
                    if i < NUN:
                        gi, m = units[i]
                        c0 = P if alone(gi, m) else 0
                        eng.wait_ge(s["nm"], i + 1)
                        for e in range(2):
                            nc.scalar.activation(sc[:, i % 2, e, c0:256], sc[:, i % 2, e, c0:256], ACT.Exp,
                                                 bias=nm[:, i % 2, e:e + 1]).then_inc(s["ex"], 1)
                    if 1 <= i < NUN + 1:
                        gi, m = units[i - 1]
                        eng.wait_ge(s["t"], i)
                        if i >= 3:
                            eng.wait_ge(s["o"], i - 2)
                        k = (i - 1) % 2
                        if alone(gi, m):
                            nc.scalar.copy(pT[:, k, :].rearrange("p (a b) -> p a b", a=2)[:, :, P:256],
                                           g.ps[:, 4 + k, :].rearrange("p (a b) -> p a b", a=2)[:, :, P:256]).then_inc(s["pt"], 1)
                        else:
                            nc.scalar.copy(pT[:, k, :], g.ps[:, 4 + k, :]).then_inc(s["pt"], 1)
                for gi in range(3):
                    eng.wait_ge(s["mxb"], gi + 1)
                    nc.scalar.activation(res[:, gi, 2, :], res[:, gi, 2, :], ACT.Exp).then_inc(s["e2"], 1)

            @block.vector
            def _(eng):
                for kv in range(2):
                    eng.wait_ge(s["nt"], kv + 1)
                    V_.tensor_copy(g.new[:, kv].rearrange("t g n -> t (g n)"), g.ps[0:TS, 6 + kv, 0:3 * P]).then_inc(s["ne"], 1)
                for f in range(NTR):
                    eng.wait_ge(s["tr"], f + 1)
                    q = len(tr[4 * f:4 * f + 4])
                    dst = vt[:, f // 2, 4 * (f % 2):4 * (f % 2) + 4, :] if f < 6 else kt[:, 4 * (f - 6):4 * (f - 6) + q, :]
                    V_.tensor_copy(dst.rearrange("p a b -> p (a b)"), g.ps[:, 4 + f % 2, 0:q * P]).then_inc(s["te"], 1)
                eng.wait_ge(s["c"], 16)
                for i in range(NUN + 2):
                    if i < NUN:
                        gi, m = units[i]
                        c0, k = (P if alone(gi, m) else 0), i % 2
                        eng.wait_ge(s["s"], i + 1)
                        if i >= 2:
                            eng.wait_ge(s["t"], i - 1)
                        V_.scalar_tensor_tensor(out=sc[:, k, :, c0:256], in0=g.ps[:, 2 * k:2 * k + 2, c0:256], scalar=HD ** -0.5,
                                                in1=bias[:, gi, :, c0:256], op0=ALU.mult, op1=ALU.add).then_inc(s["sc"], 1)
                        eng.wait_ge(s["sc"], i + 1)
                        if i >= 2:
                            eng.wait_ge(s["ex"], 2 * (i - 1))
                            eng.wait_ge(s["dg"], 2 * (i - 1))
                        V_.tensor_reduce(mx[:, k, :], sc[:, k, :, c0:256], AX.X, ALU.max).then_inc(s["mx"], 1)
                        eng.wait_ge(s["mx"], i + 1)
                        V_.tensor_scalar(nm[:, k, :], mx[:, k, :], -1.0, None, ALU.mult).then_inc(s["nm"], 1)
                    if i >= 2:
                        gi, m = units[i - 2]
                        k = i % 2
                        eng.wait_ge(s["o"], i - 1)
                        for w in range(3):
                            src = g.ps[:, 6 + k, w * P:(w + 1) * P]
                            V_.tensor_copy(c_tile(res[:, gi, w, :], gi, m), src).then_inc(s["oe"], 1)
                    if i < NUN:
                        for e in range(2):
                            V_.tensor_scalar(dg[:, i % 2, e, :], g.ident, mx[:, i % 2, e:e + 1], None,
                                             ALU.mult).then_inc(s["dg"], 1)
                eng.wait_ge(s["oe"], 3 * NUN)
                n_ch = [0]

                def link(ins):
                    n_ch[0] += 1
                    ins.then_inc(s["ch"], 1)
                    eng.wait_ge(s["ch"], n_ch[0])
                top = sc[:, :, :, :].rearrange("p a e n -> p (a e n)")
                link(V_.tensor_tensor(top, res[:, 0, 2, :], res[:, 1, 2, :], ALU.max))
                link(V_.tensor_tensor(top, top, res[:, 2, 2, :], ALU.max))
                for gi in range(3):
                    V_.tensor_tensor(res[:, gi, 2, :], res[:, gi, 2, :], top, ALU.subtract).then_inc(s["mxb"], 1)
                for gi in range(3):
                    eng.wait_ge(s["e2"], gi + 1)
                    V_.tensor_tensor(res[:, gi, 0, :], res[:, gi, 0, :], res[:, gi, 2, :], ALU.mult)
                    link(V_.tensor_tensor(res[:, gi, 1, :], res[:, gi, 1, :], res[:, gi, 2, :], ALU.mult))
                for w in range(2):
                    link(V_.tensor_tensor(res[:, 0, w, :], res[:, 0, w, :], res[:, 1, w, :], ALU.add))
                    link(V_.tensor_tensor(res[:, 0, w, :], res[:, 0, w, :], res[:, 2, w, :], ALU.add))
                link(V_.reciprocal(top, res[:, 0, 1, :]))
                V_.tensor_tensor(g.oc[:, 0:SEQ], res[:, 0, 0, :], top, ALU.mult).then_inc(s["ch"], 1)


def c_sample(g):
    nc, a, V_, qc = g.nc, g.a, g.nc.vector, g.qc
    CLS = [(gi, r) for gi in range(3) for r in range((1, 4, 8)[gi])]
    NC = len(CLS)
    S0 = 192
    with ExitStack() as ctx:
        sb = lambda name, shape, dt=F32: ctx.enter_context(nc.sbuf_tensor(name, shape, dt))
        win = sb("cs_win", [P, NB, NC, 2 * P])
        qm = sb("cs_qm", [P, NC, NB, 32])
        qf = sb("cs_qf", [P, 3, NB, 2, NQ])
        kT = sb("cs_kT", [P, NC, P])
        bias = sb("cs_bias", [P, 3, S0])
        sc = sb("cs_sc", [P, 3, S0])
        st = sb("cs_st", [P, 4])
        pT = sb("cs_pT", [P, 3, P])
        pn = sb("cs_pn", [TS, 3, P])
        names = ("c", "z", "q", "tp", "te", "s", "sn", "sc", "mx", "nm", "ex", "iv", "pr", "t", "pt", "o", "cp")
        s = {n: g.sem(f"cs_{n}") for n in names}
        s_w = [g.sem(f"cs_w{b}") for b in range(NB)]
        with nc.Block() as block:
            @block.sync
            def _(eng):
                for b in range(NB):
                    eng.dma_start(win[:, b, 0, :], a["cache_win0"][0, b].rearrange("t a h d -> t (a h d)")).then_inc(s_w[b], 16)
                    eng.dma_start(win[:, b, 1:5, :].rearrange("p r n -> p (r n)"),
                                  a["cache_win1"][0, b].rearrange("(i r) a h d -> i (r a h d)", r=4)).then_inc(s_w[b], 16)
                    eng.dma_start(win[:, b, 5:13, :].rearrange("p r n -> p (r n)"),
                                  a["cache_win2"][0, b].rearrange("(i r) a h d -> i (r a h d)", r=16)[:, 0:8 * 256]).then_inc(s_w[b], 16)
                eng.dma_start(bias[:, :, :], a["c_sbias"]).then_inc(s["c"], 16)
                for gi in range(3):
                    W = 128 * DILS[gi]
                    for b in range(NB):
                        eng.dma_start(g.o[f"win{gi}_sample"][0, b, 0:W - NQ].rearrange("t a h d -> t (a h d)"),
                                      a[f"cache_win{gi}"][0, b, NQ:W].rearrange("t a h d -> t (a h d)")).then_inc(s["cp"], 16)
                eng.wait_ge(s["cp"], 16 * 3 * NB)

            @block.gpsimd
            def _(eng):
                eng.memset(qm[:, :, :, :], 0.0).then_inc(s["z"], 1)
                eng.memset(qf[:, :, :, :, :], 0.0).then_inc(s["z"], 1)

            @block.tensor
            def _(eng):
                eng.wait_ge(s["q"], 2)
                for b in range(NB):
                    eng.wait_ge(s_w[b], 48)
                    for f in range(4):
                        if b:
                            eng.wait_ge(s["te"], 4 * (b - 1) + f + 1)
                        for i in range(4 * f, min(4 * f + 4, NC)):
                            mm = nc.tensor.transpose(g.ps[:, 3 + f, (i - 4 * f) * P:(i - 4 * f + 1) * P],
                                                     win[:, b, i, 0:P], g.ident)
                        mm.then_inc(s["tp"], 1)
                    rows = slice(32 * (b // 2), 32 * (b // 2) + 32)
                    for i, (gi, r) in enumerate(CLS):
                        if i % 4 == 0:
                            eng.wait_ge(s["te"], 4 * b + i // 4 + 1)
                        mm = nc.tensor.matmul(g.ps[rows, gi, 0:P], qm[:, i, b, :], kT[:, i, :],
                                              start=(r == 0 and b % 2 == 0), stop=(b % 2 == 1 and (i == NC - 1 or CLS[i + 1][0] != gi)),
                                              skip_group_check=True)
                    mm.then_inc(s["s"], 1)
                for gi in range(3):
                    mm = nc.tensor.matmul(g.ps[:, gi, P:S0], qf[:, gi].rearrange("p b e q -> p (b e q)"), qc[:, 3 + gi, SEQ:T],
                                          start=True, stop=True, skip_group_check=True)
                mm.then_inc(s["sn"], 1)
                eng.wait_ge(s["pr"], 1)
                for gi in range(3):
                    nc.tensor.transpose(g.ps[:, 3, gi * P:(gi + 1) * P], sc[:, gi, 0:P], g.ident)
                    mm = nc.tensor.transpose(g.ps[0:TS, 4, gi * P:(gi + 1) * P], sc[:, gi, P:S0], g.ident)
                mm.then_inc(s["t"], 1)
                eng.wait_ge(s["pt"], 2)
                out = g.ps[:, 5, 0:P]
                for gi in range(3):
                    nc.tensor.matmul(out, g.new[:, 1, gi, :], pn[:, gi, :], start=(gi == 0), stop=False, skip_group_check=True)
                for b in range(NB):
                    for i, (gi, r) in enumerate(CLS):
                        step = (1, 4, 8)[gi]
                        cols = lambda t: t.rearrange("p (x q) -> p x q", q=NQ)[:, 2 * b:2 * b + 2, r:NQ:step]
                        mm = nc.tensor.matmul(cols(out), win[:, b, i, P:2 * P], cols(pT[:, gi, :]), start=False,
                                              stop=(b == NB - 1 and i == NC - 1), skip_group_check=True)
                mm.then_inc(s["o"], 1)

            @block.scalar
            def _(eng):
                for b in range(NB):
                    for f in range(4):
                        n = min(4 * f + 4, NC) - 4 * f
                        eng.wait_ge(s["tp"], 4 * b + f + 1)
                        if b:
                            eng.wait_ge(s["s"], b)
                        nc.scalar.copy(kT[:, 4 * f:4 * f + n, :].rearrange("p a n -> p (a n)"),
                                       g.ps[:, 3 + f, 0:n * P]).then_inc(s["te"], 1)
                eng.wait_ge(s["nm"], 1)
                nc.scalar.activation(sc[:, :, :], sc[:, :, :], ACT.Exp, bias=st[:, 1:2]).then_inc(s["ex"], 1)

            @block.vector
            def _(eng):
                eng.wait_ge(s["z"], 2)
                for e in range(2):
                    rows = slice(HD * e, HD * e + HD)
                    for gi in range(3):
                        qv = qc[rows, gi, SEQ:T].rearrange("p (b q) -> p b q", q=NQ)
                        ins = V_.tensor_copy(qf[rows, gi, :, e, :], qv)
                    for i, (gi, r) in enumerate(CLS):
                        step = (1, 4, 8)[gi]
                        for par in range(2):
                            qv = qc[rows, gi, SEQ:T].rearrange("p (b q) -> p b q", q=NQ)[:, par:NB:2, r:NQ:step]
                            ins = V_.tensor_copy(qm[rows, i, par:NB:2, 16 * par + 8 * e + r:16 * par + 8 * e + NQ:step], qv)
                    ins.then_inc(s["q"], 1)
                eng.wait_ge(s["c"], 16)
                eng.wait_ge(s["sn"], 1)
                V_.scalar_tensor_tensor(out=sc[:, :, :], in0=g.ps[:, 0:3, 0:S0], scalar=HD ** -0.5, in1=bias[:, :, :],
                                        op0=ALU.mult, op1=ALU.add).then_inc(s["sc"], 1)
                eng.wait_ge(s["sc"], 1)
                V_.tensor_reduce(st[:, 0:1], sc[:, :, :], AX.XY, ALU.max).then_inc(s["mx"], 1)
                eng.wait_ge(s["mx"], 1)
                V_.tensor_scalar(st[:, 1:2], st[:, 0:1], -1.0, None, ALU.mult).then_inc(s["nm"], 1)
                eng.wait_ge(s["ex"], 1)
                V_.tensor_reduce(st[:, 2:3], sc[:, :, :], AX.XY, ALU.add).then_inc(s["iv"], 1)
                eng.wait_ge(s["iv"], 1)
                V_.reciprocal(st[:, 3:4], st[:, 2:3]).then_inc(s["iv"], 1)
                eng.wait_ge(s["iv"], 2)
                V_.tensor_scalar(sc[:, :, :], sc[:, :, :], st[:, 3:4], None, ALU.mult).then_inc(s["pr"], 1)
                eng.wait_ge(s["t"], 1)
                V_.tensor_copy(pT[:, :, :].rearrange("p g n -> p (g n)"), g.ps[:, 3, 0:3 * P]).then_inc(s["pt"], 1)
                V_.tensor_copy(pn[:, :, :].rearrange("p g n -> p (g n)"), g.ps[0:TS, 4, 0:3 * P]).then_inc(s["pt"], 1)
                eng.wait_ge(s["o"], 1)
                for e in range(2):
                    rows = slice(HD * e, HD * e + HD)
                    V_.tensor_copy(g.oc[rows, SEQ:T].rearrange("p (b q) -> p b q", q=NQ),
                                   g.ps[rows, 5, 0:P].rearrange("p (b e q) -> p b e q", e=2, q=NQ)[:, :, e, :])


GATE0 = A_COLS + SB_COLS + DIL_COLS
EXT = 2 + SEQ + NB * (NQ + 2)


def stage_merge(g):
    nc, a, V_ = g.nc, g.a, g.nc.vector
    w_in = a["w_in"][0].rearrange("(k p) f -> p k f", p=P)
    src = [(g.oa[:, k, :] for k in range(3)), (g.ob[:, k, :] for k in range(2)), (g.oc[:, :] for _ in range(1))]
    src = [list(x) for x in src]
    wbr = [a[f"w_branch_{x}"][0].rearrange("(k p) f -> p k f", p=P) for x in "abc"]
    with ExitStack() as ctx:
        sb = lambda name, shape, dt=F32: ctx.enter_context(nc.sbuf_tensor(name, shape, dt))
        reload_xn(g, ctx, "mx")
        wg = sb("wg", [P, 3, KT, P])
        wb = sb("wb", [P, 3, 3, P])
        sg = sb("sg", [P, 3, T])
        tmp = sb("mg_tmp", [P, T])
        s = {n: g.sem(f"mg_{n}") for n in ("g", "b", "sg", "m", "add")}
        s_w = [g.sem(f"mg_w{i}") for i in range(3)]

        def tiles(eng, body):
            body(0, True)
            with eng.Fori(1, KT) as f:
                body(f, False)
        with nc.Block() as block:
            @block.sync
            def _(eng):
                def body(f, peeled):
                    for i in range(3):
                        if not peeled:
                            eng.wait_ge(s["b"], 3 * f + i - 2)
                        eng.dma_start(wg[:, i], w_in[:, :, bass.ds(GATE0 + i * D + f * P, P)]).then_inc(s_w[i], 16)
                        eng.dma_start(wb[:, i, 0:3 - i], wbr[i][:, :, bass.ds(f * P, P)]).then_inc(s_w[i], 16)
                tiles(eng, body)

            @block.tensor
            def _(eng):
                def body(f, peeled):
                    for i in range(3):
                        eng.wait_ge(s_w[i], 32 * f + 32)
                        if not peeled or i:
                            eng.wait_ge(s["sg"], 3 * f + i)
                        for c, (c0, n) in enumerate(CH):
                            for k in range(KT):
                                mm = nc.tensor.matmul(g.ps[:, c, 0:n], wg[:, i, k, :], g.xn[:, k, c0:c0 + n],
                                                      start=(k == 0), stop=(k == KT - 1))
                        mm.then_inc(s["g"], 1)
                        if not peeled or i:
                            eng.wait_ge(s["m"], 3 * f + i)
                        for c, (c0, n) in enumerate(CH):
                            for k in range(3 - i):
                                mm = nc.tensor.matmul(g.ps[:, 3 + c, 0:n], wb[:, i, k, :], src[i][k][:, c0:c0 + n],
                                                      start=(k == 0), stop=(k == 2 - i))
                        mm.then_inc(s["b"], 1)
                tiles(eng, body)

            @block.scalar
            def _(eng):
                def body(f, peeled):
                    for i in range(3):
                        eng.wait_ge(s["g"], 3 * f + i + 1)
                        if not peeled:
                            eng.wait_ge(s["m"], 3 * f + i - 2)
                        for c, (c0, n) in enumerate(CH):
                            ins = nc.scalar.activation(sg[:, i, c0:c0 + n], g.ps[:, c, 0:n], ACT.Sigmoid)
                        ins.then_inc(s["sg"], 1)
                tiles(eng, body)

            @block.vector
            def _(eng):
                def body(f, peeled):
                    out = g.mg[:, bass.ds(f, 1), :].rearrange("p a t -> p (a t)")
                    for i in range(3):
                        eng.wait_ge(s["sg"], 3 * f + i + 1)
                        eng.wait_ge(s["b"], 3 * f + i + 1)
                        if i == 2:
                            eng.wait_ge(s["add"], 2 * f + 1)
                        elif i == 1 and not peeled:
                            eng.wait_ge(s["add"], 2 * f)
                        for c, (c0, n) in enumerate(CH):
                            dst = g.mg[:, bass.ds(f, 1), c0:c0 + n].rearrange("p a t -> p (a t)") if i == 0 else tmp[:, c0:c0 + n]
                            ins = V_.tensor_tensor(dst, sg[:, i, c0:c0 + n], g.ps[:, 3 + c, 0:n], ALU.mult)
                        ins.then_inc(s["m"], 1)
                        if i:
                            eng.wait_ge(s["m"], 3 * f + i + 1)
                            V_.tensor_tensor(out, out, tmp[:, :], ALU.add).then_inc(s["add"], 1)
                tiles(eng, body)


def project_add(g, pre, w, kt, src, dst):
    nc = g.nc
    with ExitStack() as ctx:
        wt = ctx.enter_context(nc.sbuf_tensor(f"{pre}_w", [P, 2, kt, P], F32))
        s_w = [g.sem(f"{pre}_w{i}") for i in range(2)]
        s_mm, s_v = (g.sem(f"{pre}_{n}") for n in ("mm", "v"))
        with nc.Block() as block:
            @block.sync
            def _(eng):
                def body(t, b):
                    if not first(t):
                        eng.wait_ge(s_mm, t - 1)
                    eng.dma_start(wt[:, b, :, :], w[:, :, bass.ds(t * P, P)]).then_inc(s_w[b], 16)
                in_pairs(eng, KT, body)

            @block.tensor
            def _(eng):
                def body(t, b):
                    eng.wait_ge(s_w[b], 16 * ((t - b) // 2 + 1) if isinstance(t, int) else 8 * (t - b) + 16)
                    if not first(t):
                        eng.wait_ge(s_v, t - 1)
                    for c, (c0, n) in enumerate(CH):
                        for k in range(kt):
                            mm = nc.tensor.matmul(g.ps[:, 3 * b + c, 0:n], wt[:, b, k, :], src[:, k, c0:c0 + n],
                                                  start=(k == 0), stop=(k == kt - 1))
                    mm.then_inc(s_mm, 1)
                in_pairs(eng, KT, body)

            @block.vector
            def _(eng):
                def body(t, b):
                    eng.wait_ge(s_mm, t + 1)
                    for c, (c0, n) in enumerate(CH):
                        d = dst[:, bass.ds(t, 1), c0:c0 + n].rearrange("p a t -> p (a t)")
                        ins = nc.vector.tensor_tensor(d, d, g.ps[:, 3 * b + c, 0:n], ALU.add)
                    ins.then_inc(s_v, 1)
                in_pairs(eng, KT, body)


def copy_dram(g, pre, dst, src):
    s_c = g.sem(f"{pre}_copy")
    with g.nc.Block() as block:
        @block.sync
        def _(eng):
            eng.dma_start(dst, src).then_inc(s_c, 16)
            eng.wait_ge(s_c, 16)


def norm(g, pre, src, gain, dst):
    nc = g.nc
    with ExitStack() as ctx:
        sq = ctx.enter_context(nc.sbuf_tensor(f"{pre}_sqb", [P, 2, T], F32))
        inv = ctx.enter_context(nc.sbuf_tensor(f"{pre}_invb", [P, T], F32))
        n_act, n_pe, n_dve, _ = norm_program(g, pre, src, sq, inv, gain, dst, T, CH)
        with nc.Block() as block:
            block.scalar(n_act)
            block.tensor(n_pe)
            block.vector(n_dve)


def stage_up(g, xf, act):
    with g.nc.sbuf_tensor("co", [P, UT, 2 + 2 * NB], F32) as co:
        ffn_up(g, xf, act, co)
        conv_state(g, co)


def ffn_up(g, xf, act, co):
    nc, a, V_ = g.nc, g.a, g.nc.vector
    w = a["w_up"][0].rearrange("(k p) f -> p k f", p=P)
    S0 = 2 + SEQ
    with ExitStack() as ctx:
        sb = lambda name, shape, dt=F32: ctx.enter_context(nc.sbuf_tensor(name, shape, dt))
        wt = sb("fu_w", [P, 2, KT, P])
        u = sb("fu_u", [P, 2, EXT])
        cv = sb("fu_cv", [P, 2, EXT])
        sg = sb("fu_sg", [P, EXT])
        s = {n: g.sem(f"fu_{n}") for n in ("z", "mm", "ev", "st", "t0", "t1", "cv", "sg", "m", "act", "co")}
        s_w = [g.sem(f"fu_w{i}") for i in range(2)]
        E = EXT - 2
        samp = lambda t, o: t[:, S0:EXT].rearrange("p (b q) -> p b q", q=NQ + 2)[:, :, o:o + NQ]
        col = lambda t, half, j: t[:, bass.ds(half * FT + j, 1)]

        def tiles(eng, body):
            body(0, True)
            with eng.Fori(1, FT) as j:
                body(j, False)
        with nc.Block() as block:
            @block.sync
            def _(eng):
                def body(j, peeled):
                    for h in range(2):
                        if not peeled:
                            eng.wait_ge(s["mm"], 2 * j + h - 1)
                        eng.dma_start(wt[:, h], w[:, :, bass.ds(h * FF + j * P, P)]).then_inc(s_w[h], 16)
                tiles(eng, body)

            @block.tensor
            def _(eng):
                def body(j, peeled):
                    for h in range(2):
                        eng.wait_ge(s_w[h], 16 * j + 16)
                        if not peeled:
                            eng.wait_ge(s["ev"], 2 * j + h - 1)
                        for c, (c0, n) in enumerate(CH):
                            for k in range(KT):
                                mm = nc.tensor.matmul(g.ps[:, 3 * h + c, 0:n], wt[:, h, k, :], xf[:, k, c0:c0 + n],
                                                      start=(k == 0), stop=(k == KT - 1))
                        mm.then_inc(s["mm"], 1)
                tiles(eng, body)

            @block.gpsimd
            def _(eng):
                eng.memset(u[:, :, 0:2], 0.0).then_inc(s["z"], 1)

                def body(j, peeled):
                    for h in range(2):
                        if not peeled:
                            wait_apart(eng, s["cv"], 2 * j + h - 1, s["z"])
                        t = h * FT + j
                        eng.tensor_copy(u[:, h, S0:EXT].rearrange("p (b q) -> p b q", q=NQ + 2)[:, :, 0:2],
                                        g.cst[:, bass.ds(t, 1), :].rearrange("p a (b r) -> p (a b) r", r=2)).then_inc(s["st"], 1)
                        wait_apart(eng, s["ev"], 2 * j + h + 1, s["z"])
                        eng.tensor_copy(co[:, bass.ds(t, 1), 0:2].rearrange("p a r -> p (a r)"), u[:, h, SEQ:SEQ + 2])
                        eng.tensor_copy(co[:, bass.ds(t, 1), 2:2 + 2 * NB].rearrange("p a (b r) -> p (a b) r", r=2),
                                        u[:, h, S0:EXT].rearrange("p (b q) -> p b q", q=NQ + 2)[:, :, NQ:NQ + 2]).then_inc(s["co"], 1)
                tiles(eng, body)

            @block.scalar
            def _(eng):
                def body(j, peeled):
                    for h in range(2):
                        eng.wait_ge(s["mm"], 2 * j + h + 1)
                        if not peeled:
                            eng.wait_ge(s["cv"], 2 * j + h - 1)
                            eng.wait_ge(s["co"], 2 * j + h - 1)
                        b0 = 3 * h
                        nc.scalar.copy(u[:, h, 2:2 + CH[0][1]], g.ps[:, b0, 0:CH[0][1]])
                        nc.scalar.copy(u[:, h, 2 + CH[1][0]:2 + CH[2][0]], g.ps[:, b0 + 1, 0:CH[1][1]])
                        n = SEQ - CH[2][0]
                        nc.scalar.copy(u[:, h, 2 + CH[2][0]:2 + SEQ], g.ps[:, b0 + 2, 0:n])
                        nc.scalar.copy(samp(u[:, h], 2), g.ps[:, b0 + 2, n:n + TS].rearrange("p (b q) -> p b q", q=NQ)).then_inc(s["ev"], 1)
                    eng.wait_ge(s["cv"], 2 * j + 1)
                    if not peeled:
                        eng.wait_ge(s["m"], j)
                    nc.scalar.activation(sg[:, 0:E], cv[:, 0, 0:E], ACT.Sigmoid).then_inc(s["sg"], 1)
                tiles(eng, body)

            @block.vector
            def _(eng):
                eng.wait_ge(s["z"], 1)

                def body(j, peeled):
                    for h in range(2):
                        eng.wait_ge(s["ev"], 2 * j + h + 1)
                        eng.wait_ge(s["st"], 2 * j + h + 1)
                        if not peeled:
                            eng.wait_ge(s["act"], 2 * j)
                        V_.tensor_scalar(cv[:, h, 0:E], u[:, h, 0:E], col(g.cw[:, 0], h, j), col(g.cb, h, j),
                                         ALU.mult, ALU.add).then_inc(s["t0"], 1)
                        eng.wait_ge(s["t0"], 2 * j + h + 1)
                        V_.scalar_tensor_tensor(out=cv[:, h, 0:E], in0=u[:, h, 1:1 + E], scalar=col(g.cw[:, 1], h, j),
                                                in1=cv[:, h, 0:E], op0=ALU.mult, op1=ALU.add).then_inc(s["t1"], 1)
                        eng.wait_ge(s["t1"], 2 * j + h + 1)
                        V_.scalar_tensor_tensor(out=cv[:, h, 0:E], in0=u[:, h, 2:2 + E], scalar=col(g.cw[:, 2], h, j),
                                                in1=cv[:, h, 0:E], op0=ALU.mult, op1=ALU.add).then_inc(s["cv"], 1)
                    eng.wait_ge(s["sg"], j + 1)
                    V_.tensor_tensor(sg[:, 0:E], sg[:, 0:E], cv[:, 0, 0:E], ALU.mult).then_inc(s["m"], 1)
                    eng.wait_ge(s["m"], j + 1)
                    eng.wait_ge(s["cv"], 2 * j + 2)
                    out = lambda c0, n: act[:, bass.ds(j, 1), c0:c0 + n].rearrange("p a t -> p (a t)")
                    V_.tensor_tensor(out(0, SEQ), sg[:, 0:SEQ], cv[:, 1, 0:SEQ], ALU.mult).then_inc(s["act"], 1)
                    V_.tensor_tensor(out(SEQ, TS).rearrange("p (b q) -> p b q", q=NQ), samp(sg, 0), samp(cv[:, 1], 0),
                                     ALU.mult).then_inc(s["act"], 1)
                tiles(eng, body)


def conv_state(g, co):
    nc = g.nc
    R = 2 + 2 * NB
    with ExitStack() as ctx:
        rows = ctx.enter_context(nc.sbuf_tensor("cs_rows", [R, UT, P], F32))
        s_t, s_a, s_v, s_o = (g.sem(f"co_{n}") for n in "tavo")
        NF = UT // 4
        with nc.Block() as block:
            @block.tensor
            def _(eng):
                for f in range(NF):
                    if f >= 2:
                        eng.wait_ge(s_a if f % 2 == 0 else s_v, f // 2)
                    for q in range(4):
                        mm = nc.tensor.transpose(g.ps[0:R, f % 2, q * P:(q + 1) * P], co[:, 4 * f + q, :], g.ident)
                    mm.then_inc(s_t, 1)

            @block.scalar
            def _(eng):
                for f in range(0, NF, 2):
                    eng.wait_ge(s_t, f + 1)
                    nc.scalar.copy(rows[:, 4 * f:4 * f + 4, :].rearrange("r a n -> r (a n)"), g.ps[0:R, 0, :]).then_inc(s_a, 1)

            @block.vector
            def _(eng):
                for f in range(1, NF, 2):
                    eng.wait_ge(s_t, f + 1)
                    nc.vector.tensor_copy(rows[:, 4 * f:4 * f + 4, :].rearrange("r a n -> r (a n)"), g.ps[0:R, 1, :]).then_inc(s_v, 1)

            @block.sync
            def _(eng):
                eng.wait_ge(s_a, (NF + 1) // 2)
                eng.wait_ge(s_v, NF // 2)
                eng.dma_start(g.o["conv_prompt"][0, 0], rows[0:2].rearrange("r a n -> r (a n)")).then_inc(s_o, 16)
                eng.dma_start(g.o["conv_sample"][0].rearrange("b r f -> (b r) f"), rows[2:R].rearrange("r a n -> r (a n)")).then_inc(s_o, 16)
                eng.wait_ge(s_o, 32)


def store_rows(g, y):
    nc = g.nc
    NT = SEQ // P
    with ExitStack() as ctx:
        rows = ctx.enter_context(nc.sbuf_tensor("y_rows", [P, 3, D], F32))
        s_t, s_a, s_v = (g.sem(f"yr_{n}") for n in "tav")
        s_o = [g.sem(f"yr_o{i}") for i in range(3)]
        with nc.Block() as block:
            @block.tensor
            def _(eng):
                for j in range(NT + 1):
                    n = P if j < NT else TS
                    for h in range(2):
                        if j >= 2:
                            eng.wait_ge((s_a, s_v)[h], j - 1)
                        for q in range(4):
                            mm = nc.tensor.transpose(g.ps[0:n, 2 * (j % 2) + h, q * P:(q + 1) * P],
                                                     y[:, 4 * h + q, j * P:j * P + n], g.ident)
                        mm.then_inc(s_t, 1)

            def copies(eng, h, copy, sem):
                for j in range(NT + 1):
                    n = P if j < NT else TS
                    eng.wait_ge(s_t, 2 * j + h + 1)
                    if j >= 3:
                        eng.wait_ge(s_o[j % 3], 16 * (j // 3))
                    copy(rows[0:n, j % 3, 512 * h:512 * h + 512], g.ps[0:n, 2 * (j % 2) + h, :]).then_inc(sem, 1)

            @block.scalar
            def _(eng):
                copies(eng, 0, nc.scalar.copy, s_a)

            @block.vector
            def _(eng):
                copies(eng, 1, nc.vector.tensor_copy, s_v)

            @block.sync
            def _(eng):
                for j in range(NT + 1):
                    n = P if j < NT else TS
                    eng.wait_ge(s_a, j + 1)
                    eng.wait_ge(s_v, j + 1)
                    dst = g.o["y_prompt"][0, j * P:(j + 1) * P, :] if j < NT else g.o["y_sample"].rearrange("b q d -> (b q) d")
                    eng.dma_start(dst, rows[0:n, j % 3, :]).then_inc(s_o[j % 3], 16)
                for i in range(3):
                    eng.wait_ge(s_o[i], 48)


_INS = ['x_prompt', 'x_sample', 'cache_sb_k', 'cache_sb_v', 'page_table', 'cache_win0', 'cache_win1', 'cache_win2',
        'state_wkv', 'state_shift', 'state_conv', 'norm_mix', 'w_in', 'rwkv_mu', 'rwkv_w0', 'rwkv_w2', 'rwkv_a0',
        'rwkv_a2', 'rwkv_g2', 'rwkv_k_k', 'rwkv_k_a', 'rwkv_r_k', 'rwkv_ln_w', 'rwkv_ln_b', 'sb_bias', 'w_branch_a',
        'w_branch_b', 'w_branch_c', 'w_out', 'norm_ffn', 'w_up', 'conv_w', 'conv_b', 'w_down', 'norm_final']
_OUTS = [("y_prompt", (1, SEQ, D)), ("y_sample", (NB, NQ, D)),
         ("sb_k_prompt", (1, 1, SEQ, SBH, HD)), ("sb_k_sample", (1, NB, NQ, SBH, HD)),
         ("sb_v_prompt", (1, 1, SEQ, SBH, HD)), ("sb_v_sample", (1, NB, NQ, SBH, HD)),
         ("win0_prompt", (1, 1, 128, 2, 2, HD)), ("win0_sample", (1, NB, 128, 2, 2, HD)),
         ("win1_prompt", (1, 1, 512, 2, 2, HD)), ("win1_sample", (1, NB, 512, 2, 2, HD)),
         ("win2_prompt", (1, 1, SEQ, 2, 2, HD)), ("win2_sample", (1, NB, 2048, 2, 2, HD)),
         ("wkv_prompt", (1, 1, AH, HD, HD)), ("wkv_sample", (1, NB, AH, HD, HD)),
         ("shift_prompt", (1, 1, D)), ("shift_sample", (1, NB, D)),
         ("conv_prompt", (1, 1, 2, 2 * FF)), ("conv_sample", (1, NB, 2, 2 * FF))]


def declare(nc, inputs):
    arrays, a = {}, {}
    for name in _INS:
        x = np.ascontiguousarray(inputs[name])
        arrays[f"in_{name}"] = x
        a[name] = nc.dram_tensor(f"in_{name}", x.shape, mybir.dt.from_np(x.dtype), kind="ExternalInput").ap()
    for name, x in constants().items():
        arrays[name] = x
        a[name] = nc.dram_tensor(name, x.shape, mybir.dt.from_np(x.dtype), kind="ExternalInput").ap()
    o = {n: nc.dram_tensor(f"out_{n}", s, F32, kind="ExternalOutput").ap() for n, s in _OUTS}
    scratch = {"xt": nc.dram_tensor("scr_xt", (P, KT, T), F32, kind="Internal").ap(),
               "xn": nc.dram_tensor("scr_xn", (P, KT, T), F32, kind="Internal").ap()}
    return arrays, (a, o, scratch)


def kernel(**inputs):
    import concourse.bacc as _bacc
    from concourse.bass_utils import run_bass_kernel_spmd as _run

    nc = _bacc.Bacc("TRN2", target_bir_lowering=False, num_devices=1)
    arrays, tensors = declare(nc, inputs)
    build(nc, *tensors)
    r = _run(nc, [arrays], core_ids=[0])
    return tuple(r.results[0][f"out_{n}"] for n, _ in _OUTS)
```

```python
from contextlib import ExitStack, contextmanager

import numpy as np

import concourse.bass as bass
from concourse import mybir

ALU = mybir.AluOpType
ACT = mybir.ActivationFunctionType
AX = mybir.AxisListType
F32, F32R, I32 = mybir.dt.float32, mybir.dt.float32r, mybir.dt.int32

P = 128
D = 1024
KT = D // P
SEQ, NB, NQ = 1024, 8, 8
TS = NB * NQ
T = SEQ + TS
TP = T + NB
HD = 64
AH, AW = 6, 384
AT = 11
PAIRS = 3
SBH = 4
DILS = (1, 4, 16)
FF = 2816
FT = FF // P
UT = 2 * FT
EPS = 1e-6
GN_EPS = 64e-5
NPAGE = 32
PAST = 4096
CHUNK = P
NU = SEQ // CHUNK + 1
LEVELS = 7
CH = ((0, 384), (384, 352), (736, 352))
CHP = ((0, 384), (384, 352), (736, 360))
NEG = -1e30


PROWS, _at = {}, 0
for _n, _c in (("norm_mix", 8), ("rwkv_mu", 11), ("rwkv_w0", 3), ("rwkv_a0", 3), ("rwkv_k_k", 3),
               ("rwkv_k_a", 3), ("rwkv_r_k", 3), ("rwkv_ln_w", 3), ("rwkv_ln_b", 3), ("norm_ffn", 8),
               ("norm_final", 8), ("conv_b", 44)):
    PROWS[_n] = (_at, _c)
    _at += _c
NPROW = _at


def constants():
    r, c = np.arange(P)[:, None], np.arange(P)[None, :]
    same = lambda n: (r // n) == (c // n)
    f = np.zeros((P, 5, P), np.float32)
    f[:, 0] = r == c
    f[:, 1] = 1.0
    f[:, 2] = same(HD)
    f[:, 3] = r >= c
    f[:, 4] = r < c
    u = np.zeros((P, 2 * LEVELS + 6, P), np.int32)
    for l in range(1, LEVELS + 1):
        low = same(2 ** l) & (r % 2 ** l >= 2 ** (l - 1)) & (c % 2 ** l < 2 ** (l - 1))
        u[:, l - 1] = low
        u[:, LEVELS + l - 1] = low.T
    for n, s in enumerate((np.ones((P, P), bool), same(NQ))):
        u[:, 2 * LEVELS + 3 * n] = (c < r) & s
        u[:, 2 * LEVELS + 3 * n + 1] = (r < c) & s
        u[:, 2 * LEVELS + 3 * n + 2] = (r <= c) & s
    e = np.zeros((P, NB, TS), np.float32)
    e[:] = (np.arange(TS)[None, :] // NQ) == np.arange(NB)[:, None]
    h = np.zeros((TS, NB), np.float32)
    h[:] = (np.arange(TS)[:, None] // NQ) == np.arange(NB)[None, :]
    row, new = np.arange(P)[:, None, None], np.arange(TS)[None, None, :]
    group = np.arange(2)[None, :, None]
    seen = (new // NQ == 4 * group + row // 32) & (new % NQ < row % NQ)
    hide = (~seen).astype(np.int32)
    hot = (np.arange(P)[:, None] // NQ % SBH == np.arange(SBH)[None, :]).astype(np.float32)
    slope = lambda h: 2.0 ** (-8.0 * (h + 1) / 6)
    bias = np.full((P, 3, 2, 256), NEG, np.float32)
    t, k = np.arange(P)[:, None], np.arange(256)[None, :]
    for gi, dil in enumerate(DILS):
        for half in range(2):
            d = t + P - k
            ok = (d >= 0) & (d <= P)
            if gi == 2:
                ok = (d >= 0) & (k >= P) & (d % 2 == 0)
                d = d // 2
            bias[:, gi, half] = np.where(ok, -slope(2 * gi + half) * dil * d, NEG)
    sbias = np.full((P, 3, 192), NEG, np.float32)
    row, i, n = np.arange(P)[:, None], np.arange(P)[None, :], np.arange(TS)[None, :]
    b, slot, q = row // 16, row // 8 % 2, row % 8
    for gi, dil in enumerate(DILS):
        sl = np.where(slot == 0, slope(2 * gi), slope(2 * gi + 1)) * dil
        d = P + q // dil - i
        sbias[:, gi, 0:P] = np.where(d <= P, -sl * d, NEG)
        d = q - n % 8
        sbias[:, gi, P:] = np.where((n // 8 == b) & (d >= 0) & (d % dil == 0), -sl * (d // dil), NEG)
    later = (r >= c).astype(np.int32)
    return {"c_bias": bias, "c_sbias": sbias, "c_later": later, "c_new": hide, "c_hot": hot, "c_f32": f,
            "c_mask": u, "c_col": e, "c_row": h}


def high(eng, dst, src):
    return eng.tensor_copy(dst.bitcast(F32R), src)


def low(eng, dst, x, xh):
    return eng.tensor_tensor(dst.bitcast(F32R), x, xh, ALU.subtract)


def product(nc, out, w, x, start, stop):
    (wh, wl), (xh, xl) = ((t.bitcast(F32R) for t in pair) for pair in (w, x))
    nc.tensor.matmul(out, wh, xl, start=start, stop=False)
    nc.tensor.matmul(out, wh, xh, start=False, stop=False)
    return nc.tensor.matmul(out, wl, xh, start=False, stop=stop)


def high_weights(eng, wh, raw, s_load, n_load, s):
    wait_apart(eng, s_load, n_load, s["vec"])
    high(eng, wh, raw).then_inc(s["wh"], 1)


def low_weights(eng, wl, raw, wh, s, n):
    wait_apart(eng, s["wh"], n, s["pool"])
    low(eng, wl, raw, wh).then_inc(s["ws"], 1)


class Tensors:
    pass


@contextmanager
def semaphores(g):
    made = []

    def sem(name):
        made.append(g.nc.alloc_semaphore(name))
        return made[-1]
    g.sem = sem
    yield
    g.nc.clear_and_free_semaphores(made)
    g.nc.all_engine_barrier()


def build(nc, a, outs, scratch):
    with ExitStack() as ctx:
        g = Tensors()
        g.nc, g.a, g.o, g.dr = nc, a, outs, scratch
        sb = lambda name, shape, dt=F32: ctx.enter_context(nc.sbuf_tensor(name, shape, dt))
        g.ps = ctx.enter_context(nc.psum_tensor("ps", [P, 8, 512], F32))
        g.cf = sb("cf", [P, 2, P])
        g.ident, g.ones = g.cf[:, 0, :], g.cf[:, 1, :]
        g.par = sb("par", [P, NPROW])
        g.cw = sb("cw", [P, 3, UT])
        g.cst = sb("cst", [P, UT, 2 * NB])
        g.sbb = sb("sbb", [P, SBH])
        c0 = PROWS["conv_b"][0]
        g.cb = g.par[:, c0:c0 + UT]
        g.col = lambda name, i: g.par[:, PROWS[name][0] + i:PROWS[name][0] + i + 1]
        tensor = lambda name, shape: nc.sbuf_tensor(name, shape, F32)
        with tensor("o", [P, 6, T]) as g.branches:
            g.oa, g.ob, g.oc = g.branches[:, 0:3, :], g.branches[:, 3:5, :], g.branches[:, 5, :]
            with tensor("aux", [P, 3, P]) as g.aux:
                g.blk, g.tri, g.untri = (g.aux[:, i, :] for i in range(3))
                with tensor("pa", [P, AT, T]) as g.pa:
                    with semaphores(g), tensor("xl_a", [P, KT, TP]) as g.xl, tensor("xh_a", [P, KT, TP]) as g.xh:
                        stage_load(g)
                        a_project(g)
                    with semaphores(g):
                        stage_branch_a(g)
                with semaphores(g):
                    stage_branch_b(g)
                with semaphores(g):
                    stage_branch_c(g)
            with tensor("mh", [P, KT, T]) as mh, tensor("ml", [P, KT, T]) as ml:
                with semaphores(g):
                    stage_merge(g, mh, ml)
                with tensor("x1", [P, KT, T]) as x1:
                    with semaphores(g):
                        w_out = a["w_out"][0].rearrange("(k p) f -> p k f", p=P)
                        project_add(g, "wo", w_out, KT, mh, ml, x1, scratch["xt"])
                        norm(g, "n2", x1, "norm_ffn", (mh, ml))
                    with semaphores(g):
                        stage_ffn(g, mh, ml, x1)
                    with semaphores(g), tensor("y", [P, KT, T]) as y:
                        norm(g, "n3", x1, "norm_final", y)
                        store_rows(g, y)


def norm_program(g, pre, src, sq, inv, gain, dst, n_cols, chunks, rows=None):
    nc = g.nc
    s_sq, s_sum, s_mean, s_root, s_inv, s_out, s_h, s_l = (
        g.sem(f"{pre}_{n}") for n in ("sq", "sum", "mean", "root", "inv", "out", "h", "l"))
    parts = isinstance(dst, tuple)

    def act(eng):
        for k in range(KT):
            if k >= 2:
                eng.wait_ge(s_sum, k - 1)
            nc.scalar.activation(sq[:, k % 2, 0:n_cols], src[:, k, 0:n_cols], ACT.Square).then_inc(s_sq, 1)
        eng.wait_ge(s_mean, len(chunks))
        nc.scalar.activation(inv[:, 0:n_cols], inv[:, 0:n_cols], ACT.Sqrt).then_inc(s_root, 1)
        if parts:
            for k in range(KT):
                eng.wait_ge(s_out, k + 1)
                x = sq[:, k % 2, 0:n_cols]
                if rows is not None:
                    nc.scalar.copy(rows[:, k, :], x[:, SEQ - 1:T:NQ])
                nc.scalar.copy(dst[0][:, k, 0:n_cols].bitcast(F32R), x).then_inc(s_h, 1)

    def pe(eng):
        for k in range(KT):
            eng.wait_ge(s_sq, k + 1)
            for b, (c0, n) in enumerate(chunks):
                mm = nc.tensor.matmul(g.ps[:, b, 0:n], g.ones, sq[:, k % 2, c0:c0 + n],
                                      start=(k == 0), stop=(k == KT - 1))
            mm.then_inc(s_sum, 1)

    def dve(eng):
        eng.wait_ge(s_sum, KT)
        for b, (c0, n) in enumerate(chunks):
            nc.vector.tensor_scalar(inv[:, c0:c0 + n], g.ps[:, b, 0:n], 1.0 / D, EPS, ALU.mult,
                                    ALU.add).then_inc(s_mean, 1)
        eng.wait_ge(s_root, 1)
        nc.vector.reciprocal(inv[:, 0:n_cols], inv[:, 0:n_cols]).then_inc(s_inv, 1)
        eng.wait_ge(s_inv, 1)
        for k in range(KT):
            if parts and k >= 2:
                eng.wait_ge(s_l, k - 1)
            out = sq[:, k % 2, 0:n_cols] if parts else dst[:, k, 0:n_cols]
            nc.vector.scalar_tensor_tensor(out=out, in0=src[:, k, 0:n_cols], scalar=g.col(gain, k),
                                           in1=inv[:, 0:n_cols], op0=ALU.mult, op1=ALU.mult).then_inc(s_out, 1)

    def pool(eng):
        for k in range(KT):
            eng.wait_ge(s_h, k + 1)
            low(eng, dst[1][:, k, 0:n_cols], sq[:, k % 2, 0:n_cols], dst[0][:, k, 0:n_cols]).then_inc(s_l, 1)

    return act, pe, dve, pool, s_h


def stage_load(g):
    nc, a = g.nc, g.a
    NT = SEQ // P
    with ExitStack() as ctx:
        sb = lambda name, shape, dt=F32: ctx.enter_context(nc.sbuf_tensor(name, shape, dt))
        prow = sb("prow", [NPROW, P])
        cwrow = sb("cwrow", [UT, 3, P])
        room = g.pa[:, :, :].rearrange("p k t -> p (k t)")
        crow = room[0:2 * NB, 0:2 * FF]
        xrow = room[:, 2 * FF:2 * FF + 3 * D].rearrange("p (i d) -> p i d", d=D)
        shrow = room[0:NB, 2 * FF + 3 * D:2 * FF + 4 * D]
        last = room[0:NB + 1, 2 * FF + 4 * D:2 * FF + 5 * D]
        prev = sb("prev", [P, KT, NB])
        nlast = sb("nlast", [P, KT, NB + 1])
        xt = sb("xt", [P, KT, T])
        sq = sb("sq", [P, 2, T])
        inv = sb("inv", [P, T])
        s_par = g.sem("s_par")
        s_x = [g.sem(f"s_x{i}") for i in range(3)]
        s_xt, s_xc = g.sem("s_xt"), g.sem("s_xc")
        s_pt, s_pc = g.sem("s_pt"), g.sem("s_pc")
        s_lt, s_lc, s_st = g.sem("s_lt"), g.sem("s_lc"), g.sem("s_st")
        s_h, s_l = g.sem("s_h"), g.sem("s_l")
        n_act, n_pe, n_dve, n_pool, n_high = norm_program(g, "n1", xt, sq, inv, "norm_mix", (g.xh, g.xl), T, CH, nlast)
        loads = [0]

        with nc.Block() as block:
            @block.sync
            def _(eng):
                def par(dst, src):
                    eng.dma_start(dst, src).then_inc(s_par, 16)
                    loads[0] += 1
                par(g.cf[:, :, :], a["c_f32"][:, 0:2, :])
                par(g.aux[:, :, :], a["c_f32"][:, 2:5, :])
                for n, (r0, rows) in PROWS.items():
                    src = a[n].rearrange("(r c) -> r c", c=P) if n == "norm_final" else \
                        a[n][0].rearrange("h c -> (h c)").rearrange("(r c) -> r c", c=P) if n == "rwkv_r_k" else \
                        a[n][0].rearrange("(r c) -> r c", c=P)
                    par(prow[r0:r0 + rows, :], src)
                for i in range(3):
                    par(cwrow[:, i, :], a["conv_w"][0, i].rearrange("(r c) -> r c", c=P))
                par(crow[:, :], a["state_conv"][0].rearrange("b r f -> (b r) f"))
                par(shrow[:, :], a["state_shift"][0])
                par(g.sbb[:, :], a["sb_bias"].broadcast_to([P, SBH]))
                for j in range(NT + 1):
                    if j >= 3:
                        eng.wait_ge(s_xt, 2 * (j - 2))
                    n = P if j < NT else TS
                    src = a["x_prompt"][0, j * P:(j + 1) * P, :] if j < NT else \
                        a["x_sample"].rearrange("b q d -> (b q) d")
                    eng.dma_start(xrow[0:n, j % 3, :], src).then_inc(s_x[j % 3], 16)
                eng.wait_ge(s_xc, 2 * (NT + 1))
                eng.dma_start(g.dr["xt"], xt[:, :, :]).then_inc(s_st, 16)
                eng.wait_ge(s_lc, 2)
                eng.dma_start(g.o["shift_prompt"][0], last[0:1, :]).then_inc(s_st, 16)
                eng.dma_start(g.o["shift_sample"][0], last[1:1 + NB, :]).then_inc(s_st, 16)
                eng.wait_ge(s_st, 48)

            @block.gpsimd
            def _(eng):
                eng.wait_ge(s_h, 1)
                low(eng, g.xl[:, :, T:TP], prev[:, :, :], g.xh[:, :, T:TP]).then_inc(s_l, 1)
                n_pool(eng)

            @block.tensor
            def _(eng):
                eng.wait_ge(s_par, 16 * loads[0])
                nc.tensor.transpose(g.ps[:, 0, 0:NPROW], prow[:, :], g.ident[0:NPROW, 0:NPROW]).then_inc(s_pt, 1)
                for i in range(3):
                    mm = nc.tensor.transpose(g.ps[:, 1, i * UT:(i + 1) * UT], cwrow[:, i, :], g.ident[0:UT, 0:UT])
                mm.then_inc(s_pt, 1)
                for i in range(UT):
                    mm = nc.tensor.transpose(g.ps[:, 2 + i // 32, i % 32 * 16:i % 32 * 16 + 16],
                                             crow[:, i * P:(i + 1) * P], g.ident[0:16, 0:16])
                mm.then_inc(s_pt, 1)
                for i in range(KT):
                    mm = nc.tensor.transpose(g.ps[:, 4, i * NB:(i + 1) * NB], shrow[:, i * P:(i + 1) * P],
                                             g.ident[0:NB, 0:NB])
                mm.then_inc(s_pt, 1)
                eng.wait_ge(s_pc, 5)
                for j in range(NT + 1):
                    n = P if j < NT else TS
                    eng.wait_ge(s_x[j % 3], 16 * (j // 3 + 1))
                    for h in range(2):
                        u = 2 * j + h
                        if u >= 4:
                            eng.wait_ge(s_xc, u - 3)
                        for c in range(4):
                            k = 4 * h + c
                            mm = nc.tensor.transpose(g.ps[:, u % 4, c * P:c * P + n],
                                                     xrow[0:n, j % 3, k * P:(k + 1) * P], g.ident[0:n, 0:n])
                        mm.then_inc(s_xt, 1)
                eng.wait_ge(s_xc, 2 * (NT + 1))
                n_pe(eng)
                eng.wait_ge(n_high, KT)
                for h in range(2):
                    for c in range(4):
                        k = 4 * h + c
                        mm = nc.tensor.transpose(g.ps[0:NB + 1, 4 + h, c * P:(c + 1) * P],
                                                 nlast[:, k, :], g.ident)
                    mm.then_inc(s_lt, 1)

            @block.scalar
            def _(eng):
                for u in range(0, 2 * NT + 2, 2):
                    n = P if u // 2 < NT else TS
                    eng.wait_ge(s_xt, u + 1)
                    if u:
                        eng.wait_ge(s_xc, u)
                    j = u // 2
                    nc.scalar.copy(xt[:, 0:4, j * P:j * P + n],
                                   g.ps[:, u % 4, :].rearrange("p (c n) -> p c n", n=P)[:, :, 0:n]).then_inc(s_xc, 1)
                eng.wait_ge(s_xc, 2 * (NT + 1))
                n_act(eng)

            @block.vector
            def _(eng):
                eng.wait_ge(s_pt, 4)
                nc.vector.tensor_copy(g.par[:, :], g.ps[:, 0, 0:NPROW]).then_inc(s_pc, 1)
                nc.vector.tensor_copy(g.cw[:, :, :].rearrange("p a b -> p (a b)"), g.ps[:, 1, 0:3 * UT]).then_inc(s_pc, 1)
                nc.vector.tensor_copy(g.cst[:, 0:32, :].rearrange("p a b -> p (a b)"), g.ps[:, 2, :]).then_inc(s_pc, 1)
                nc.vector.tensor_copy(g.cst[:, 32:UT, :].rearrange("p a b -> p (a b)"),
                                      g.ps[:, 3, 0:(UT - 32) * 16]).then_inc(s_pc, 1)
                nc.vector.tensor_copy(prev[:, :, :], g.ps[:, 4, 0:KT * NB].rearrange("p (k b) -> p k b", b=NB)).then_inc(s_pc, 1)
                eng.wait_ge(s_pc, 5)
                high(eng, g.xh[:, :, T:TP], prev[:, :, :]).then_inc(s_h, 1)
                for u in range(1, 2 * NT + 2, 2):
                    n = P if u // 2 < NT else TS
                    eng.wait_ge(s_xt, u + 1)
                    eng.wait_ge(s_xc, u)
                    j = u // 2
                    nc.vector.tensor_copy(xt[:, 4:8, j * P:j * P + n],
                                          g.ps[:, u % 4, :].rearrange("p (c n) -> p c n", n=P)[:, :, 0:n]).then_inc(s_xc, 1)
                n_dve(eng)
                for h in range(2):
                    eng.wait_ge(s_lt, h + 1)
                    nc.vector.tensor_copy(last[:, h * 512:(h + 1) * 512], g.ps[0:NB + 1, 4 + h, :]).then_inc(s_lc, 1)


def in_pairs(eng, n, body):
    body(0, 0)
    body(1, 1)
    if n // 2 > 1:
        with eng.Fori(1, n // 2) as i:
            body(2 * i, 0)
            body(2 * i + 1, 1)
    if n % 2:
        body(n - 1, 0)


def ahead(eng, n, prepare, body):
    prepare(0, 0)
    for t in range(2):
        prepare(t + 1, 1 - t)
        body(t, t)
    with eng.Fori(1, n // 2 if n % 2 else n // 2 - 1) as i:
        for b in range(2):
            prepare(2 * i + b + 1, 1 - b)
            body(2 * i + b, b)
    if n % 2 == 0:
        prepare(n - 1, 1)
        body(n - 2, 0)
    body(n - 1, (n - 1) % 2)


def high_pair(eng, t, wh, raw, s_mm, s):
    if not first(t):
        eng.wait_ge(s_mm, t - 1)
    high_weights(eng, wh, raw, s["w"], 16 * t + 16, s)


def first(t):
    return isinstance(t, int) and t < 2


def wait_apart(eng, sem, value, tick):
    eng.wait_ge(sem, value)
    eng.sem_inc(tick)


def stage_branch_a(g):
    nc = g.nc
    with ExitStack() as ctx:
        sb = lambda name, shape, dt=F32: ctx.enter_context(nc.sbuf_tensor(name, shape, dt))
        g.av = sb("av", [P, PAIRS, T])
        g.at = sb("at", [P, PAIRS, T])
        g.bn = sb("bn", [P, PAIRS, T])
        g.sc = sb("sc", [P, NU - 1, PAIRS])
        g.scs = sb("scs", [P, PAIRS, NB])
        a_prepare(g)
        a_delta_rule(g)
        a_finish(g)


def a_project(g):
    nc, a = g.nc, g.a
    w = a["w_in"][0].rearrange("(k p) f -> p k f", p=P)
    with ExitStack() as ctx:
        sb = lambda name, shape, dt=F32: ctx.enter_context(nc.sbuf_tensor(name, shape, dt))
        wt = sb("ap_wt", [P, KT, P])
        wl, wh = sb("ap_wl", [P, 2, KT, P]), sb("ap_wh", [P, 2, KT, P])
        raw = sb("ap_raw", [P, 2, 1 + TP])
        dif = sb("ap_dif", [P, 2, T])
        s_mm, s_ev, s_z, s_d, s_mix = (g.sem(f"ap_{n}") for n in ("mm", "ev", "z", "d", "mix"))
        s = {n: g.sem(f"ap_{n}") for n in ("w", "wh", "ws", "sync", "pool", "vec", "st")}
        with nc.Block() as block:
            @block.sync
            def _(eng):
                def body(t, b):
                    if not isinstance(t, int) or t:
                        wait_apart(eng, s["ws"], t, s["sync"])
                    eng.dma_start(wt[:, :, :], w[:, :, bass.ds(t * P, P)]).then_inc(s["w"], 16)
                in_pairs(eng, AT, body)
                eng.dma_start(g.dr["xh"], g.xh[:, :, 0:T]).then_inc(s["st"], 16)
                eng.dma_start(g.dr["xl"], g.xl[:, :, 0:T]).then_inc(s["st"], 16)
                eng.wait_ge(s["st"], 32)

            @block.gpsimd
            def _(eng):
                def body(t, b):
                    low_weights(eng, wl[:, b], wt[:, :, :], wh[:, b], s, t + 1)
                in_pairs(eng, AT, body)

            @block.tensor
            def _(eng):
                def body(t, b):
                    eng.wait_ge(s["ws"], t + 1)
                    if not first(t):
                        eng.wait_ge(s_ev, t - 1)
                    for c, (c0, n) in enumerate(CHP):
                        for k in range(KT):
                            mm = product(nc, g.ps[:, 3 * b + c, 0:n], (wh[:, b, k, :], wl[:, b, k, :]),
                                         (g.xh[:, k, c0:c0 + n], g.xl[:, k, c0:c0 + n]), k == 0, k == KT - 1)
                    mm.then_inc(s_mm, 1)
                in_pairs(eng, AT, body)

            @block.scalar
            def _(eng):
                def body(t, b):
                    eng.wait_ge(s_mm, t + 1)
                    if not first(t):
                        eng.wait_ge(s_mix, t - 1)
                    nc.scalar.copy(raw[:, b, 1:1 + CHP[0][1]], g.ps[:, 3 * b, 0:CHP[0][1]])
                    nc.scalar.copy(raw[:, b, 1 + CHP[1][0]:1 + CHP[2][0]], g.ps[:, 3 * b + 1, 0:CHP[1][1]])
                    nc.scalar.copy(raw[:, b, 1 + CHP[2][0]:1 + TP], g.ps[:, 3 * b + 2, 0:CHP[2][1]]).then_inc(s_ev, 1)
                in_pairs(eng, AT, body)

            @block.vector
            def _(eng):
                nc.vector.memset(raw[:, :, 0:1], 0.0).then_inc(s_z, 1)
                eng.wait_ge(s_z, 1)

                def body(t, b):
                    eng.wait_ge(s_ev, t + 1)
                    if not first(t):
                        eng.wait_ge(s_mix, t - 1)
                    nc.vector.tensor_tensor(dif[:, b, :], raw[:, b, 0:T], raw[:, b, 1:1 + T], ALU.subtract).then_inc(s_d, 1)
                    eng.wait_ge(s_d, 2 * t + 1)
                    nc.vector.tensor_tensor(dif[:, b, SEQ:T:NQ], raw[:, b, 1 + T:1 + TP],
                                            raw[:, b, 1 + SEQ:1 + T:NQ], ALU.subtract).then_inc(s_d, 1)
                    eng.wait_ge(s_d, 2 * t + 2)
                    nc.vector.scalar_tensor_tensor(
                        out=g.pa[:, bass.ds(t, 1), :].rearrange("p a t -> p (a t)"), in0=dif[:, b, :],
                        scalar=g.par[:, bass.ds(PROWS["rwkv_mu"][0] + t, 1)], in1=raw[:, b, 1:1 + T],
                        op0=ALU.mult, op1=ALU.add).then_inc(s_mix, 1)
                ahead(eng, AT, lambda t, b: high_pair(eng, t, wh[:, b], wt[:, :, :], s_mm, s), body)


def a_prepare(g):
    nc, a, pa = g.nc, g.a, g.pa
    R, K, V, LWA = 0, 3, 6, 9
    with ExitStack() as ctx:
        sb = lambda name, shape, dt=F32: ctx.enter_context(nc.sbuf_tensor(name, shape, dt))
        wa2 = sb("wa2", [P, AW])
        keep = sb("keep", [P, T])
        ld = sb("ld", [P, PAIRS, T])
        cu = sb("cu", [P, PAIRS, T])
        kk = sb("kk", [P, PAIRS, T])
        tmp = sb("tmp", [P, 2, T])
        ex = sb("ex", [P, 3, T])
        mid = sb("mid", [P, NU - 1, PAIRS])
        end = sb("end", [P, NU - 1, PAIRS])
        ends = sb("ends", [P, PAIRS, NB])
        omk = sb("omk", [P, PAIRS])
        names = ("w", "th", "lo", "sg", "chain", "cu", "kk", "sq", "ss", "rk", "bs", "nm", "rt", "ex", "ux", "end", "kn")
        s = {n: g.sem(f"pp_{n}") for n in names}
        cols = lambda t: t.rearrange("p (c n) -> p c n", n=CHUNK)
        with nc.Block() as block:
            @block.sync
            def _(eng):
                eng.dma_start(wa2[0:HD, :], a["rwkv_w2"][0]).then_inc(s["w"], 16)
                eng.dma_start(wa2[HD:P, :], a["rwkv_a2"][0]).then_inc(s["w"], 16)

            @block.tensor
            def _(eng):
                eng.wait_ge(s["w"], 32)
                eng.wait_ge(s["th"], 1)
                for p in range(PAIRS):
                    if p:
                        eng.wait_ge(s["sg"], 2 * p)
                    for half in range(2):
                        rows = slice(HD * half, HD * half + HD)
                        for c, (c0, n) in enumerate(CH):
                            mm = nc.tensor.matmul(g.ps[:, 3 * half + c, 0:n], wa2[rows, p * P:(p + 1) * P],
                                                  pa[rows, LWA, c0:c0 + n], start=True, stop=True)
                        mm.then_inc(s["lo"], 1)
                eng.wait_ge(s["sg"], 2 * PAIRS)
                for p in range(PAIRS):
                    if p:
                        eng.wait_ge(s["nm"], 2 * p)
                    eng.wait_ge(s["sq"], p + 1)
                    for c, (c0, n) in enumerate(CH):
                        mm = nc.tensor.matmul(g.ps[:, c, 0:n], g.blk, ex[:, p, c0:c0 + n], start=True, stop=True)
                    mm.then_inc(s["ss"], 1)
                    eng.wait_ge(s["rk"], p + 1)
                    for c, (c0, n) in enumerate(CH):
                        mm = nc.tensor.matmul(g.ps[:, 3 + c, 0:n], g.blk, g.at[:, p, c0:c0 + n], start=True, stop=True)
                    mm.then_inc(s["bs"], 1)

            @block.scalar
            def _(eng):
                nc.scalar.activation(pa[0:HD, LWA, :], pa[0:HD, LWA, :], ACT.Tanh).then_inc(s["th"], 1)
                for p in range(PAIRS):
                    for half, (dst, par) in enumerate(((ld, "rwkv_w0"), (g.av, "rwkv_a0"))):
                        eng.wait_ge(s["lo"], 2 * p + half + 1)
                        for c, (c0, n) in enumerate(CH):
                            i = nc.scalar.activation(dst[:, p, c0:c0 + n], g.ps[:, 3 * half + c, 0:n], ACT.Sigmoid,
                                                     bias=g.col(par, p))
                        i.then_inc(s["sg"], 1)
                for p in range(PAIRS):
                    eng.wait_ge(s["kk"], p + 1)
                    nc.scalar.activation(ex[:, p, :], kk[:, p, :], ACT.Square).then_inc(s["sq"], 1)
                for p in range(PAIRS):
                    eng.wait_ge(s["nm"], 2 * p + 1)
                    nc.scalar.activation(ex[:, p, :], ex[:, p, :], ACT.Sqrt).then_inc(s["rt"], 1)
                eng.wait_ge(s["end"], 1)
                nc.scalar.activation(g.sc[:, :, :], end[:, :, :], ACT.Exp)
                nc.scalar.activation(g.scs[:, :, :], ends[:, :, :], ACT.Exp).then_inc(s["end"], 1)
                for p in range(PAIRS):
                    eng.wait_ge(s["kn"], PAIRS)
                    if p:
                        eng.wait_ge(s["ux"], p)
                    nc.scalar.activation(ex[:, 0, :], cu[:, p, :], ACT.Exp)
                    nc.scalar.activation(ex[:, 1, :], cu[:, p, :], ACT.Exp, scale=-1.0)
                    nc.scalar.activation(ex[:, 2, :], ld[:, p, :], ACT.Exp).then_inc(s["ex"], 1)

            @block.vector
            def _(eng):
                n_chain = [0]

                def link(ins):
                    n_chain[0] += 1
                    ins.then_inc(s["chain"], 1)
                    eng.wait_ge(s["chain"], n_chain[0])

                V_ = nc.vector
                link(V_.memset(keep[:, :], 1.0))
                link(V_.memset(keep[:, 0:SEQ:CHUNK], 0.0))
                link(V_.memset(keep[:, SEQ:T:NQ], 0.0))
                k0 = PROWS["rwkv_k_a"][0]
                link(V_.tensor_scalar(omk[:, :], g.par[:, k0:k0 + PAIRS], -1.0, 1.0, ALU.mult, ALU.add))
                for p in range(PAIRS):
                    V_.tensor_scalar(kk[:, p, :], pa[:, K + p, :], g.col("rwkv_k_k", p), None, ALU.mult).then_inc(s["kk"], 1)
                    eng.wait_ge(s["sg"], 2 * p + 1)
                    link(V_.tensor_scalar(ld[:, p, :], ld[:, p, :], -float(np.exp(-0.5)), None, ALU.mult))
                    link(V_.tensor_tensor_scan(cu[:, p, :], keep[:, :], ld[:, p, :], 0.0, ALU.mult, ALU.add))
                    V_.tensor_copy(mid[:, :, p], cu[:, p, CHUNK // 2 - 1:SEQ:CHUNK])
                    V_.tensor_copy(end[:, :, p], cu[:, p, CHUNK - 1:SEQ:CHUNK])
                    link(V_.tensor_copy(ends[:, p, :], cu[:, p, SEQ + NQ - 1:T:NQ]))
                    link(V_.tensor_tensor(cols(cu[:, p, 0:SEQ]), cols(cu[:, p, 0:SEQ]),
                                          mid[:, :, p:p + 1].broadcast_to([P, NU - 1, CHUNK]), ALU.subtract))
                    V_.tensor_tensor(ld[:, p, :], cu[:, p, :], ld[:, p, :], ALU.subtract).then_inc(s["cu"], 1)
                    eng.wait_ge(s["sg"], 2 * p + 2)
                    link(V_.tensor_scalar(tmp[:, 0, :], g.av[:, p, :], g.col("rwkv_k_a", p), omk[:, p:p + 1],
                                          ALU.mult, ALU.add))
                    link(V_.tensor_tensor(pa[:, K + p, :], pa[:, K + p, :], tmp[:, 0, :], ALU.mult))
                    V_.scalar_tensor_tensor(out=g.at[:, p, :], in0=pa[:, R + p, :], scalar=g.col("rwkv_r_k", p),
                                            in1=pa[:, K + p, :], op0=ALU.mult, op1=ALU.mult).then_inc(s["rk"], 1)
                link(V_.tensor_tensor(end[:, :, :], end[:, :, :], mid[:, :, :], ALU.subtract))
                V_.tensor_tensor(end[:, 0:NU - 2, :], end[:, 0:NU - 2, :], mid[:, 1:NU - 1, :], ALU.add).then_inc(s["end"], 1)
                for p in range(PAIRS):
                    eng.wait_ge(s["ss"], p + 1)
                    for c, (c0, n) in enumerate(CH):
                        i = V_.tensor_scalar(ex[:, p, c0:c0 + n], g.ps[:, c, 0:n], 1e-24, None, ALU.max)
                    i.then_inc(s["nm"], 1)
                    eng.wait_ge(s["bs"], p + 1)
                    for c, (c0, n) in enumerate(CH):
                        i = V_.tensor_tensor(g.bn[:, p, c0:c0 + n], g.ps[:, 3 + c, 0:n], pa[:, V + p, c0:c0 + n], ALU.mult)
                    i.then_inc(s["nm"], 1)
                for p in range(PAIRS):
                    eng.wait_ge(s["rt"], p + 1)
                    link(V_.reciprocal(tmp[:, 1, :], ex[:, p, :]))
                    V_.tensor_tensor(kk[:, p, :], kk[:, p, :], tmp[:, 1, :], ALU.mult).then_inc(s["kn"], 1)
                    eng.wait_ge(s["kn"], p + 1)
                for p in range(PAIRS):
                    eng.wait_ge(s["ex"], p + 1)
                    V_.tensor_tensor(pa[:, R + p, :], pa[:, R + p, :], ex[:, 0, :], ALU.mult)
                    V_.tensor_tensor(pa[:, K + p, :], pa[:, K + p, :], ex[:, 1, :], ALU.mult)
                    link(V_.tensor_tensor(g.av[:, p, :], g.av[:, p, :], ex[:, 1, :], ALU.mult))
                    V_.tensor_tensor(g.av[:, p, :], g.av[:, p, :], kk[:, p, :], ALU.mult)
                    V_.scalar_tensor_tensor(out=g.at[:, p, :], in0=kk[:, p, :], scalar=-1.0, in1=ex[:, 2, :],
                                            op0=ALU.mult, op1=ALU.mult).then_inc(s["ux"], 1)


def a_delta_rule(g):
    with ExitStack() as ctx:
        d = DeltaParts(g, ctx, "dp", 2, P)
        delta_prompt(g, ctx, d)
    with ExitStack() as ctx:
        d = DeltaParts(g, ctx, "ds", 1, TS)
        delta_sample(g, ctx, d)


R0, K0, V0 = 0, 3, 6
NM = 2 * LEVELS


class DeltaParts:

    def __init__(self, g, ctx, pre, nb, n):
        nc = g.nc
        sb = lambda name, shape, dt=F32: ctx.enter_context(nc.sbuf_tensor(f"{pre}_{name}", shape, dt))
        self.g, self.n = g, n
        self.msk = sb("msk", [n, NM + 6, n], I32)
        stg = sb("stg", [P, nb, 5, PAIRS, n])
        tok = sb("tok", [P, nb, 3, PAIRS, P])
        mats = [sb(x, [P, nb, 2, PAIRS, n]) for x in ("lm", "ak", "rb", "rk", "tm", "wm", "zm")]
        ym, um = sb("ym", [P, 2, PAIRS, HD]), sb("um", [P, 2, PAIRS, HD])
        names = ("c", "stg", "stv", "tp", "tk", "pr", "cp", "z", "ze", "pl", "lv", "y", "ye", "u", "ue",
                 "o", "oe", "se", "wi", "zi", "ft", "fe", "out", "x", "sx", "pe", "dve", "pool")
        self.s = {x: g.sem(f"{pre}_{x}") for x in names}
        self.all = (self.s, stg, tok, *mats, ym, um)

    def mask(self, i):
        return self.msk[0:self.n, i:i + 1, 0:self.n].broadcast_to([self.n, PAIRS, self.n])

    def banks(self, q, e):
        return self.g.ps[0:self.n, 2 * q + e, 0:PAIRS * P].rearrange("r (p n) -> r p n", n=P)[:, :, 0:self.n]

    def pe_products(self, eng, b, tp0, cp0):
        nc, g, n = self.g.nc, self.g, self.n
        s, stg = self.s, self.all[1]
        R, A, K, B, V = (stg[:, b, i] for i in range(5))
        eng.wait_ge(s["stg"], tp0 + 1)
        eng.wait_ge(s["stv"], tp0 + 1)
        for q, src in enumerate((K, B, V)):
            for p in range(PAIRS):
                mm = nc.tensor.transpose(g.ps[0:n, q, p * P:(p + 1) * P], src[:, p, :], g.ident)
        mm.then_inc(s["tp"], 1)
        for i, (q, lhs, rhs) in enumerate(((2, A, B), (3, B, A), (0, K, A), (1, B, R), (2, K, R))):
            if i == 2:
                eng.wait_ge(s["tk"], tp0 + 1)
            if i == 4:
                eng.wait_ge(s["cp"], cp0 + 1)
            for e, p, rows in HEADS:
                mm = nc.tensor.matmul(g.ps[0:n, 2 * q + e, p * P:p * P + n], lhs[rows, p, :], rhs[rows, p, :],
                                      start=True, stop=True)
            mm.then_inc(s["pr"], 1)

    def dve_products(self, eng, b, kind, cp0):
        s, _, _, lm, ak, rb, rk, tm, wm, _, _, _ = self.all
        mk = lambda i: self.mask(NM + 3 * kind + i)
        for i, (q, jobs) in enumerate(((2, ((lm, mk(0)), (tm, self.mask(0)))), (3, ((wm, self.mask(LEVELS)),)),
                                       (0, ((ak, mk(1)),)), (1, ((rb, mk(2)),)), (2, ((rk, mk(2)),)))):
            eng.wait_ge(s["zi"], 4)
            wait_apart(eng, s["pr"], cp0 + i + 1, s["dve"])
            for dst, m in jobs:
                for e in range(2):
                    ins = self.g.nc.vector.copy_predicated(dst[0:self.n, b, e], m, self.banks(q, e))
            ins.then_inc(s["cp"], 1)

    def pe_level(self, b, what, q):
        _, _, _, lm, _, _, _, tm, wm, zm, _, _ = self.all
        lhs, rhs = {"z": (lm, wm), "w": (tm, zm), "t": (zm, tm)}[what]
        for e, p, _ in HEADS:
            mm = self.g.nc.tensor.matmul(self.g.ps[0:self.n, 2 * q + e, p * P:p * P + self.n], lhs[0:self.n, b, e, p, :],
                                         rhs[0:self.n, b, e, p, :], start=True, stop=True)
        return mm

    def dve_level(self, b, dst, m, q):
        for e in range(2):
            ins = self.g.nc.vector.copy_predicated(dst[0:self.n, b, e], self.mask(m), self.banks(q, e))
        ins.then_inc(self.s["lv"], 1)


HEADS = [(e, p, slice(HD * e, HD * e + HD)) for e in range(2) for p in range(PAIRS)]


def delta_prompt(g, ctx, d):
    nc, a, pa, V_ = g.nc, g.a, g.pa, g.nc.vector
    sb = lambda name, shape, dt=F32: ctx.enter_context(nc.sbuf_tensor(name, shape, dt))
    st = sb("st", [P, PAIRS, HD])
    so = sb("so", [HD, PAIRS, P])
    s, stg, tok, lm, ak, rb, rk, tm, wm, zm, ym, um = d.all
    G = lambda q: slice(2 * q, 2 * q + 2)
    LV = 4 * (LEVELS - 1) - 2
    with nc.Block() as block:
        @block.sync
        def _(eng):
            eng.dma_start(d.msk[:, :, :], a["c_mask"][0:d.n, :, 0:d.n]).then_inc(s["c"], 16)
            for gi in range(3):
                W = P * DILS[gi]
                for b in range(NB):
                    eng.dma_start(g.o[f"win{gi}_sample"][0, b, 0:W - NQ].rearrange("t a h d -> t (a h d)"),
                                  a[f"cache_win{gi}"][0, b, NQ:W].rearrange("t a h d -> t (a h d)")).then_inc(s["out"], 16)
            eng.wait_ge(s["fe"], 1)
            eng.dma_start(g.o["wkv_prompt"][0, 0].rearrange("h v k -> v h k"),
                          so[:, :, :].rearrange("v p (e k) -> v (p e) k", e=2)).then_inc(s["out"], 16)
            eng.wait_ge(s["out"], 16 * (3 * NB + 1))

        @block.gpsimd
        def _(eng):
            ident = g.ident.rearrange("p (a n) -> p a n", a=1).broadcast_to([P, 2 * PAIRS, P])

            def identity(b):
                for t in (tm, wm):
                    eng.tensor_copy(t[:, b].rearrange("p e a n -> p (e a) n"), ident).then_inc(s["wi"], 1)

            def stage(u, b):
                for q, t in enumerate((pa[:, R0:R0 + 3], g.at, pa[:, K0:K0 + 3], g.av)):
                    ins = eng.tensor_copy(stg[:, b, q], t[:, :, bass.ds(u * P, P)])
                ins.then_inc(s["stg"], 1)

            stage(0, 0)
            for t in (lm, ak, rb, rk):
                eng.memset(t[:, :, :, :, :], 0.0).then_inc(s["zi"], 1)
            identity(0)
            stage(1, 1)
            identity(1)
            with eng.Fori(1, 4) as i:
                for b in range(2):
                    eng.wait_ge(s["ue"], 2 * i + b - 1)
                    wait_apart(eng, s["o"], 2 * i + b - 1, s["pool"])
                    identity(b)
                    stage(2 * i + b, b)

        @block.tensor
        def _(eng):
            def sequential(b, u):
                tk, tb, tv = (tok[:, b, i] for i in range(3))
                eng.wait_ge(s["se"], u + 1)
                for e, p, rows in HEADS:
                    out = g.ps[:, e, p * HD:(p + 1) * HD]
                    nc.tensor.matmul(out, stg[rows, b, 1, p, :], st[rows, p, :], start=True, stop=False)
                    mm = nc.tensor.matmul(out, ak[:, b, e, p, :], tv[:, p, HD * e:HD * e + HD], start=False, stop=True)
                mm.then_inc(s["y"], 1)
                eng.wait_ge(s["ye"], u + 1)
                for e, p, rows in HEADS:
                    mm = nc.tensor.matmul(g.ps[:, 2 + e, p * HD:(p + 1) * HD], wm[:, b, e, p, :], ym[:, e, p, :],
                                          start=True, stop=True)
                mm.then_inc(s["u"], 1)
                wait_apart(eng, s["ue"], u + 1, s["pe"])
                for e, p, rows in HEADS:
                    out = g.ps[rows, 6 + e, p * HD:(p + 1) * HD]
                    hc = slice(HD * e, HD * e + HD)
                    nc.tensor.matmul(out, g.ident[rows, rows], st[rows, p, :], start=True, stop=False)
                    nc.tensor.matmul(out, tk[:, p, hc], tv[:, p, hc], start=False, stop=False)
                    mm = nc.tensor.matmul(out, tb[:, p, hc], um[:, e, p, :], start=False, stop=True)
                if not isinstance(u, int) or u:
                    wait_apart(eng, s["oe"], 2 * u, s["pe"])
                for e, p, rows in HEADS:
                    out = g.ps[rows, 4 + e, p * P:(p + 1) * P]
                    hc = slice(HD * e, HD * e + HD)
                    nc.tensor.matmul(out, st[rows, p, :], stg[rows, b, 0, p, :], start=True, stop=False)
                    nc.tensor.matmul(out, tv[:, p, hc], rk[:, b, e, p, :], start=False, stop=False)
                    mm = nc.tensor.matmul(out, um[:, e, p, :], rb[:, b, e, p, :], start=False, stop=True)
                mm.then_inc(s["o"], 1)

            def duo(i, peeled):
                for b in range(2):
                    u = 2 * i + b
                    if b == 0 and not peeled:
                        eng.wait_ge(s["oe"], 2 * u)
                        eng.wait_ge(s["se"], u + 1)
                    if not peeled or b:
                        eng.wait_ge(s["cp"], 5 * u)
                    d.pe_products(eng, b, u, 5 * u)
                for l in range(2, LEVELS + 1):
                    for b in range(2):
                        if l == 2:
                            if b == 0:
                                eng.wait_ge(s["cp"], 10 * i + 10)
                        elif l > 2:
                            eng.wait_ge(s["lv"], LV * i + 4 * (l - 2) - 2 + 2 * b)
                        d.pe_level(b, "z", b).then_inc(s["z"], 1)
                    for b in range(2):
                        eng.wait_ge(s["ze"], 12 * i + 2 * (l - 2) + b + 1)
                        for j, what in enumerate("wt" if l < LEVELS else "w"):
                            base = 4 * (l - 2) + 2 * b + j if l < LEVELS else 4 * (l - 2) + b
                            if b:
                                eng.wait_ge(s["lv"], LV * i + (base - 1 if l < LEVELS else base))
                            d.pe_level(b, what, 2 + j).then_inc(s["pl"], 1)
                eng.wait_ge(s["lv"], LV * i + LV)
                for b in range(2):
                    sequential(b, 2 * i + b)

            duo(0, True)
            with eng.Fori(1, 4) as i:
                duo(i, False)
            eng.wait_ge(s["se"], NU)
            for p in range(PAIRS):
                mm = nc.tensor.transpose(g.ps[0:HD, 6, p * P:(p + 1) * P], st[:, p, :], g.ident)
            mm.then_inc(s["ft"], 1)

        @block.scalar
        def _(eng):
            def sequential(b, u):
                eng.wait_ge(s["y"], u + 1)
                nc.scalar.copy(ym[:, :, :, :].rearrange("t e p v -> t e (p v)"),
                               g.ps[:, 0:2, 0:PAIRS * HD]).then_inc(s["ye"], 1)
                eng.wait_ge(s["o"], u + 1)
                for e in range(2):
                    rows = slice(HD * e, HD * e + HD)
                    nc.scalar.copy(g.oa[rows, :, bass.ds(u * P, P)],
                                   g.ps[rows, 4 + e, 0:PAIRS * P].rearrange("r (p t) -> r p t", t=P)).then_inc(s["oe"], 1)

            def duo(i):
                for b in range(2):
                    u = 2 * i + b
                    eng.wait_ge(s["tp"], u + 1)
                    nc.scalar.copy(tok[:, b].rearrange("t q p n -> t q (p n)"), g.ps[:, 0:3, 0:PAIRS * P]).then_inc(s["tk"], 1)
                for l in range(2, LEVELS + 1):
                    for b in range(2):
                        eng.wait_ge(s["z"], 12 * i + 2 * (l - 2) + b + 1)
                        nc.scalar.copy(zm[:, b].rearrange("t e p n -> t e (p n)"),
                                       g.ps[:, G(b), 0:PAIRS * P]).then_inc(s["ze"], 1)
                for b in range(2):
                    sequential(b, 2 * i + b)
            def stage_v(i, peeled):
                for b in range(2):
                    if not peeled:
                        eng.wait_ge(s["tp"], 2 * i + b - 1)
                    nc.scalar.copy(stg[:, b, 4], pa[:, V0:V0 + 3, bass.ds((2 * i + b) * P, P)]).then_inc(s["stv"], 1)
            stage_v(0, True)
            duo(0)
            with eng.Fori(1, 4) as i:
                stage_v(i, False)
                duo(i)

        @block.vector
        def _(eng):
            eng.wait_ge(s["c"], 16)
            eng.wait_ge(s["zi"], 4)
            V_.memset(st[:, :, :], 0.0).then_inc(s["se"], 1)

            def sequential(b, u):
                eng.wait_ge(s["u"], u + 1)
                V_.tensor_copy(um[:, :, :, :].rearrange("t e p v -> t e (p v)"),
                               g.ps[:, 2:4, 0:PAIRS * HD]).then_inc(s["ue"], 1)
                eng.wait_ge(s["o"], u + 1)
                for e in range(2):
                    rows = slice(HD * e, HD * e + HD)
                    ins = V_.tensor_tensor(st[rows, :, :],
                                           g.ps[rows, 6 + e, 0:PAIRS * HD].rearrange("r (p v) -> r p v", v=HD),
                                           g.sc[rows, bass.ds(u, 1), :].rearrange("r a p -> r (a p)").rearrange(
                                               "r (p a) -> r p a", a=1).broadcast_to([HD, PAIRS, HD]), ALU.mult)
                ins.then_inc(s["se"], 1)

            def duo(i, peeled):
                for b in range(2):
                    u = 2 * i + b
                    eng.wait_ge(s["wi"], 2 * u + 2)
                    d.dve_products(eng, b, 0, 5 * u)
                for l in range(2, LEVELS + 1):
                    for b in range(2):
                        for j in range(2 if l < LEVELS else 1):
                            n_pl = LV * i + 4 * (l - 2) + (2 * b + j if l < LEVELS else b)
                            wait_apart(eng, s["pl"], n_pl + 1, s["dve"])
                            d.dve_level(b, (wm, tm)[j], (LEVELS + l - 1, l - 1)[j], 2 + j)
                for b in range(2):
                    sequential(b, 2 * i + b)
            duo(0, True)
            with eng.Fori(1, 4) as i:
                duo(i, False)
            eng.wait_ge(s["ft"], 1)
            V_.tensor_copy(so[:, :, :].rearrange("v p k -> v (p k)"), g.ps[0:HD, 6, 0:PAIRS * P]).then_inc(s["fe"], 1)


def delta_sample(g, ctx, d):
    nc, a, pa, V_ = g.nc, g.a, g.pa, g.nc.vector
    sb = lambda name, shape, dt=F32: ctx.enter_context(nc.sbuf_tensor(name, shape, dt))
    sr = sb("sr", [HD, NB, AH, HD])
    s0 = sb("s0", [P, PAIRS, NB, HD])
    sn = sb("sn", [HD, NB, AH, HD])
    am = sb("am", [P, PAIRS, NB, TS])
    ux = sb("ux", [P, 2, PAIRS, NB, HD])
    vx = sb("vx", [P, 2, PAIRS, NB, HD])
    colm = sb("colm", [P, NB, TS])
    rowm = sb("rowm", [TS, NB])
    s, stg, tok, lm, ak, rb, rk, tm, wm, zm, ym, um = d.all
    tk, tb, tv = (tok[:, 0, i] for i in range(3))
    NL = 3
    with nc.Block() as block:
        @block.sync
        def _(eng):
            eng.dma_start(d.msk[:, :, :], a["c_mask"][0:d.n, :, 0:d.n]).then_inc(s["c"], 16)
            eng.dma_start(colm[:, :, :], a["c_col"]).then_inc(s["c"], 16)
            eng.dma_start(rowm[:, :], a["c_row"]).then_inc(s["c"], 16)
            for b in range(NB):
                eng.dma_start(sr[:, b], a["state_wkv"][0, b].rearrange("h v k -> v h k")).then_inc(s["sx"], 16)
            for b in range(NB):
                eng.wait_ge(s["fe"], 2 * PAIRS)
                eng.dma_start(g.o["wkv_sample"][0, b].rearrange("h v k -> v h k"), sn[:, b]).then_inc(s["out"], 16)
            eng.wait_ge(s["out"], 16 * NB)

        @block.gpsimd
        def _(eng):
            for t in (tok, lm, ak, rb, rk, ux, vx):
                eng.memset(t[:, :, :, :, :], 0.0).then_inc(s["zi"], 1)
            eng.memset(um[:, :, :, :], 0.0).then_inc(s["zi"], 1)
            ident = g.ident[0:TS, 0:TS].rearrange("p (a n) -> p a n", a=1).broadcast_to([TS, 2 * PAIRS, TS])
            for t in (tm, wm):
                eng.tensor_copy(t[0:TS, 0].rearrange("p e a n -> p (e a) n"), ident).then_inc(s["wi"], 1)
            for q, t in enumerate((pa[:, R0:R0 + 3], g.at, pa[:, K0:K0 + 3], g.av)):
                ins = eng.tensor_copy(stg[:, 0, q], t[:, :, SEQ:T])
            ins.then_inc(s["stg"], 1)

        @block.tensor
        def _(eng):
            d.pe_products(eng, 0, 0, 0)
            for l in range(2, NL + 1):
                eng.wait_ge(s["cp"], 5)
                eng.wait_ge(s["lv"], 2 * (l - 2))
                d.pe_level(0, "z", 0).then_inc(s["z"], 1)
                eng.wait_ge(s["ze"], l - 1)
                d.pe_level(0, "w", 2).then_inc(s["pl"], 1)
                d.pe_level(0, "t", 3).then_inc(s["pl"], 1)
            eng.wait_ge(s["lv"], 2 * (NL - 1))
            eng.wait_ge(s["sx"], 16 * NB)
            for p in range(PAIRS):
                for b in range(NB):
                    mm = nc.tensor.transpose(g.ps[:, 2 + p, b * HD:(b + 1) * HD],
                                             sr[:, b, 2 * p:2 * p + 2, :].rearrange("v h k -> v (h k)"),
                                             g.ident[0:HD, 0:HD])
            mm.then_inc(s["x"], 1)
            eng.wait_ge(s["se"], 1)
            for e, p, rows in HEADS:
                out = g.ps[0:TS, e, p * HD:(p + 1) * HD]
                for b in range(NB):
                    nc.tensor.matmul(out, am[rows, p, b, :], s0[rows, p, b, :], start=(b == 0), stop=False)
                mm = nc.tensor.matmul(out, ak[:, 0, e, p, :], tv[:, p, HD * e:HD * e + HD], start=False, stop=True)
            mm.then_inc(s["y"], 1)
            eng.wait_ge(s["ye"], 1)
            for e, p, rows in HEADS:
                mm = nc.tensor.matmul(g.ps[0:TS, 2 + e, p * HD:(p + 1) * HD], wm[0:TS, 0, e, p, :], ym[0:TS, e, p, :],
                                      start=True, stop=True)
            mm.then_inc(s["u"], 1)
            eng.wait_ge(s["ue"], 1)
            for e, p, rows in HEADS:
                hc = slice(HD * e, HD * e + HD)
                for b in range(NB):
                    nc.tensor.matmul(g.ps[rows, e, p * TS + NQ * b:p * TS + NQ * b + NQ], s0[rows, p, b, :],
                                     stg[rows, 0, 0, p, NQ * b:NQ * b + NQ], start=(b == 0), stop=False,
                                     skip_group_check=True)
                out = g.ps[rows, e, p * TS:(p + 1) * TS]
                nc.tensor.matmul(out, tv[:, p, hc], rk[:, 0, e, p, :], start=False, stop=False, skip_group_check=True)
                mm = nc.tensor.matmul(out, um[:, e, p, :], rb[:, 0, e, p, :], start=False, stop=True,
                                      skip_group_check=True)
            mm.then_inc(s["o"], 1)
            eng.wait_ge(s["ue"], 2)
            for e, p, rows in HEADS:
                out = g.ps[rows, 2 + 2 * p + e, :]
                hc = slice(HD * e, HD * e + HD)
                nc.tensor.matmul(out, g.ident[rows, rows], s0[rows, p].rearrange("k b v -> k (b v)"), start=True, stop=False)
                nc.tensor.matmul(out, tk[:, p, hc], vx[:, e, p].rearrange("t b v -> t (b v)"), start=False, stop=False)
                mm = nc.tensor.matmul(out, tb[:, p, hc], ux[:, e, p].rearrange("t b v -> t (b v)"), start=False, stop=True)
            mm.then_inc(s["o"], 1)
            eng.wait_ge(s["oe"], 2)
            eng.wait_ge(s["se"], 2)
            for i in range(2 * PAIRS):
                p, half = i // 2, i % 2
                for j in range(4):
                    mm = nc.tensor.transpose(g.ps[0:HD, i, j * P:(j + 1) * P], s0[:, p, 4 * half + j, :], g.ident)
                mm.then_inc(s["ft"], 1)

        @block.scalar
        def _(eng):
            nc.scalar.copy(stg[:, 0, 4], pa[:, V0:V0 + 3, SEQ:T]).then_inc(s["stv"], 1)
            eng.wait_ge(s["tp"], 1)
            eng.wait_ge(s["zi"], 8)
            nc.scalar.copy(tok[0:TS, 0].rearrange("t q p n -> t q (p n)"), g.ps[0:TS, 0:3, 0:PAIRS * P]).then_inc(s["tk"], 1)
            for l in range(2, NL + 1):
                eng.wait_ge(s["z"], l - 1)
                for e in range(2):
                    ins = nc.scalar.copy(zm[0:TS, 0, e], d.banks(0, e))
                ins.then_inc(s["ze"], 1)
            eng.wait_ge(s["y"], 1)
            nc.scalar.copy(ym[0:TS, :, :, :].rearrange("t e p v -> t e (p v)"), g.ps[0:TS, 0:2, 0:PAIRS * HD]).then_inc(s["ye"], 1)
            eng.wait_ge(s["o"], 1)
            for e in range(2):
                rows = slice(HD * e, HD * e + HD)
                nc.scalar.copy(g.oa[rows, :, SEQ:T], g.ps[rows, e, 0:PAIRS * TS].rearrange("r (p t) -> r p t", t=TS)).then_inc(s["oe"], 1)
            eng.wait_ge(s["oe"], 2)

        @block.vector
        def _(eng):
            eng.wait_ge(s["c"], 48)
            eng.wait_ge(s["zi"], 8)
            eng.wait_ge(s["wi"], 2)
            d.dve_products(eng, 0, 1, 0)
            for l in range(2, NL + 1):
                for j in range(2):
                    eng.wait_ge(s["pl"], 2 * (l - 2) + j + 1)
                    d.dve_level(0, (wm, tm)[j], (LEVELS + l - 1, l - 1)[j], 2 + j)
            eng.wait_ge(s["stg"], 1)
            for p in range(PAIRS):
                V_.tensor_tensor(am[:, p], stg[:, 0, 1, p:p + 1, :].broadcast_to([P, NB, TS]), colm[:, :, :], ALU.mult)
            eng.wait_ge(s["x"], 1)
            V_.tensor_copy(s0[:, :, :, :].rearrange("k p b v -> k p (b v)"), g.ps[:, 2:5, :]).then_inc(s["se"], 1)
            eng.wait_ge(s["u"], 1)
            V_.tensor_copy(um[0:TS, :, :, :].rearrange("t e p v -> t e (p v)"), g.ps[0:TS, 2:4, 0:PAIRS * HD]).then_inc(s["ue"], 1)
            eng.wait_ge(s["ue"], 1)
            eng.wait_ge(s["tk"], 1)
            rm = rowm[:, :].rearrange("t (b a) -> t b a", a=1).broadcast_to([TS, NB, HD])
            for e, p, rows in HEADS:
                V_.tensor_tensor(ux[0:TS, e, p], um[0:TS, e, p:p + 1, :].broadcast_to([TS, NB, HD]), rm, ALU.mult)
                ins = V_.tensor_tensor(vx[0:TS, e, p], tv[0:TS, p:p + 1, HD * e:HD * e + HD].broadcast_to([TS, NB, HD]), rm, ALU.mult)
            ins.then_inc(s["ue"], 1)
            eng.wait_ge(s["o"], 2)
            for e, p, rows in HEADS:
                ins = V_.tensor_tensor(s0[rows, p], g.ps[rows, 2 + 2 * p + e, :].rearrange("k (b v) -> k b v", v=HD),
                                       g.scs[rows, p, :].rearrange("k (b a) -> k b a", a=1).broadcast_to([HD, NB, HD]), ALU.mult)
            ins.then_inc(s["se"], 1)
            for i in range(2 * PAIRS):
                p, half = i // 2, i % 2
                eng.wait_ge(s["ft"], i + 1)
                V_.tensor_copy(sn[:, 4 * half:4 * half + 4, 2 * p:2 * p + 2, :].rearrange("v b h k -> v b (h k)"),
                               g.ps[0:HD, i, :].rearrange("v (b x) -> v b x", x=P)).then_inc(s["fe"], 1)


def a_finish(g):
    nc, a, oa, V_ = g.nc, g.a, g.oa, g.nc.vector
    with ExitStack() as ctx:
        sb = lambda name, shape, dt=F32: ctx.enter_context(nc.sbuf_tensor(name, shape, dt))
        g2 = sb("g2", [P, AW])
        om = sb("om", [P, PAIRS, T])
        sq = sb("af_sq", [P, PAIRS, T])
        iv = sb("af_iv", [P, PAIRS, T])
        names = ("w", "lg", "mean", "om", "sq", "var", "ms", "rt", "chain", "g", "done")
        s = {n: g.sem(f"af_{n}") for n in names}
        with nc.Block() as block:
            @block.sync
            def _(eng):
                eng.dma_start(g2[:, :], a["rwkv_g2"][0]).then_inc(s["w"], 16)

            @block.tensor
            def _(eng):
                def put(lhs, rhs, b0, inc):
                    for c, (c0, n) in enumerate(CH):
                        mm = nc.tensor.matmul(g.ps[:, b0 + c, 0:n], lhs, rhs[:, c0:c0 + n], start=True, stop=True)
                    mm.then_inc(s[inc], 1)
                for p in range(PAIRS):
                    if p > 0:
                        eng.wait_ge(s["om"], p)
                    put(g.blk, oa[:, p, :], 0, "mean")
                    if p > 0:
                        eng.wait_ge(s["ms"], p)
                    eng.wait_ge(s["sq"], p + 1)
                    put(g.blk, sq[:, p, :], 3, "var")
                eng.wait_ge(s["w"], 16)
                eng.wait_ge(s["lg"], 1)
                for p in range(PAIRS):
                    eng.wait_ge(s["om"], PAIRS)
                    eng.wait_ge(s["ms"], PAIRS)
                    if p == 2:
                        eng.wait_ge(s["done"], 1)
                    put(g2[:, p * P:(p + 1) * P], g.pa[:, 10, :], 3 * (p % 2), "g")

            @block.scalar
            def _(eng):
                nc.scalar.activation(g.pa[:, 10, :], g.pa[:, 10, :], ACT.Sigmoid).then_inc(s["lg"], 1)
                for p in range(PAIRS):
                    eng.wait_ge(s["om"], p + 1)
                    nc.scalar.activation(sq[:, p, :], om[:, p, :], ACT.Square).then_inc(s["sq"], 1)
                for p in range(PAIRS):
                    eng.wait_ge(s["ms"], p + 1)
                    nc.scalar.activation(iv[:, p, :], iv[:, p, :], ACT.Sqrt).then_inc(s["rt"], 1)

            @block.vector
            def _(eng):
                n_chain = [0]

                def link(ins):
                    n_chain[0] += 1
                    ins.then_inc(s["chain"], 1)
                    eng.wait_ge(s["chain"], n_chain[0])
                for p in range(PAIRS):
                    eng.wait_ge(s["mean"], p + 1)
                    for c, (c0, n) in enumerate(CH):
                        ins = V_.scalar_tensor_tensor(out=om[:, p, c0:c0 + n], in0=g.ps[:, c, 0:n], scalar=-1.0 / HD,
                                                      in1=oa[:, p, c0:c0 + n], op0=ALU.mult, op1=ALU.add)
                    ins.then_inc(s["om"], 1)
                    eng.wait_ge(s["var"], p + 1)
                    for c, (c0, n) in enumerate(CH):
                        ins = V_.tensor_scalar(iv[:, p, c0:c0 + n], g.ps[:, 3 + c, 0:n], 1.0 / HD, GN_EPS, ALU.mult, ALU.add)
                    ins.then_inc(s["ms"], 1)
                for p in range(PAIRS):
                    eng.wait_ge(s["rt"], p + 1)
                    link(V_.reciprocal(sq[:, p, :], iv[:, p, :]))
                    link(V_.tensor_tensor(om[:, p, :], om[:, p, :], sq[:, p, :], ALU.mult))
                    link(V_.scalar_tensor_tensor(out=om[:, p, :], in0=om[:, p, :], scalar=g.col("rwkv_ln_w", p),
                                                 in1=g.bn[:, p, :], op0=ALU.mult, op1=ALU.add))
                    eng.wait_ge(s["g"], p + 1)
                    for c, (c0, n) in enumerate(CH):
                        ins = V_.scalar_tensor_tensor(out=oa[:, p, c0:c0 + n], in0=om[:, p, c0:c0 + n],
                                                      scalar=g.col("rwkv_ln_b", p), in1=g.ps[:, 3 * (p % 2) + c, 0:n],
                                                      op0=ALU.add, op1=ALU.mult)
                    ins.then_inc(s["done"], 1)


def project(g, pre, w, n_tiles, dst):
    nc = g.nc
    with ExitStack() as ctx:
        wl, wh = (ctx.enter_context(nc.sbuf_tensor(f"{pre}_w{x}", [P, 2, KT, P], F32)) for x in "lh")
        wt = ctx.enter_context(nc.sbuf_tensor(f"{pre}_wt", [P, KT, P], F32))
        g.xh, g.xl = (ctx.enter_context(nc.sbuf_tensor(f"{pre}_x{x}", [P, KT, T], F32)) for x in "hl")
        s_mm, s_a, s_v = (g.sem(f"{pre}_{n}") for n in ("mm", "a", "v"))
        s = {n: g.sem(f"{pre}_{n}") for n in ("w", "wh", "ws", "sync", "pool", "vec")}
        s_x = [g.sem(f"{pre}_x{i}") for i in range(len(CH))]
        with nc.Block() as block:
            @block.sync
            def _(eng):
                def body(t, b):
                    if not isinstance(t, int) or t:
                        wait_apart(eng, s["ws"], t, s["sync"])
                    eng.dma_start(wt[:, :, :], w[:, :, bass.ds(t * P, P)]).then_inc(s["w"], 16)
                in_pairs(eng, n_tiles, body)

            @block.gpsimd
            def _(eng):
                def body(t, b):
                    low_weights(eng, wl[:, b], wt[:, :, :], wh[:, b], s, t + 1)
                in_pairs(eng, n_tiles, body)

            @block.tensor
            def _(eng):
                def body(t, b):
                    eng.wait_ge(s["ws"], t + 1)
                    if not first(t):
                        eng.wait_ge(s_a, t - 1)
                        eng.wait_ge(s_v, t - 1)
                    for c, (c0, n) in enumerate(CH):
                        if isinstance(t, int) and t == 0:
                            eng.wait_ge(s_x[c], 32)
                        for k in range(KT):
                            mm = product(nc, g.ps[:, 3 * b + c, 0:n], (wh[:, b, k, :], wl[:, b, k, :]),
                                         (g.xh[:, k, c0:c0 + n], g.xl[:, k, c0:c0 + n]), k == 0, k == KT - 1)
                    mm.then_inc(s_mm, 1)
                in_pairs(eng, n_tiles, body)

            def out(t, c0, n):
                return dst[:, bass.ds(t, 1), c0:c0 + n].rearrange("p a t -> p (a t)")

            @block.scalar
            def _(eng):
                load_xn(g, eng, g.xh, g.xl, s_x)

                def body(t, b):
                    eng.wait_ge(s_mm, t + 1)
                    nc.scalar.copy(out(t, *CH[0]), g.ps[:, 3 * b, 0:CH[0][1]]).then_inc(s_a, 1)
                in_pairs(eng, n_tiles, body)

            @block.vector
            def _(eng):
                def body(t, b):
                    eng.wait_ge(s_mm, t + 1)
                    n = CH[1][1]
                    nc.vector.tensor_copy(out(t, CH[1][0], 2 * n).rearrange("p (c t) -> p c t", t=n),
                                          g.ps[:, 3 * b + 1:3 * b + 3, 0:n]).then_inc(s_v, 1)
                ahead(eng, n_tiles, lambda t, b: high_pair(eng, t, wh[:, b], wt[:, :, :], s_mm, s), body)


def load_xn(g, eng, xh, xl, s_x):
    for c, (c0, n) in enumerate(CH):
        eng.dma_start(xh[:, :, c0:c0 + n], g.dr["xh"][:, :, c0:c0 + n]).then_inc(s_x[c], 16)
        eng.dma_start(xl[:, :, c0:c0 + n], g.dr["xl"][:, :, c0:c0 + n]).then_inc(s_x[c], 16)


A_COLS, SB_COLS, DIL_COLS = 1408, 768, 1152


def stage_branch_b(g):
    nc, a = g.nc, g.a
    w_in = a["w_in"][0].rearrange("(k p) f -> p k f", p=P)
    with ExitStack() as ctx:
        g.qb = ctx.enter_context(nc.sbuf_tensor("qb", [P, 6, T], F32))
        project(g, "bp", w_in[:, :, A_COLS:A_COLS + SB_COLS], 6, g.qb)
        g.kvt = ctx.enter_context(nc.sbuf_tensor("kvt", [P, SEQ // P + 1, 512], F32))
        b_prompt(g)
        b_sample(g)


def b_prompt(g):
    nc, a, V_ = g.nc, g.a, g.nc.vector
    NT = SEQ // P
    with ExitStack() as ctx:
        sb = lambda name, shape, dt=F32: ctx.enter_context(nc.sbuf_tensor(name, shape, dt))
        x = sb("bq_x", [P, 3, 512])
        l, sp, at = (sb(f"bq_{n}", [P, 2, 512]) for n in ("l", "sp", "at"))
        later = sb("bq_later", [P, P], I32)
        zero = sb("bq_zero", [P, P])
        names = ("c", "kt", "ka", "kv", "st", "z", "x", "l", "sp", "tri", "arg", "at", "am", "pv", "ob", "ch", "raw")
        s = {n: g.sem(f"bq_{n}") for n in names}
        units = [(p, j, b, e) for p in range(2) for j in range(2) for b in range(4 * j + 3, -1, -1) for e in range(2)]
        NUN = len(units)
        top = lambda j, b: b == 4 * j + 3
        skip = lambda j, b: max(0, b * P - 512 * j)
        diag = lambda j, b: b >= 4 * j
        masked = lambda i: sum(diag(j, b) for _, j, b, _ in units[:i + 1])
        group = lambda i: units[i][0] * 2 + units[i][1]

        with nc.Block() as block:
            @block.sync
            def _(eng):
                eng.dma_start(later[:, :], a["c_later"]).then_inc(s["c"], 16)
                eng.wait_ge(s["ka"], NT // 2 + 1)
                eng.wait_ge(s["kv"], NT // 2)
                for n, c in (("k", 0), ("v", 256)):
                    eng.dma_start(g.o[f"sb_{n}_prompt"][0, 0].rearrange("(j p) h d -> p j (h d)", p=P),
                                  g.kvt[:, 0:NT, c:c + 256]).then_inc(s["st"], 16)
                    eng.dma_start(g.o[f"sb_{n}_sample"][0].rearrange("b q h d -> (b q) (h d)"),
                                  g.kvt[0:TS, NT, c:c + 256]).then_inc(s["st"], 16)
                eng.wait_ge(s["st"], 64)

            @block.tensor
            def _(eng):
                for j in range(NT + 1):
                    n = P if j < NT else TS
                    if j >= 2:
                        eng.wait_ge(s["ka"] if j % 2 == 0 else s["kv"], j // 2)
                    for q in range(4):
                        mm = nc.tensor.transpose(g.ps[0:n, 6 + j % 2, q * P:(q + 1) * P],
                                                 g.qb[:, 2 + q, j * P:j * P + n], g.ident)
                    mm.then_inc(s["kt"], 1)
                eng.wait_ge(s["ka"], NT // 2 + 1)
                eng.wait_ge(s["kv"], NT // 2)

                def part(i):
                    p, j, b, e = units[i]
                    c0 = skip(j, b)
                    return p, j, b, e, c0, slice(HD * e, HD * e + HD)
                for i in range(NUN + 3):
                    if i < NUN:
                        p, j, b, e, c0, rows = part(i)
                        if i >= 2:
                            eng.wait_ge(s["x"], i - 1)
                        nc.tensor.matmul(g.ps[:, i % 2, c0:512], g.qb[rows, 2 + p, b * P:(b + 1) * P],
                                         g.qb[rows, p, 512 * j + c0:512 * (j + 1)], start=True, stop=True).then_inc(s["z"], 1)
                    if i >= 3:
                        p, j, b, e, c0, rows = part(i - 3)
                        eng.wait_ge(s["at"], i - 2)
                        eng.wait_ge(s["am"], masked(i - 3))
                        if top(j, b) and group(i - 3):
                            eng.wait_ge(s["ob"], 2 * (group(i - 3) - 1) + e + 1)
                        nc.tensor.matmul(g.ps[rows, 4 + e, c0:512], g.kvt[:, b, 256 + P * p + HD * e:256 + P * p + HD * e + HD],
                                         at[:, (i - 3) % 2, c0:512], start=top(j, b), stop=(b == 0),
                                         skip_group_check=True).then_inc(s["pv"], 1)
                    if 2 <= i < NUN + 2:
                        p, j, b, e, c0, rows = part(i - 2)
                        eng.wait_ge(s["arg"], i - 1)
                        nc.tensor.matmul(g.ps[:, 2 + e, c0:512], g.untri, sp[:, (i - 2) % 2, c0:512],
                                         start=False, stop=True, skip_group_check=True).then_inc(s["ch"], 1)
                    if 1 <= i < NUN + 1:
                        p, j, b, e, c0, rows = part(i - 1)
                        eng.wait_ge(s["sp"], i)
                        nc.tensor.matmul(g.ps[:, 2 + e, c0:512], g.tri, sp[:, (i - 1) % 2, c0:512],
                                         start=top(j, b), stop=True, skip_group_check=True).then_inc(s["tri"], 1)

            @block.scalar
            def _(eng):
                nc.scalar.preload_act_table_set("natural_log_exp_and_others")
                for j in range(0, NT + 1, 2):
                    n = P if j < NT else TS
                    eng.wait_ge(s["kt"], j + 1)
                    nc.scalar.copy(g.kvt[0:n, j, :], g.ps[0:n, 6, :]).then_inc(s["ka"], 1)
                nl = 0
                for i in range(NUN + 2):
                    if i >= 2:
                        p, j, b, e = units[i - 2]
                        c0, k = skip(j, b), i % 2
                        eng.wait_ge(s["arg"], i - 1)
                        if i >= 4:
                            eng.wait_ge(s["pv"], i - 3)
                        nc.scalar.activation(at[:, k, c0:512], at[:, k, c0:512], ACT.Exp).then_inc(s["at"], 1)
                    if i < NUN:
                        p, j, b, e = units[i]
                        c0, k = skip(j, b), i % 2
                        eng.wait_ge(s["x"], i + 1)
                        if i >= 2:
                            eng.wait_ge(s["sp"], i - 1)
                        for func, kw in ((ACT.Abs, {}), (ACT.Exp, {"scale": -1.0}), (ACT.Ln, {"bias": 1.0})):
                            src = x[:, i % 3, c0:512] if func == ACT.Abs else l[:, k, c0:512]
                            nl += 1
                            nc.scalar.activation(l[:, k, c0:512], src, func, **kw).then_inc(s["l"], 1)
                            eng.wait_ge(s["l"], nl)

            @block.vector
            def _(eng):
                V_.memset(zero[:, :], 0.0).then_inc(s["c"], 1)
                for j in range(1, NT + 1, 2):
                    eng.wait_ge(s["kt"], j + 1)
                    V_.tensor_copy(g.kvt[:, j, :], g.ps[:, 7, :]).then_inc(s["kv"], 1)
                eng.wait_ge(s["c"], 17)
                for i in range(NUN + 3):
                    if i >= 3:
                        p, j, b, e = units[i - 3]
                        c0, k = skip(j, b), (i - 3) % 2
                        eng.wait_ge(s["at"], i - 2)
                        if diag(j, b):
                            V_.copy_predicated(at[:, k, c0:c0 + P], later[:, :], zero[:, :]).then_inc(s["am"], 1)
                    if 2 <= i < NUN + 2:
                        p, j, b, e = units[i - 2]
                        c0, k = skip(j, b), (i - 2) % 2
                        eng.wait_ge(s["tri"], i - 1)
                        if i >= 4:
                            eng.wait_ge(s["pv"], i - 3)
                        V_.tensor_tensor(at[:, k, c0:512], x[:, (i - 2) % 3, c0:512], g.ps[:, 2 + e, c0:512],
                                         ALU.subtract).then_inc(s["arg"], 1)
                    if 1 <= i < NUN + 1:
                        p, j, b, e = units[i - 1]
                        c0, k = skip(j, b), (i - 1) % 2
                        eng.wait_ge(s["l"], 3 * i)
                        eng.wait_ge(s["x"], i)
                        if i >= 3:
                            eng.wait_ge(s["ch"], i - 2)
                        ins = V_.scalar_tensor_tensor(out=sp[:, k, c0:512], in0=x[:, (i - 1) % 3, c0:512], scalar=0.0,
                                                      in1=l[:, k, c0:512], op0=ALU.max, op1=ALU.add)
                        if diag(j, b):
                            ins.then_inc(s["raw"], 1)
                            eng.wait_ge(s["raw"], masked(i - 1))
                            ins = V_.copy_predicated(sp[:, k, c0:c0 + P], later[:, :], zero[:, :])
                        ins.then_inc(s["sp"], 1)
                    if i < NUN:
                        p, j, b, e = units[i]
                        c0 = skip(j, b)
                        eng.wait_ge(s["z"], i + 1)
                        if i >= 3:
                            eng.wait_ge(s["arg"], i - 2)
                        V_.tensor_scalar(x[:, i % 3, c0:512], g.ps[:, i % 2, c0:512], HD ** -0.5,
                                         g.sbb[:, 2 * p + e:2 * p + e + 1], ALU.mult, ALU.add).then_inc(s["x"], 1)
                    if i >= 3:
                        p, j, b, e = units[i - 3]
                        if b == 0:
                            eng.wait_ge(s["pv"], i - 2)
                            rows = slice(HD * e, HD * e + HD)
                            V_.tensor_copy(g.ob[rows, p, 512 * j:512 * (j + 1)], g.ps[rows, 4 + e, :]).then_inc(s["ob"], 1)


def b_sample(g):
    nc, a, V_ = g.nc, g.a, g.nc.vector
    NG, GB = 2, NB // 2
    HQ = SBH * NQ
    UP = 4
    NC, CW = NPAGE // UP, UP * P
    NK = PAST + TS
    with ExitStack() as ctx:
        sb = lambda name, shape, dt=F32: ctx.enter_context(nc.sbuf_tensor(f"bs_{name}", shape, dt))
        kp, vp = sb("kp", [P, GB, UP, 256]), sb("vp", [P, GB, UP, 256])
        kT = sb("kT", [P, 2, 2, CW])
        pt = sb("pt", [1, NB * NPAGE], I32)
        qz = sb("qz", [P, 2, NB, HQ])
        x, l = sb("x", [P, NG, NK]), sb("l", [P, NG, NK])
        aT = sb("aT", [P, 2, CW])
        o = sb("o", [P, NG, 256])
        hide = sb("hide", [P, NG, TS], I32)
        hot = sb("hot", [P, SBH])
        bias = sb("bias", [P, 1])
        zero = sb("zero", [P, TS])
        s_k = [g.sem(f"bs_k{i}") for i in range(GB)]
        s_v = [g.sem(f"bs_v{i}") for i in range(GB)]
        s_vp = [g.sem(f"bs_vp{i}") for i in range(GB)]
        names = ("c", "pt", "init", "bias", "q", "tp", "kt", "zn", "z", "x", "l", "sp", "hid", "scan", "arg", "exp",
                 "am", "at", "ac", "pv", "ot", "o", "ob", "act", "pe", "dve", "pool", "sync")
        s = {n: g.sem(f"bs_{n}") for n in names}

        SYNC_KEYS, ACT_KEYS = ((0, 1, 2), (0, 1), (0, 1), (0, 1)), ((3,), (2, 3), (2, 3), (2, 3))
        SYNC_VALUES, ACT_VALUES, POOL_VALUES = ((0, 1), (0,), (0, 1), (0,)), ((2,), (1, 2), (2,), (1, 2)), ((3,),) * 4

        def load_unit(eng, grp, c, i, dst, cache, sem, pages):
            for k in pages:
                page = eng.value_load(pt[0:1, bass.ds(((GB * grp + i) * NPAGE + k) + c * UP, 1)], min_val=0,
                                      max_val=a[cache].shape[1] - 1)
                eng.dma_start(dst[:, i, k, :], a[cache][0, bass.ds(page, 1)].rearrange(
                    "a t h d -> (a t) (h d)")).then_inc(sem[i], 16)

        def load_keys(eng, tick, grp, c, pages):
            for i in range(GB):
                if not (grp == 0 and isinstance(c, int) and c == 0):
                    wait_apart(eng, s["tp"], GB * (NC * grp + c - 1) + i + 1, s[tick])
                load_unit(eng, grp, c, i, kp, "cache_sb_k", s_k, pages[i])

        def load_values(eng, tick, grp, c, pages):
            for i in range(GB):
                if not (grp == 0 and isinstance(c, int) and c == 0):
                    wait_apart(eng, s["pv"], GB * ((NC + 1) * grp + c - 1) + i + 1, s[tick])
                load_unit(eng, grp, c, i, vp, "cache_sb_v", s_vp if tick == "pool" else s_v, pages[i])

        def chunks(eng, body):
            body(0, 0)
            with eng.Fori(1, NC) as c:
                body(0, c)
            with eng.Fori(0, NC) as c:
                body(1, c)

        with nc.Block() as block:
            @block.sync
            def _(eng):
                eng.dma_start(pt[:, :], a["page_table"].rearrange("b n -> (b n)").rearrange("(a n) -> a n", a=1)).then_inc(s["pt"], 16)
                eng.dma_start(hide[:, :, :], a["c_new"]).then_inc(s["c"], 16)
                eng.dma_start(hot[:, :], a["c_hot"]).then_inc(s["c"], 16)
                eng.wait_ge(s["pt"], 16)
                chunks(eng, lambda grp, c: load_keys(eng, "sync", grp, c, SYNC_KEYS))
                chunks(eng, lambda grp, c: load_values(eng, "sync", grp, c, SYNC_VALUES))

            @block.gpsimd
            def _(eng):
                eng.memset(qz[:, :, :, :], 0.0).then_inc(s["init"], 1)
                eng.memset(zero[:, :], 0.0).then_inc(s["init"], 1)
                eng.wait_ge(s["pt"], 16)
                chunks(eng, lambda grp, c: load_values(eng, "pool", grp, c, POOL_VALUES))

            @block.tensor
            def _(eng):
                eng.wait_ge(s["q"], 4)
                for b in range(NB):
                    grp, i = b // GB, b % GB
                    for p in range(2):
                        mm = nc.tensor.matmul(g.ps[HQ * i:HQ * i + HQ, 5, grp * TS:(grp + 1) * TS], qz[:, p, b, :],
                                              g.qb[:, 2 + p, SEQ:T], start=(p == 0), stop=(p == 1))
                mm.then_inc(s["zn"], 1)

                def turn(grp, c, i, new):
                    n = GB * (NC * grp + c) + i
                    wait_apart(eng, s_k[i], 16 * UP * (NC * grp + c + 1), s["pe"])
                    if not (new and i < 2):
                        wait_apart(eng, s["kt"], n - 1, s["pe"])
                    for p in range(2):
                        for k in range(UP):
                            mm = nc.tensor.transpose(g.ps[:, 2 * (i % 2) + p, k * P:(k + 1) * P],
                                                     kp[:, i, k, p * P:(p + 1) * P], g.ident)
                    mm.then_inc(s["tp"], 1)

                def score(grp, c, i, new):
                    wait_apart(eng, s["kt"], GB * (NC * grp + c) + i + 1, s["pe"])
                    if i == 0 and not new:
                        wait_apart(eng, s["x"], NC * grp + c + 1, s["pe"])
                    for p in range(2):
                        mm = nc.tensor.matmul(g.ps[HQ * i:HQ * i + HQ, 4, :], qz[:, p, GB * grp + i, :],
                                              kT[:, i % 2, p, :], start=(p == 0), stop=(p == 1))
                    mm.then_inc(s["z"], 1)

                def body(grp, c, leads):
                    new = grp == 0 and leads
                    for i in range(GB):
                        turn(grp, c, i, new)
                        if i:
                            score(grp, c, i - 1, new)
                        elif not leads:
                            score(grp, c - 1, GB - 1, False)
                for grp in range(NG):
                    body(grp, 0, True)
                    with eng.Fori(1, NC) as c:
                        body(grp, c, False)
                    score(grp, NC - 1, GB - 1, False)

                for grp in range(NG):
                    eng.wait_ge(s["am"], grp + 1)
                    for c in range(NC + 2):
                        if c <= NC:
                            n = c + (NC + 1) * grp
                            if n >= 2:
                                eng.wait_ge(s["ac"], n - 1)
                            for k in range(UP if c < NC else 1):
                                w = P if c < NC else TS
                                mm = nc.tensor.transpose(g.ps[0:w, 4 + n % 2, k * P:(k + 1) * P],
                                                         x[:, grp, c * CW + k * P:c * CW + k * P + w], g.ident)
                            mm.then_inc(s["at"], 1)
                        if c >= 1:
                            n = c - 1 + (NC + 1) * grp
                            eng.wait_ge(s["ac"], n + 1)
                            for i in range(GB):
                                if c <= NC:
                                    eng.wait_ge(s_v[i], 16 * (UP - 1) * (NC * grp + c))
                                    eng.wait_ge(s_vp[i], 16 * (NC * grp + c))
                                for k in range(UP if c <= NC else 1):
                                    rows = P if c <= NC else TS
                                    rhs = vp[:, i, k, :] if c <= NC else g.kvt[0:TS, SEQ // P, 256:512]
                                    mm = nc.tensor.matmul(g.ps[HQ * i:HQ * i + HQ, 6 + grp, 0:256],
                                                          aT[0:rows, n % 2, k * P + HQ * i:k * P + HQ * i + HQ], rhs,
                                                          start=(c == 1 and k == 0), stop=(c == NC + 1),
                                                          skip_group_check=True)
                                mm.then_inc(s["pv"], 1)
                    eng.wait_ge(s["ot"], grp + 1)
                    for p in range(2):
                        mm = nc.tensor.transpose(g.ps[:, 2 * grp + p, 0:P], o[:, grp, p * P:(p + 1) * P], g.ident)
                    mm.then_inc(s["o"], 1)

            @block.scalar
            def _(eng):
                nc.scalar.preload_act_table_set("natural_log_exp_and_others")
                eng.wait_ge(s["pt"], 16)

                def soft(grps, c0, n, k):
                    wait_apart(eng, s["x"], k + 1, s["act"])
                    cols = lambda t: t[:, grps, bass.ds(c0, n)]
                    for i, (func, kw) in enumerate(((ACT.Abs, {}), (ACT.Exp, {"scale": -1.0}), (ACT.Ln, {"bias": 1.0}))):
                        nc.scalar.activation(cols(l), cols(x if i == 0 else l), func, **kw).then_inc(s["l"], 1)
                        wait_apart(eng, s["l"], 3 * k + i + 1, s["act"])

                def soft_chunk(grp, c):
                    soft(slice(grp, grp + 1), c * CW, CW, NC * grp + c + 1)

                def attend(grp):
                    eng.wait_ge(s["arg"], grp + 1)
                    nc.scalar.activation(x[:, grp, :], x[:, grp, :], ACT.Exp).then_inc(s["exp"], 1)
                load_keys(eng, "act", 0, 0, ACT_KEYS)
                soft(slice(0, NG), PAST, TS, 0)
                with eng.Fori(1, NC) as c:
                    load_keys(eng, "act", 0, c, ACT_KEYS)
                    soft_chunk(0, c - 1)
                load_keys(eng, "act", 1, 0, ACT_KEYS)
                soft_chunk(0, NC - 1)
                with eng.Fori(1, NC) as c:
                    load_keys(eng, "act", 1, c, ACT_KEYS)
                    soft_chunk(1, c - 1)
                load_values(eng, "act", 0, 0, ACT_VALUES)
                attend(0)
                soft_chunk(1, NC - 1)
                with eng.Fori(1, 3) as c:
                    load_values(eng, "act", 0, c, ACT_VALUES)
                attend(1)
                with eng.Fori(3, NC) as c:
                    load_values(eng, "act", 0, c, ACT_VALUES)
                with eng.Fori(0, NC) as c:
                    load_values(eng, "act", 1, c, ACT_VALUES)

            @block.vector
            def _(eng):
                eng.wait_ge(s["init"], 2)
                for p in range(2):
                    for e in range(2):
                        rows, h = slice(HD * e, HD * e + HD), 2 * p + e
                        V_.tensor_copy(qz[rows, p, :, NQ * h:NQ * h + NQ],
                                       g.qb[rows, p, SEQ:T].rearrange("r (b q) -> r b q", q=NQ)).then_inc(s["q"], 1)
                eng.wait_ge(s["c"], 32)
                V_.tensor_tensor(hot[:, :], hot[:, :], g.sbb[:, :], ALU.mult).then_inc(s["bias"], 1)
                eng.wait_ge(s["bias"], 1)
                V_.reduce_sum(bias[:, :], hot[:, :], axis=AX.X).then_inc(s["bias"], 1)
                eng.wait_ge(s["bias"], 2)

                def sp(grps, c0, n, k):
                    wait_apart(eng, s["l"], 3 * k + 3, s["dve"])
                    cols = lambda t: t[:, grps, bass.ds(c0, n)]
                    V_.scalar_tensor_tensor(out=cols(l), in0=cols(x), scalar=0.0, in1=cols(l), op0=ALU.max,
                                            op1=ALU.add).then_inc(s["sp"], 1)

                def sp_chunk(grp, c):
                    wait_apart(eng, s["x"], NC * grp + c + 2, s["dve"])
                    sp(slice(grp, grp + 1), c * CW, CW, NC * grp + c + 1)

                def hide_new(t, grp):
                    return V_.copy_predicated(t[:, grp, PAST:NK], hide[:, grp, :], zero[:, :])

                eng.wait_ge(s["zn"], 1)
                V_.tensor_scalar(x[:, :, PAST:NK], g.ps[:, 5, 0:NG * TS].rearrange("r (g n) -> r g n", n=TS), HD ** -0.5,
                                 bias[:, :], ALU.mult, ALU.add).then_inc(s["x"], 1)

                def scores(grp, c):
                    wait_apart(eng, s["z"], GB * (NC * grp + c + 1), s["dve"])
                    V_.tensor_scalar(x[:, grp, bass.ds(c * CW, CW)], g.ps[:, 4, :], HD ** -0.5, bias[:, :], ALU.mult,
                                     ALU.add).then_inc(s["x"], 1)

                def body(grp, c, leads):
                    for i in range(GB):
                        n = GB * (NC * grp + c) + i
                        wait_apart(eng, s["tp"], n + 1, s["dve"])
                        if not (grp == 0 and leads and i < 2):
                            wait_apart(eng, s["z"], n - 1, s["dve"])
                        V_.tensor_copy(kT[:, i % 2], g.ps[:, 2 * (i % 2):2 * (i % 2) + 2, :]).then_inc(s["kt"], 1)
                        if i == 0 and not leads:
                            scores(grp, c - 1)

                def sums(grp):
                    eng.wait_ge(s["sp"], NC * (grp + 1) + 1)
                    eng.wait_ge(s["hid"], 2)
                    back = l[:, grp, ::-1]
                    V_.tensor_tensor_scan(back, g.cf[:, 1, 0:1].broadcast_to([P, NK]), back, 0.0, ALU.mult,
                                          ALU.add).then_inc(s["scan"], 1)
                    eng.wait_ge(s["scan"], grp + 1)
                    V_.tensor_tensor(x[:, grp, :], x[:, grp, :], l[:, grp, :], ALU.subtract).then_inc(s["arg"], 1)

                def hide_attention(grp):
                    eng.wait_ge(s["exp"], grp + 1)
                    hide_new(x, grp).then_inc(s["am"], 1)
                body(0, 0, True)
                sp(slice(0, NG), PAST, TS, 0)
                eng.wait_ge(s["sp"], 1)
                for grp in range(NG):
                    hide_new(l, grp).then_inc(s["hid"], 1)
                with eng.Fori(1, NC) as c:
                    body(0, c, False)
                    sp_chunk(0, c - 1)
                scores(0, NC - 1)
                body(1, 0, True)
                sp_chunk(0, NC - 1)
                sums(0)
                with eng.Fori(1, NC) as c:
                    body(1, c, False)
                    sp_chunk(1, c - 1)
                scores(1, NC - 1)
                hide_attention(0)
                sp_chunk(1, NC - 1)
                sums(1)
                for grp in range(NG):
                    for c in range(NC + 1):
                        n = c + (NC + 1) * grp
                        w, rows = (CW, P) if c < NC else (P, TS)
                        if n == 5:
                            hide_attention(1)
                        eng.wait_ge(s["at"], n + 1)
                        if n >= 2:
                            eng.wait_ge(s["pv"], GB * (n - 1))
                        V_.tensor_copy(aT[0:rows, n % 2, 0:w], g.ps[0:rows, 4 + n % 2, 0:w]).then_inc(s["ac"], 1)
                    eng.wait_ge(s["pv"], GB * (NC + 1) * (grp + 1))
                    V_.tensor_copy(o[:, grp, :], g.ps[:, 6 + grp, 0:256]).then_inc(s["ot"], 1)
                    eng.wait_ge(s["o"], grp + 1)
                    for p in range(2):
                        for e in range(2):
                            rows, h = slice(HD * e, HD * e + HD), 2 * p + e
                            t0 = SEQ + grp * GB * NQ
                            V_.tensor_copy(g.ob[rows, p, t0:t0 + GB * NQ].rearrange("r (b q) -> r b q", q=NQ),
                                           g.ps[rows, 2 * grp + p, 0:P].rearrange("r (b h q) -> r b h q", h=SBH, q=NQ)[:, :, h, :]
                                           ).then_inc(s["ob"], 1)


def stage_branch_c(g):
    nc, a = g.nc, g.a
    w_in = a["w_in"][0].rearrange("(k p) f -> p k f", p=P)
    c0 = A_COLS + SB_COLS
    with ExitStack() as ctx:
        g.qc = ctx.enter_context(nc.sbuf_tensor("qc", [P, 9, T], F32))
        g.new = ctx.enter_context(nc.sbuf_tensor("new", [TS, 2, 3, P], F32))
        project(g, "cp", w_in[:, :, c0:c0 + DIL_COLS], 9, g.qc)
        c_prompt(g)
        c_sample(g)


def c_tile(t, gi, m):
    if gi == 0:
        return t[:, m * P:(m + 1) * P]
    if gi == 1:
        return t[:, 512 * (m % 2) + m // 2:512 * (m % 2 + 1):4]
    return t[:, m:SEQ:8]


def c_prompt(g):
    nc, a, V_, qc = g.nc, g.a, g.nc.vector, g.qc
    with ExitStack() as ctx:
        sb = lambda name, shape, dt=F32: ctx.enter_context(nc.sbuf_tensor(name, shape, dt))
        vt = sb("cq_vt", [P, 3, 8, P])
        kt = sb("cq_kt", [P, 13, P])
        bias = sb("cq_bias", [P, 3, 2, 256])
        sc = sb("cq_sc", [P, 2, 2, 256])
        pT = sb("cq_pT", [P, 2, 512])
        dg = sb("cq_dg", [P, 2, 2, P])
        mx, nm = sb("cq_mx", [P, 2, 2]), sb("cq_nm", [P, 2, 2])
        res = sb("cq_res", [P, 3, 3, SEQ])
        kts = [(0, 7)] + [(1, m) for m in (1, 3, 5, 7)] + [(2, m) for m in range(8)]
        tr = [(6, gi, m, vt[:, gi, m, :]) for gi in range(3) for m in range(8)] + \
             [(3, gi, m, kt[:, i, :]) for i, (gi, m) in enumerate(kts)]
        names = ("c", "tr", "te", "nt", "ne", "s", "sc", "mx", "nm", "dg", "ex", "t", "pt", "o", "oe", "st", "mxb", "ch", "e2")
        s = {n: g.sem(f"cq_{n}") for n in names}
        units = [(gi, m) for gi in range(3) for m in range(8)]
        alone = lambda gi, m: gi == 2 or (gi == 0 and m == 0) or (gi == 1 and m % 2 == 0)
        NUN = len(units)
        NTR = (len(tr) + 3) // 4
        with nc.Block() as block:
            @block.sync
            def _(eng):
                eng.dma_start(bias[:, :, :, :], a["c_bias"]).then_inc(s["c"], 16)
                n = [0]

                def store(dst, src):
                    eng.dma_start(dst, src).then_inc(s["st"], 16)
                    n[0] += 1
                eng.wait_ge(s["te"], NTR)
                eng.wait_ge(s["ne"], 2)
                for kv in range(2):
                    src = lambda i, gi, m: (vt[:, gi, m, :] if kv else kt[:, i, :])
                    for i, (gi, m) in enumerate(kts):
                        w = g.o[f"win{gi}_prompt"][0, 0, :, kv].rearrange("t h d -> t (h d)")
                        if gi == 0:
                            store(w, src(i, gi, m))
                        elif gi == 1:
                            store(w.rearrange("(i s) n -> s i n", s=4)[m // 2], src(i, gi, m))
                        else:
                            store(w.rearrange("(i s) n -> s i n", s=8)[m], src(i, gi, m))
                    for gi in range(3):
                        W = 128 * DILS[gi]
                        for b in range(NB):
                            store(g.o[f"win{gi}_sample"][0, b, W - NQ:W, kv].rearrange("t h d -> t (h d)"),
                                  g.new[NQ * b:NQ * b + NQ, kv, gi, :])
                eng.wait_ge(s["st"], 16 * n[0])

            @block.tensor
            def _(eng):
                for kv in range(2):
                    for gi in range(3):
                        mm = nc.tensor.transpose(g.ps[0:TS, 6 + kv, gi * P:(gi + 1) * P],
                                                 qc[:, 3 + 3 * kv + gi, SEQ:T], g.ident)
                    mm.then_inc(s["nt"], 1)
                for f in range(NTR):
                    if f >= 2:
                        eng.wait_ge(s["te"], f - 1)
                    for q, (base, gi, m, _) in enumerate(tr[4 * f:4 * f + 4]):
                        mm = nc.tensor.transpose(g.ps[:, 4 + f % 2, q * P:(q + 1) * P], c_tile(qc[:, base + gi, :], gi, m), g.ident)
                    mm.then_inc(s["tr"], 1)
                eng.wait_ge(s["te"], NTR)
                eng.wait_ge(s["ne"], 2)
                for i in range(NUN + 2):
                    if i < NUN:
                        gi, m = units[i]
                        if i >= 2:
                            eng.wait_ge(s["sc"], i - 1)
                        for e in range(2):
                            rows = slice(HD * e, HD * e + HD)
                            for blk in ((1,) if alone(gi, m) else (0, 1)):
                                mm = nc.tensor.matmul(g.ps[:, 2 * (i % 2) + e, blk * P:(blk + 1) * P],
                                                      c_tile(qc[rows, gi, :], gi, m), c_tile(qc[rows, 3 + gi, :], gi, m + blk - 1),
                                                      start=True, stop=True)
                        mm.then_inc(s["s"], 1)
                    if 1 <= i < NUN + 1:
                        gi, m = units[i - 1]
                        eng.wait_ge(s["ex"], 2 * i)
                        if i >= 3:
                            eng.wait_ge(s["pt"], i - 2)
                        for e in range(2):
                            for blk in ((1,) if alone(gi, m) else (0, 1)):
                                mm = nc.tensor.transpose(g.ps[:, 4 + (i - 1) % 2, (2 * e + blk) * P:(2 * e + blk + 1) * P],
                                                         sc[:, (i - 1) % 2, e, blk * P:(blk + 1) * P], g.ident)
                        mm.then_inc(s["t"], 1)
                    if i >= 2:
                        gi, m = units[i - 2]
                        k = i % 2
                        eng.wait_ge(s["pt"], i - 1)
                        eng.wait_ge(s["dg"], 2 * (i - 1))
                        if i >= 4:
                            eng.wait_ge(s["oe"], 3 * (i - 3))
                        for e in range(2):
                            rows = slice(HD * e, HD * e + HD)
                            bl = (1,) if alone(gi, m) else (0, 1)
                            for what in range(2):
                                for blk in bl:
                                    lhs = g.ones[:, 0:HD] if what else vt[:, gi, m + blk - 1, HD * e:HD * e + HD]
                                    nc.tensor.matmul(g.ps[rows, 6 + k, what * P:(what + 1) * P], lhs,
                                                     pT[:, k, (2 * e + blk) * P:(2 * e + blk + 1) * P],
                                                     start=(blk == bl[0]), stop=(blk == 1))
                            mm = nc.tensor.matmul(g.ps[rows, 6 + k, 2 * P:3 * P], g.ones[:, 0:HD], dg[:, k, e, :],
                                                  start=True, stop=True)
                        mm.then_inc(s["o"], 1)

            @block.scalar
            def _(eng):
                for i in range(NUN + 2):
                    if i < NUN:
                        gi, m = units[i]
                        c0 = P if alone(gi, m) else 0
                        eng.wait_ge(s["nm"], i + 1)
                        for e in range(2):
                            nc.scalar.activation(sc[:, i % 2, e, c0:256], sc[:, i % 2, e, c0:256], ACT.Exp,
                                                 bias=nm[:, i % 2, e:e + 1]).then_inc(s["ex"], 1)
                    if 1 <= i < NUN + 1:
                        gi, m = units[i - 1]
                        eng.wait_ge(s["t"], i)
                        if i >= 3:
                            eng.wait_ge(s["o"], i - 2)
                        k = (i - 1) % 2
                        if alone(gi, m):
                            nc.scalar.copy(pT[:, k, :].rearrange("p (a b) -> p a b", a=2)[:, :, P:256],
                                           g.ps[:, 4 + k, :].rearrange("p (a b) -> p a b", a=2)[:, :, P:256]).then_inc(s["pt"], 1)
                        else:
                            nc.scalar.copy(pT[:, k, :], g.ps[:, 4 + k, :]).then_inc(s["pt"], 1)
                for gi in range(3):
                    eng.wait_ge(s["mxb"], gi + 1)
                    nc.scalar.activation(res[:, gi, 2, :], res[:, gi, 2, :], ACT.Exp).then_inc(s["e2"], 1)

            @block.vector
            def _(eng):
                for kv in range(2):
                    eng.wait_ge(s["nt"], kv + 1)
                    V_.tensor_copy(g.new[:, kv].rearrange("t g n -> t (g n)"), g.ps[0:TS, 6 + kv, 0:3 * P]).then_inc(s["ne"], 1)
                for f in range(NTR):
                    eng.wait_ge(s["tr"], f + 1)
                    q = len(tr[4 * f:4 * f + 4])
                    dst = vt[:, f // 2, 4 * (f % 2):4 * (f % 2) + 4, :] if f < 6 else kt[:, 4 * (f - 6):4 * (f - 6) + q, :]
                    V_.tensor_copy(dst.rearrange("p a b -> p (a b)"), g.ps[:, 4 + f % 2, 0:q * P]).then_inc(s["te"], 1)
                eng.wait_ge(s["c"], 16)
                for i in range(NUN + 2):
                    if i < NUN:
                        gi, m = units[i]
                        c0, k = (P if alone(gi, m) else 0), i % 2
                        eng.wait_ge(s["s"], i + 1)
                        if i >= 2:
                            eng.wait_ge(s["t"], i - 1)
                        V_.scalar_tensor_tensor(out=sc[:, k, :, c0:256], in0=g.ps[:, 2 * k:2 * k + 2, c0:256], scalar=HD ** -0.5,
                                                in1=bias[:, gi, :, c0:256], op0=ALU.mult, op1=ALU.add).then_inc(s["sc"], 1)
                        eng.wait_ge(s["sc"], i + 1)
                        if i >= 2:
                            eng.wait_ge(s["ex"], 2 * (i - 1))
                            eng.wait_ge(s["dg"], 2 * (i - 1))
                        V_.tensor_reduce(mx[:, k, :], sc[:, k, :, c0:256], AX.X, ALU.max).then_inc(s["mx"], 1)
                        eng.wait_ge(s["mx"], i + 1)
                        V_.tensor_scalar(nm[:, k, :], mx[:, k, :], -1.0, None, ALU.mult).then_inc(s["nm"], 1)
                    if i >= 2:
                        gi, m = units[i - 2]
                        k = i % 2
                        eng.wait_ge(s["o"], i - 1)
                        for w in range(3):
                            src = g.ps[:, 6 + k, w * P:(w + 1) * P]
                            V_.tensor_copy(c_tile(res[:, gi, w, :], gi, m), src).then_inc(s["oe"], 1)
                    if i < NUN:
                        for e in range(2):
                            V_.tensor_scalar(dg[:, i % 2, e, :], g.ident, mx[:, i % 2, e:e + 1], None,
                                             ALU.mult).then_inc(s["dg"], 1)
                eng.wait_ge(s["oe"], 3 * NUN)
                n_ch = [0]

                def link(ins):
                    n_ch[0] += 1
                    ins.then_inc(s["ch"], 1)
                    eng.wait_ge(s["ch"], n_ch[0])
                top = sc[:, :, :, :].rearrange("p a e n -> p (a e n)")
                link(V_.tensor_tensor(top, res[:, 0, 2, :], res[:, 1, 2, :], ALU.max))
                link(V_.tensor_tensor(top, top, res[:, 2, 2, :], ALU.max))
                for gi in range(3):
                    V_.tensor_tensor(res[:, gi, 2, :], res[:, gi, 2, :], top, ALU.subtract).then_inc(s["mxb"], 1)
                for gi in range(3):
                    eng.wait_ge(s["e2"], gi + 1)
                    V_.tensor_tensor(res[:, gi, 0, :], res[:, gi, 0, :], res[:, gi, 2, :], ALU.mult)
                    link(V_.tensor_tensor(res[:, gi, 1, :], res[:, gi, 1, :], res[:, gi, 2, :], ALU.mult))
                for w in range(2):
                    link(V_.tensor_tensor(res[:, 0, w, :], res[:, 0, w, :], res[:, 1, w, :], ALU.add))
                    link(V_.tensor_tensor(res[:, 0, w, :], res[:, 0, w, :], res[:, 2, w, :], ALU.add))
                link(V_.reciprocal(top, res[:, 0, 1, :]))
                V_.tensor_tensor(g.oc[:, 0:SEQ], res[:, 0, 0, :], top, ALU.mult).then_inc(s["ch"], 1)


def c_sample(g):
    nc, a, V_, qc = g.nc, g.a, g.nc.vector, g.qc
    CLS = [(gi, r) for gi in range(3) for r in range((1, 4, 8)[gi])]
    NC = len(CLS)
    S0 = 192
    with ExitStack() as ctx:
        sb = lambda name, shape, dt=F32: ctx.enter_context(nc.sbuf_tensor(name, shape, dt))
        win = sb("cs_win", [P, NB, NC, 2 * P])
        qm = sb("cs_qm", [P, NC, NB, 32])
        qf = sb("cs_qf", [P, 3, NB, 2, NQ])
        kT = sb("cs_kT", [P, NC, P])
        bias = sb("cs_bias", [P, 3, S0])
        sc = sb("cs_sc", [P, 3, S0])
        st = sb("cs_st", [P, 4])
        pT = sb("cs_pT", [P, 3, P])
        pn = sb("cs_pn", [TS, 3, P])
        names = ("c", "z", "q", "tp", "te", "s", "sn", "sc", "mx", "nm", "ex", "iv", "pr", "t", "pt", "o")
        s = {n: g.sem(f"cs_{n}") for n in names}
        s_w = [g.sem(f"cs_w{b}") for b in range(NB)]
        with nc.Block() as block:
            @block.sync
            def _(eng):
                for b in range(NB):
                    eng.dma_start(win[:, b, 0, :], a["cache_win0"][0, b].rearrange("t a h d -> t (a h d)")).then_inc(s_w[b], 16)
                    eng.dma_start(win[:, b, 1:5, :].rearrange("p r n -> p (r n)"),
                                  a["cache_win1"][0, b].rearrange("(i r) a h d -> i (r a h d)", r=4)).then_inc(s_w[b], 16)
                    eng.dma_start(win[:, b, 5:13, :].rearrange("p r n -> p (r n)"),
                                  a["cache_win2"][0, b].rearrange("(i r) a h d -> i (r a h d)", r=16)[:, 0:8 * 256]).then_inc(s_w[b], 16)
                eng.dma_start(bias[:, :, :], a["c_sbias"]).then_inc(s["c"], 16)

            @block.gpsimd
            def _(eng):
                eng.memset(qm[:, :, :, :], 0.0).then_inc(s["z"], 1)
                eng.memset(qf[:, :, :, :, :], 0.0).then_inc(s["z"], 1)

            @block.tensor
            def _(eng):
                eng.wait_ge(s["q"], 2)
                for b in range(NB + 1):
                    for f in range(4):
                        classes = list(enumerate(CLS))[4 * f:4 * f + 4]
                        if b < NB:
                            if f == 0:
                                eng.wait_ge(s_w[b], 48)
                            if b:
                                eng.wait_ge(s["te"], 4 * (b - 1) + f + 1)
                            for i, _ in classes:
                                mm = nc.tensor.transpose(g.ps[:, 3 + f, (i - 4 * f) * P:(i - 4 * f + 1) * P],
                                                         win[:, b, i, 0:P], g.ident)
                            mm.then_inc(s["tp"], 1)
                        if b > 0:
                            c = b - 1
                            rows = slice(32 * (c // 2), 32 * (c // 2) + 32)
                            eng.wait_ge(s["te"], 4 * c + f + 1)
                            for i, (gi, r) in classes:
                                mm = nc.tensor.matmul(g.ps[rows, gi, 0:P], qm[:, i, c, :], kT[:, i, :],
                                                      start=(r == 0 and c % 2 == 0),
                                                      stop=(c % 2 == 1 and (i == NC - 1 or CLS[i + 1][0] != gi)),
                                                      skip_group_check=True)
                            mm.then_inc(s["s"], 1)
                for gi in range(3):
                    mm = nc.tensor.matmul(g.ps[:, gi, P:S0], qf[:, gi].rearrange("p b e q -> p (b e q)"), qc[:, 3 + gi, SEQ:T],
                                          start=True, stop=True, skip_group_check=True)
                mm.then_inc(s["sn"], 1)
                eng.wait_ge(s["pr"], 1)
                for gi in range(3):
                    nc.tensor.transpose(g.ps[:, 3, gi * P:(gi + 1) * P], sc[:, gi, 0:P], g.ident)
                    mm = nc.tensor.transpose(g.ps[0:TS, 4, gi * P:(gi + 1) * P], sc[:, gi, P:S0], g.ident)
                mm.then_inc(s["t"], 1)
                eng.wait_ge(s["pt"], 2)
                out = g.ps[:, 5, 0:P]
                for gi in range(3):
                    nc.tensor.matmul(out, g.new[:, 1, gi, :], pn[:, gi, :], start=(gi == 0), stop=False, skip_group_check=True)
                for b in range(NB):
                    for i, (gi, r) in enumerate(CLS):
                        step = (1, 4, 8)[gi]
                        cols = lambda t: t.rearrange("p (x q) -> p x q", q=NQ)[:, 2 * b:2 * b + 2, r:NQ:step]
                        mm = nc.tensor.matmul(cols(out), win[:, b, i, P:2 * P], cols(pT[:, gi, :]), start=False,
                                              stop=(b == NB - 1 and i == NC - 1), skip_group_check=True)
                mm.then_inc(s["o"], 1)

            @block.scalar
            def _(eng):
                for b in range(NB):
                    for f in range(4):
                        n = min(4 * f + 4, NC) - 4 * f
                        eng.wait_ge(s["tp"], 4 * b + f + 1)
                        if b:
                            eng.wait_ge(s["s"], 4 * (b - 1) + f + 1)
                        nc.scalar.copy(kT[:, 4 * f:4 * f + n, :].rearrange("p a n -> p (a n)"),
                                       g.ps[:, 3 + f, 0:n * P]).then_inc(s["te"], 1)
                eng.wait_ge(s["nm"], 1)
                nc.scalar.activation(sc[:, :, :], sc[:, :, :], ACT.Exp, bias=st[:, 1:2]).then_inc(s["ex"], 1)

            @block.vector
            def _(eng):
                eng.wait_ge(s["z"], 2)
                for e in range(2):
                    rows = slice(HD * e, HD * e + HD)
                    for gi in range(3):
                        qv = qc[rows, gi, SEQ:T].rearrange("p (b q) -> p b q", q=NQ)
                        ins = V_.tensor_copy(qf[rows, gi, :, e, :], qv)
                    for i, (gi, r) in enumerate(CLS):
                        step = (1, 4, 8)[gi]
                        for par in range(2):
                            qv = qc[rows, gi, SEQ:T].rearrange("p (b q) -> p b q", q=NQ)[:, par:NB:2, r:NQ:step]
                            ins = V_.tensor_copy(qm[rows, i, par:NB:2, 16 * par + 8 * e + r:16 * par + 8 * e + NQ:step], qv)
                    ins.then_inc(s["q"], 1)
                eng.wait_ge(s["c"], 16)
                eng.wait_ge(s["sn"], 1)
                V_.scalar_tensor_tensor(out=sc[:, :, :], in0=g.ps[:, 0:3, 0:S0], scalar=HD ** -0.5, in1=bias[:, :, :],
                                        op0=ALU.mult, op1=ALU.add).then_inc(s["sc"], 1)
                eng.wait_ge(s["sc"], 1)
                V_.tensor_reduce(st[:, 0:1], sc[:, :, :], AX.XY, ALU.max).then_inc(s["mx"], 1)
                eng.wait_ge(s["mx"], 1)
                V_.tensor_scalar(st[:, 1:2], st[:, 0:1], -1.0, None, ALU.mult).then_inc(s["nm"], 1)
                eng.wait_ge(s["ex"], 1)
                V_.tensor_reduce(st[:, 2:3], sc[:, :, :], AX.XY, ALU.add).then_inc(s["iv"], 1)
                eng.wait_ge(s["iv"], 1)
                V_.reciprocal(st[:, 3:4], st[:, 2:3]).then_inc(s["iv"], 1)
                eng.wait_ge(s["iv"], 2)
                V_.tensor_scalar(sc[:, :, :], sc[:, :, :], st[:, 3:4], None, ALU.mult).then_inc(s["pr"], 1)
                eng.wait_ge(s["t"], 1)
                V_.tensor_copy(pT[:, :, :].rearrange("p g n -> p (g n)"), g.ps[:, 3, 0:3 * P]).then_inc(s["pt"], 1)
                V_.tensor_copy(pn[:, :, :].rearrange("p g n -> p (g n)"), g.ps[0:TS, 4, 0:3 * P]).then_inc(s["pt"], 1)
                eng.wait_ge(s["o"], 1)
                for e in range(2):
                    rows = slice(HD * e, HD * e + HD)
                    V_.tensor_copy(g.oc[rows, SEQ:T].rearrange("p (b q) -> p b q", q=NQ),
                                   g.ps[rows, 5, 0:P].rearrange("p (b e q) -> p b e q", e=2, q=NQ)[:, :, e, :])


GATE0 = A_COLS + SB_COLS + DIL_COLS
EXT = 2 + SEQ + NB * (NQ + 2)


PART = 6
CR = 2 + 2 * NB


def stage_merge(g, mh, ml):
    nc, a, V_ = g.nc, g.a, g.nc.vector
    w_in = a["w_in"][0].rearrange("(k p) f -> p k f", p=P)
    wbr = [a[f"w_branch_{x}"][0].rearrange("(k p) f -> p k f", p=P) for x in "abc"]
    with ExitStack() as ctx:
        sb = lambda name, shape, dt=F32: ctx.enter_context(nc.sbuf_tensor(name, shape, dt))
        xh, xl = sb("mx_h", [P, KT, T]), sb("mx_l", [P, KT, T])
        wt = sb("wgt", [P, KT, P])
        wgl, wgh = sb("wgl", [P, 3, KT, P]), sb("wgh", [P, 3, KT, P])
        wb = sb("wb", [P, 6, P])
        acc = sb("mg_acc", [P, T])
        sg = sb("sg", [P, T])
        s = {n: g.sem(f"mg_{n}") for n in ("g", "b", "sg", "m", "add", "mh", "ml", "w", "wh", "ws", "sync", "pool", "vec")}
        s_b = [g.sem(f"mg_b{i}") for i in range(3)]
        s_x = [g.sem(f"mg_x{i}") for i in range(len(CH))]

        def tiles(eng, body):
            body(0, True)
            with eng.Fori(1, KT) as f:
                body(f, False)
        first_tile = (0, 3, 5)
        of = lambda i: slice(first_tile[i], first_tile[i] + 3 - i)
        tile = lambda t, f: t[:, bass.ds(f, 1), :].rearrange("p a t -> p (a t)")
        with nc.Block() as block:
            @block.gpsimd
            def _(eng):
                def weights(f, i):
                    low_weights(eng, wgl[:, i], wt[:, :, :], wgh[:, i], s, 3 * f + i + 1)

                def body(f, last=False):
                    weights(f, 1)
                    weights(f, 2)
                    if not last:
                        weights(f + 1, 0)
                    wait_apart(eng, s["mh"], f + 1, s["pool"])
                    low(eng, tile(ml, f), acc[:, :], tile(mh, f)).then_inc(s["ml"], 1)
                weights(0, 0)
                with eng.Fori(0, KT - 1) as f:
                    body(f)
                body(KT - 1, True)

            @block.sync
            def _(eng):
                def body(f, peeled):
                    for i in range(3):
                        if not peeled or i:
                            wait_apart(eng, s["ws"], 3 * f + i, s["sync"])
                        eng.dma_start(wt[:, :, :], w_in[:, :, bass.ds(GATE0 + i * D + f * P, P)]).then_inc(s["w"], 16)
                        if not peeled:
                            wait_apart(eng, s["b"], 3 * f + i - 2, s["sync"])
                        eng.dma_start(wb[:, of(i)], wbr[i][:, :, bass.ds(f * P, P)]).then_inc(s_b[i], 16)
                tiles(eng, body)

            @block.tensor
            def _(eng):
                def body(f, peeled):
                    for i in range(3):
                        eng.wait_ge(s["ws"], 3 * f + i + 1)
                        if not peeled or i:
                            eng.wait_ge(s["sg"], 3 * f + i)
                        for c, (c0, n) in enumerate(CH):
                            if peeled and i == 0:
                                eng.wait_ge(s_x[c], 32)
                            for k in range(KT):
                                mm = product(nc, g.ps[:, c, 0:n], (wgh[:, i, k, :], wgl[:, i, k, :]),
                                             (xh[:, k, c0:c0 + n], xl[:, k, c0:c0 + n]), k == 0, k == KT - 1)
                        mm.then_inc(s["g"], 1)
                        if not peeled or i:
                            eng.wait_ge(s["m"], 3 * f + i)
                        eng.wait_ge(s_b[i], 16 * f + 16)
                        for c, (c0, n) in enumerate(CH):
                            for k in range(3 - i):
                                o = first_tile[i] + k
                                mm = nc.tensor.matmul(g.ps[:, 3 + c, 0:n], wb[:, o, :], g.branches[:, o, c0:c0 + n],
                                                      start=(k == 0), stop=(k == 2 - i))
                        mm.then_inc(s["b"], 1)
                tiles(eng, body)

            @block.scalar
            def _(eng):
                load_xn(g, eng, xh, xl, s_x)

                def body(f, peeled):
                    for i in range(3):
                        eng.wait_ge(s["g"], 3 * f + i + 1)
                        if i == 1:
                            eng.wait_ge(s["m"], 3 * f + 1)
                        elif i == 2 or not peeled:
                            eng.wait_ge(s["add"], 2 * f + i // 2)
                        for c, (c0, n) in enumerate(CH):
                            ins = nc.scalar.activation(sg[:, c0:c0 + n], g.ps[:, c, 0:n], ACT.Sigmoid)
                        ins.then_inc(s["sg"], 1)
                    eng.wait_ge(s["add"], 2 * f + 2)
                    nc.scalar.copy(tile(mh, f).bitcast(F32R), acc[:, :]).then_inc(s["mh"], 1)
                tiles(eng, body)

            @block.vector
            def _(eng):
                def weights(f, i, peeled):
                    if not peeled:
                        eng.wait_ge(s["g"], 3 * f + i - 2)
                    high_weights(eng, wgh[:, i], wt[:, :, :], s["w"], 16 * (3 * f + i) + 16, s)

                def body(f, peeled, last=False):
                    for i in range(3):
                        if not last or i < 2:
                            weights(f + (i + 1) // 3, (i + 1) % 3, peeled and i < 2)
                        eng.wait_ge(s["sg"], 3 * f + i + 1)
                        eng.wait_ge(s["b"], 3 * f + i + 1)
                        if i == 0 and not peeled:
                            eng.wait_ge(s["ml"], f)
                        for c, (c0, n) in enumerate(CH):
                            dst = (acc if i == 0 else sg)[:, c0:c0 + n]
                            ins = V_.tensor_tensor(dst, sg[:, c0:c0 + n], g.ps[:, 3 + c, 0:n], ALU.mult)
                        ins.then_inc(s["m"], 1)
                        if i:
                            eng.wait_ge(s["m"], 3 * f + i + 1)
                            V_.tensor_tensor(acc[:, :], acc[:, :], sg[:, :], ALU.add).then_inc(s["add"], 1)
                weights(0, 0, True)
                body(0, True)
                with eng.Fori(1, KT - 1) as f:
                    body(f, False)
                body(KT - 1, False, True)


def project_add(g, pre, w, kt, xh, xl, dst, init=None):
    nc = g.nc
    with ExitStack() as ctx:
        wt = ctx.enter_context(nc.sbuf_tensor(f"{pre}_wt", [P, kt, P], F32))
        wl, wh = (ctx.enter_context(nc.sbuf_tensor(f"{pre}_w{x}", [P, 2, kt, P], F32)) for x in "lh")
        s_mm, s_v, s_init = (g.sem(f"{pre}_{n}") for n in ("mm", "v", "init"))
        s = {n: g.sem(f"{pre}_{n}") for n in ("w", "wh", "ws", "sync", "pool", "vec")}
        with nc.Block() as block:
            @block.sync
            def _(eng):
                def body(t, b):
                    if not isinstance(t, int) or t:
                        wait_apart(eng, s["ws"], t, s["sync"])
                    eng.dma_start(wt[:, :, :], w[:, :, bass.ds(t * P, P)]).then_inc(s["w"], 16)
                in_pairs(eng, KT, body)

            if init is not None:
                @block.scalar
                def _(eng):
                    eng.dma_start(dst[:, :, :], init).then_inc(s_init, 16)

            @block.gpsimd
            def _(eng):
                def body(t, b):
                    low_weights(eng, wl[:, b], wt[:, :, :], wh[:, b], s, t + 1)
                in_pairs(eng, KT, body)

            @block.tensor
            def _(eng):
                def body(t, b):
                    eng.wait_ge(s["ws"], t + 1)
                    if not first(t):
                        eng.wait_ge(s_v, t - 1)
                    for c, (c0, n) in enumerate(CH):
                        for k in range(kt):
                            mm = product(nc, g.ps[:, 3 * b + c, 0:n], (wh[:, b, k, :], wl[:, b, k, :]),
                                         (xh[:, k, c0:c0 + n], xl[:, k, c0:c0 + n]), k == 0, k == kt - 1)
                    mm.then_inc(s_mm, 1)
                in_pairs(eng, KT, body)

            @block.vector
            def _(eng):
                def body(t, b):
                    if init is not None and isinstance(t, int) and t == 0:
                        eng.wait_ge(s_init, 16)
                    eng.wait_ge(s_mm, t + 1)
                    for c, (c0, n) in enumerate(CH):
                        d = dst[:, bass.ds(t, 1), c0:c0 + n].rearrange("p a t -> p (a t)")
                        ins = nc.vector.tensor_tensor(d, d, g.ps[:, 3 * b + c, 0:n], ALU.add)
                    ins.then_inc(s_v, 1)
                ahead(eng, KT, lambda t, b: high_pair(eng, t, wh[:, b], wt[:, :, :], s_mm, s), body)


def norm(g, pre, src, gain, dst):
    nc = g.nc
    with ExitStack() as ctx:
        sq = ctx.enter_context(nc.sbuf_tensor(f"{pre}_sqb", [P, 2, T], F32))
        inv = ctx.enter_context(nc.sbuf_tensor(f"{pre}_invb", [P, T], F32))
        n_act, n_pe, n_dve, n_pool, _ = norm_program(g, pre, src, sq, inv, gain, dst, T, CH)
        with nc.Block() as block:
            block.scalar(n_act)
            block.tensor(n_pe)
            block.vector(n_dve)
            if isinstance(dst, tuple):
                block.gpsimd(n_pool)


def stage_ffn(g, xh, xl, x1):
    nc, a, V_ = g.nc, g.a, g.nc.vector
    w_up = a["w_up"][0].rearrange("(k p) f -> p k f", p=P)
    w_down = a["w_down"][0].rearrange("(k p) f -> p k f", p=P)
    S0, E = 2 + SEQ, EXT - 2
    samp = lambda t, o: t[:, S0:EXT].rearrange("p (b q) -> p b q", q=NQ + 2)[:, :, o:o + NQ]
    col = lambda t, half, j: t[:, bass.ds(half * FT + j, 1)]
    columns = ((lambda t, j: t[:, bass.ds(j, 1), 0:SEQ].rearrange("p a t -> p (a t)"), lambda r: r[:, 0:SEQ]),
               (lambda t, j: t[:, bass.ds(j, 1), SEQ:T].rearrange("p a (b q) -> p (a b) q", q=NQ),
                lambda r: samp(r, 0)))
    free = g.branches[:, :, :].rearrange("p a t -> p (a t)")
    work = free[:, 0:5 * EXT].rearrange("p (a e) -> p a e", e=EXT)
    u, cv, sg = work[:, 0:2, :], work[:, 2:4, :], work[:, 4, :]
    co = free[:, 5 * EXT:5 * EXT + UT * CR].rearrange("p (t r) -> p t r", r=CR)
    parts = [(i, j0, min(PART, FT - j0)) for i, j0 in enumerate(range(0, FT, PART))]
    NPT = len(parts)
    up_unit = lambda i, j, h: 2 * j + h + KT * i
    down_unit = lambda i, t: 2 * (parts[i][1] + parts[i][2]) + KT * i + t

    def program(eng, up, down):
        for i, j0, n in parts:
            up(i, j0, False)
            with eng.Fori(j0 + 1, j0 + n - 1) as j:
                up(i, j, False)
            up(i, j0 + n - 1, True)
            for t in range(2):
                down(i, t, t)
            with eng.Fori(1, KT // 2 - 1) as m:
                for h in range(2):
                    down(i, 2 * m + h, h)
            for t in range(KT - 2, KT):
                down(i, t, t % 2)

    def after_up(i, j, h, last, weights):
        if last:
            weights(down_unit(i, h), h, parts[i][2])
        else:
            weights(up_unit(i, j + 1, h), h, KT)

    def after_down(i, t, h, weights):
        if not isinstance(t, int) or t < KT - 2:
            weights(down_unit(i, t + 2), h, parts[i][2])
        elif i + 1 < NPT:
            weights(up_unit(i + 1, parts[i + 1][1], h), h, KT)

    with ExitStack() as ctx:
        sb = lambda name, shape, dt=F32: ctx.enter_context(nc.sbuf_tensor(name, shape, dt))
        ah, al = sb("ah", [P, PART, T]), sb("al", [P, PART, T])
        wt = sb("fu_wt", [P, KT, P])
        wl, wh = sb("fu_wl", [P, 2, KT, P]), sb("fu_wh", [P, 2, KT, P])
        names = ("z", "mm", "ev", "st", "t0", "t1", "cv", "sg", "m", "act", "ah", "al", "co", "v", "w", "wh", "ws",
                 "sync", "pool", "vec")
        s = {n: g.sem(f"fu_{n}") for n in names}
        with nc.Block() as block:
            @block.sync
            def _(eng):
                def load(n, kt, src):
                    if not isinstance(n, int) or n:
                        wait_apart(eng, s["ws"], n, s["sync"])
                    eng.dma_start(wt[:, 0:kt, :], src).then_inc(s["w"], 16)

                def up(i, j, last):
                    for h in range(2):
                        load(up_unit(i, j, h), KT, w_up[:, :, bass.ds(h * FF + j * P, P)])

                def down(i, t, h):
                    _, j0, n = parts[i]
                    load(down_unit(i, t), n, w_down[:, j0:j0 + n, bass.ds(t * P, P)])
                program(eng, up, down)

            @block.tensor
            def _(eng):
                def up(i, j, last):
                    for h in range(2):
                        eng.wait_ge(s["ws"], up_unit(i, j, h) + 1)
                        if isinstance(j, int) and j == parts[i][1]:
                            if i:
                                eng.wait_ge(s["v"], KT * i + h - 1)
                        else:
                            eng.wait_ge(s["ev"], 2 * j + h - 1)
                        for c, (c0, n) in enumerate(CH):
                            for k in range(KT):
                                mm = product(nc, g.ps[:, 3 * h + c, 0:n], (wh[:, h, k, :], wl[:, h, k, :]),
                                             (xh[:, k, c0:c0 + n], xl[:, k, c0:c0 + n]), k == 0, k == KT - 1)
                        mm.then_inc(s["mm"], 1)

                def down(i, t, h):
                    _, j0, nj = parts[i]
                    eng.wait_ge(s["ws"], down_unit(i, t) + 1)
                    if isinstance(t, int) and t < 2:
                        eng.wait_ge(s["ev"], 2 * (j0 + nj) + h - 1)
                    else:
                        eng.wait_ge(s["v"], KT * i + t - 1)
                    for k in range(nj):
                        if isinstance(t, int) and t == 0:
                            eng.wait_ge(s["al"], j0 + k + 1)
                        for c, (c0, n) in enumerate(CH):
                            mm = product(nc, g.ps[:, 3 * h + c, 0:n], (wh[:, h, k, :], wl[:, h, k, :]),
                                         (ah[:, k, c0:c0 + n], al[:, k, c0:c0 + n]), k == 0, k == nj - 1)
                    mm.then_inc(s["mm"], 1)
                program(eng, up, down)

            @block.gpsimd
            def _(eng):
                eng.memset(u[:, :, 0:2], 0.0).then_inc(s["z"], 1)

                def weights(n, h, kt):
                    low_weights(eng, wl[:, h, 0:kt], wt[:, 0:kt, :], wh[:, h, 0:kt], s, n + 1)
                for h in range(2):
                    weights(h, h, KT)

                def up(i, j, last):
                    for h in range(2):
                        if not (isinstance(j, int) and j == 0):
                            wait_apart(eng, s["cv"], 2 * j + h - 1, s["pool"])
                        t = h * FT + j
                        eng.tensor_copy(u[:, h, S0:EXT].rearrange("p (b q) -> p b q", q=NQ + 2)[:, :, 0:2],
                                        g.cst[:, bass.ds(t, 1), :].rearrange("p a (b r) -> p (a b) r", r=2)).then_inc(s["st"], 1)
                        wait_apart(eng, s["ev"], 2 * j + h + 1, s["pool"])
                        eng.tensor_copy(co[:, bass.ds(t, 1), 0:2].rearrange("p a r -> p (a r)"), u[:, h, SEQ:SEQ + 2])
                        eng.tensor_copy(co[:, bass.ds(t, 1), 2:2 + 2 * NB].rearrange("p a (b r) -> p (a b) r", r=2),
                                        u[:, h, S0:EXT].rearrange("p (b q) -> p b q", q=NQ + 2)[:, :, NQ:NQ + 2]).then_inc(s["co"], 1)
                        after_up(i, j, h, last, weights)
                    wait_apart(eng, s["ah"], j + 1, s["pool"])
                    for there, here in columns:
                        ins = low(eng, there(al, j - parts[i][1]), here(sg), there(ah, j - parts[i][1]))
                    ins.then_inc(s["al"], 1)
                program(eng, up, lambda i, t, h: after_down(i, t, h, weights))

            @block.scalar
            def _(eng):
                def up(i, j, last):
                    later = not (isinstance(j, int) and j == 0)
                    for h in range(2):
                        eng.wait_ge(s["mm"], up_unit(i, j, h) + 1)
                        if later:
                            eng.wait_ge(s["cv"], 2 * j + h - 1)
                            eng.wait_ge(s["co"], 2 * j + h - 1)
                        b0 = 3 * h
                        nc.scalar.copy(u[:, h, 2:2 + CH[0][1]], g.ps[:, b0, 0:CH[0][1]])
                        nc.scalar.copy(u[:, h, 2 + CH[1][0]:2 + CH[2][0]], g.ps[:, b0 + 1, 0:CH[1][1]])
                        n = SEQ - CH[2][0]
                        nc.scalar.copy(u[:, h, 2 + CH[2][0]:2 + SEQ], g.ps[:, b0 + 2, 0:n])
                        nc.scalar.copy(samp(u[:, h], 2), g.ps[:, b0 + 2, n:n + TS].rearrange("p (b q) -> p b q", q=NQ)).then_inc(s["ev"], 1)
                    eng.wait_ge(s["cv"], 2 * j + 1)
                    if later:
                        eng.wait_ge(s["al"], j)
                    nc.scalar.activation(sg[:, 0:E], cv[:, 0, 0:E], ACT.Sigmoid).then_inc(s["sg"], 1)
                    eng.wait_ge(s["act"], j + 1)
                    for there, here in columns:
                        ins = nc.scalar.copy(there(ah, j - parts[i][1]).bitcast(F32R), here(sg))
                    ins.then_inc(s["ah"], 1)
                program(eng, up, lambda i, t, h: None)

            @block.vector
            def _(eng):
                def weights(n, h, kt):
                    if not isinstance(n, int) or n >= 2:
                        eng.wait_ge(s["mm"], n - 1)
                    high_weights(eng, wh[:, h, 0:kt], wt[:, 0:kt, :], s["w"], 16 * n + 16, s)
                for h in range(2):
                    weights(h, h, KT)
                eng.wait_ge(s["z"], 1)

                def up(i, j, last):
                    for h in range(2):
                        eng.wait_ge(s["ev"], 2 * j + h + 1)
                        eng.wait_ge(s["st"], 2 * j + h + 1)
                        if not (isinstance(j, int) and j == 0):
                            eng.wait_ge(s["act"], j)
                        V_.tensor_scalar(cv[:, h, 0:E], u[:, h, 0:E], col(g.cw[:, 0], h, j), col(g.cb, h, j),
                                         ALU.mult, ALU.add).then_inc(s["t0"], 1)
                        eng.wait_ge(s["t0"], 2 * j + h + 1)
                        V_.scalar_tensor_tensor(out=cv[:, h, 0:E], in0=u[:, h, 1:1 + E], scalar=col(g.cw[:, 1], h, j),
                                                in1=cv[:, h, 0:E], op0=ALU.mult, op1=ALU.add).then_inc(s["t1"], 1)
                        eng.wait_ge(s["t1"], 2 * j + h + 1)
                        V_.scalar_tensor_tensor(out=cv[:, h, 0:E], in0=u[:, h, 2:2 + E], scalar=col(g.cw[:, 2], h, j),
                                                in1=cv[:, h, 0:E], op0=ALU.mult, op1=ALU.add).then_inc(s["cv"], 1)
                        after_up(i, j, h, last, weights)
                    eng.wait_ge(s["sg"], j + 1)
                    V_.tensor_tensor(sg[:, 0:E], sg[:, 0:E], cv[:, 0, 0:E], ALU.mult).then_inc(s["m"], 1)
                    eng.wait_ge(s["m"], j + 1)
                    eng.wait_ge(s["cv"], 2 * j + 2)
                    V_.tensor_tensor(sg[:, 0:E], sg[:, 0:E], cv[:, 1, 0:E], ALU.mult).then_inc(s["act"], 1)

                def down(i, t, h):
                    eng.wait_ge(s["mm"], down_unit(i, t) + 1)
                    if i:
                        eng.wait_ge(s["v"], KT * (i - 1) + t + 1)
                    for c, (c0, n) in enumerate(CH):
                        d = x1[:, bass.ds(t, 1), c0:c0 + n].rearrange("p a t -> p (a t)")
                        ins = V_.tensor_tensor(d, d, g.ps[:, 3 * h + c, 0:n], ALU.add)
                    ins.then_inc(s["v"], 1)
                    after_down(i, t, h, weights)
                program(eng, up, down)
    conv_state(g, co)


def conv_state(g, co):
    nc = g.nc
    R = CR
    with ExitStack() as ctx:
        rows = ctx.enter_context(nc.sbuf_tensor("conv_rows", [R, UT, P], F32))
        s_t, s_a, s_v, s_o = (g.sem(f"co_{n}") for n in "tavo")
        NF = UT // 4
        with nc.Block() as block:
            @block.tensor
            def _(eng):
                for f in range(NF):
                    if f >= 2:
                        eng.wait_ge(s_a if f % 2 == 0 else s_v, f // 2)
                    for q in range(4):
                        mm = nc.tensor.transpose(g.ps[0:R, f % 2, q * P:(q + 1) * P], co[:, 4 * f + q, :], g.ident)
                    mm.then_inc(s_t, 1)

            @block.scalar
            def _(eng):
                for f in range(0, NF, 2):
                    eng.wait_ge(s_t, f + 1)
                    nc.scalar.copy(rows[:, 4 * f:4 * f + 4, :].rearrange("r a n -> r (a n)"), g.ps[0:R, 0, :]).then_inc(s_a, 1)

            @block.vector
            def _(eng):
                for f in range(1, NF, 2):
                    eng.wait_ge(s_t, f + 1)
                    nc.vector.tensor_copy(rows[:, 4 * f:4 * f + 4, :].rearrange("r a n -> r (a n)"), g.ps[0:R, 1, :]).then_inc(s_v, 1)

            @block.sync
            def _(eng):
                eng.wait_ge(s_a, (NF + 1) // 2)
                eng.wait_ge(s_v, NF // 2)
                eng.dma_start(g.o["conv_prompt"][0, 0], rows[0:2].rearrange("r a n -> r (a n)")).then_inc(s_o, 16)
                eng.dma_start(g.o["conv_sample"][0].rearrange("b r f -> (b r) f"), rows[2:R].rearrange("r a n -> r (a n)")).then_inc(s_o, 16)
                eng.wait_ge(s_o, 32)


def store_rows(g, y):
    nc = g.nc
    NT = SEQ // P
    with ExitStack() as ctx:
        rows = ctx.enter_context(nc.sbuf_tensor("y_rows", [P, 3, D], F32))
        s_t, s_a, s_v = (g.sem(f"yr_{n}") for n in "tav")
        s_o = [g.sem(f"yr_o{i}") for i in range(3)]
        with nc.Block() as block:
            @block.tensor
            def _(eng):
                for j in range(NT + 1):
                    n = P if j < NT else TS
                    for h in range(2):
                        if j >= 2:
                            eng.wait_ge((s_a, s_v)[h], j - 1)
                        for q in range(4):
                            mm = nc.tensor.transpose(g.ps[0:n, 2 * (j % 2) + h, q * P:(q + 1) * P],
                                                     y[:, 4 * h + q, j * P:j * P + n], g.ident)
                        mm.then_inc(s_t, 1)

            def copies(eng, h, copy, sem):
                for j in range(NT + 1):
                    n = P if j < NT else TS
                    eng.wait_ge(s_t, 2 * j + h + 1)
                    if j >= 3:
                        eng.wait_ge(s_o[j % 3], 16 * (j // 3))
                    copy(rows[0:n, j % 3, 512 * h:512 * h + 512], g.ps[0:n, 2 * (j % 2) + h, :]).then_inc(sem, 1)

            @block.scalar
            def _(eng):
                copies(eng, 0, nc.scalar.copy, s_a)

            @block.vector
            def _(eng):
                copies(eng, 1, nc.vector.tensor_copy, s_v)

            @block.sync
            def _(eng):
                for j in range(NT + 1):
                    n = P if j < NT else TS
                    eng.wait_ge(s_a, j + 1)
                    eng.wait_ge(s_v, j + 1)
                    dst = g.o["y_prompt"][0, j * P:(j + 1) * P, :] if j < NT else g.o["y_sample"].rearrange("b q d -> (b q) d")
                    eng.dma_start(dst, rows[0:n, j % 3, :]).then_inc(s_o[j % 3], 16)
                for i in range(3):
                    eng.wait_ge(s_o[i], 48)


_INS = ['x_prompt', 'x_sample', 'cache_sb_k', 'cache_sb_v', 'page_table', 'cache_win0', 'cache_win1', 'cache_win2',
        'state_wkv', 'state_shift', 'state_conv', 'norm_mix', 'w_in', 'rwkv_mu', 'rwkv_w0', 'rwkv_w2', 'rwkv_a0',
        'rwkv_a2', 'rwkv_g2', 'rwkv_k_k', 'rwkv_k_a', 'rwkv_r_k', 'rwkv_ln_w', 'rwkv_ln_b', 'sb_bias', 'w_branch_a',
        'w_branch_b', 'w_branch_c', 'w_out', 'norm_ffn', 'w_up', 'conv_w', 'conv_b', 'w_down', 'norm_final']
_OUTS = [("y_prompt", (1, SEQ, D)), ("y_sample", (NB, NQ, D)),
         ("sb_k_prompt", (1, 1, SEQ, SBH, HD)), ("sb_k_sample", (1, NB, NQ, SBH, HD)),
         ("sb_v_prompt", (1, 1, SEQ, SBH, HD)), ("sb_v_sample", (1, NB, NQ, SBH, HD)),
         ("win0_prompt", (1, 1, 128, 2, 2, HD)), ("win0_sample", (1, NB, 128, 2, 2, HD)),
         ("win1_prompt", (1, 1, 512, 2, 2, HD)), ("win1_sample", (1, NB, 512, 2, 2, HD)),
         ("win2_prompt", (1, 1, SEQ, 2, 2, HD)), ("win2_sample", (1, NB, 2048, 2, 2, HD)),
         ("wkv_prompt", (1, 1, AH, HD, HD)), ("wkv_sample", (1, NB, AH, HD, HD)),
         ("shift_prompt", (1, 1, D)), ("shift_sample", (1, NB, D)),
         ("conv_prompt", (1, 1, 2, 2 * FF)), ("conv_sample", (1, NB, 2, 2 * FF))]


def declare(nc, inputs):
    arrays, a = {}, {}
    for name in _INS:
        x = np.ascontiguousarray(inputs[name])
        arrays[f"in_{name}"] = x
        a[name] = nc.dram_tensor(f"in_{name}", x.shape, mybir.dt.from_np(x.dtype), kind="ExternalInput").ap()
    for name, x in constants().items():
        arrays[name] = x
        a[name] = nc.dram_tensor(name, x.shape, mybir.dt.from_np(x.dtype), kind="ExternalInput").ap()
    o = {n: nc.dram_tensor(f"out_{n}", s, F32, kind="ExternalOutput").ap() for n, s in _OUTS}
    scratch = {"xt": nc.dram_tensor("scr_xt", (P, KT, T), F32, kind="Internal").ap(),
               "xh": nc.dram_tensor("scr_xh", (P, KT, T), F32, kind="Internal").ap(),
               "xl": nc.dram_tensor("scr_xl", (P, KT, T), F32, kind="Internal").ap()}
    return arrays, (a, o, scratch)


def kernel(**inputs):
    import concourse.bacc as _bacc
    from concourse.bass_utils import run_bass_kernel_spmd as _run

    nc = _bacc.Bacc("TRN2", target_bir_lowering=False, num_devices=1)
    arrays, tensors = declare(nc, inputs)
    build(nc, *tensors)
    r = _run(nc, [arrays], core_ids=[0])
    return tuple(r.results[0][f"out_{n}"] for n, _ in _OUTS)
```
